# Optimizing a Trainium2 kernel written in Bass

```python
import jax, jax.numpy as jnp
from jax import lax
import numpy as np

D_MODEL = 1024
BATCH = 1
SEQ = 512
DEPTH = 1

N_BRANCH = 4
MIX = D_MODEL // 4
ML_HEADS = 4
ML_DH = MIX // ML_HEADS
ML_CHUNK = 64
GLA_HEADS = 4
GLA_DH = MIX // GLA_HEADS
GLA_RANK = 16
GLA_TAU = 16.0
GLA_CHUNK = 16
CONF_WIDTH = 31
SC_WIDTH = 3
FFN_WIDTH = 3
FFN_HIDDEN = ((8 * D_MODEL // 3 + 255) // 256) * 256
EPS = 1e-6

IN_SPLITS = (
    ("ml_q", MIX), ("ml_k", MIX), ("ml_v", MIX), ("ml_o", MIX),
    ("ml_i", ML_HEADS), ("ml_f", ML_HEADS),
    ("gla_q", MIX), ("gla_k", MIX), ("gla_v", MIX), ("gla_r", MIX), ("gla_a", GLA_RANK),
    ("conf", 2 * MIX),
    ("sc", 3 * MIX),
    ("gate", N_BRANCH * D_MODEL),
)
IN_WIDTH = sum(w for _, w in IN_SPLITS)


def rms_norm(x, g):
    xf = x.astype(jnp.float32)
    y = xf * lax.rsqrt(jnp.mean(xf * xf, axis=-1, keepdims=True) + EPS)
    return (y * g.astype(jnp.float32)).astype(x.dtype)

def layer_norm(x, g, b):
    xf = x.astype(jnp.float32)
    mu = jnp.mean(xf, axis=-1, keepdims=True)
    xc = xf - mu
    y = xc * lax.rsqrt(jnp.mean(xc * xc, axis=-1, keepdims=True) + EPS)
    return (y * g.astype(jnp.float32) + b.astype(jnp.float32)).astype(x.dtype)

def head_rms_norm(t, g, n_heads):
    Bn, S, H, d = t.shape
    tf = t.astype(jnp.float32)
    y = tf * lax.rsqrt(jnp.mean(tf * tf, axis=-1, keepdims=True) + EPS)
    y = y * g.astype(jnp.float32).reshape(n_heads, d)
    return y.reshape(Bn, S, H * d)

def causal_dwconv(x, w):
    K, C = w.shape
    return lax.conv_general_dilated(
        x, w[:, None, :].astype(x.dtype), window_strides=(1,), padding=[(K - 1, 0)],
        dimension_numbers=("NWC", "WIO", "NWC"), feature_group_count=C)

def split_columns(proj):
    out = {}
    off = 0
    for name, width in IN_SPLITS:
        out[name] = proj[..., off:off + width]
        off += width
    return out

def split_heads(t, n_heads):
    return t.reshape(t.shape[:2] + (n_heads, t.shape[-1] // n_heads))

def to_chunks(t, L):
    Bn, S, H = t.shape[:3]
    t = t.reshape((Bn, S // L, L, H) + t.shape[3:])
    return jnp.moveaxis(t, (1, 3), (0, 2))

def from_chunks(t):
    NC, Bn, H, L = t.shape[:4]
    t = jnp.moveaxis(t, (0, 2), (1, 3))
    return t.reshape((Bn, NC * L, H) + t.shape[4:])

def mlstm_chunked(q, k, v, i_pre, f_pre):
    f32 = jnp.float32
    Bn, S, H, Dk = q.shape
    Dv = v.shape[-1]
    L = ML_CHUNK
    xs = (to_chunks(q.astype(f32) * (Dk ** -0.5), L), to_chunks(k.astype(f32), L),
          to_chunks(v.astype(f32), L), to_chunks(i_pre.astype(f32), L),
          to_chunks(jax.nn.log_sigmoid(f_pre.astype(f32)), L))
    causal = jnp.tril(jnp.ones((L, L), dtype=bool))

    def step(carry, chunk):
        C, n, m = carry
        qc, kc, vc, ic, fc = chunk
        b = jnp.cumsum(fc, axis=-1)
        logD = jnp.where(causal, b[..., :, None] - b[..., None, :] + ic[..., None, :], -jnp.inf)
        g = b + m[..., None]
        mt = jnp.maximum(g, jnp.max(logD, axis=-1))
        w_inter = jnp.exp(g - mt)
        qk = jnp.einsum('bhtd,bhsd->bhts', qc, kc) * jnp.exp(logD - mt[..., None])
        num = (w_inter[..., None] * jnp.einsum('bhtd,bhde->bhte', qc, C)
               + jnp.einsum('bhts,bhse->bhte', qk, vc))
        den = w_inter * jnp.einsum('bhtd,bhd->bht', qc, n) + jnp.sum(qk, axis=-1)
        h = num / jnp.maximum(jnp.abs(den), jnp.exp(-mt))[..., None]
        bL = b[..., -1]
        a = bL[..., None] - b + ic
        m_new = jnp.maximum(bL + m, jnp.max(a, axis=-1))
        w = jnp.exp(a - m_new[..., None])
        decay = jnp.exp(bL + m - m_new)
        C = decay[..., None, None] * C + jnp.einsum('bhs,bhsd,bhse->bhde', w, kc, vc)
        n = decay[..., None] * n + jnp.einsum('bhs,bhsd->bhd', w, kc)
        return (C, n, m_new), h

    init = (jnp.zeros((Bn, H, Dk, Dv), f32), jnp.zeros((Bn, H, Dk), f32), jnp.zeros((Bn, H), f32))
    _, h = lax.scan(step, init, xs)
    return from_chunks(h)

def gla_chunked(q, k, v, log_a):
    f32 = jnp.float32
    Bn, S, H, Dk = q.shape
    Dv = v.shape[-1]
    L = GLA_CHUNK
    xs = (to_chunks(q.astype(f32) * (Dk ** -0.5), L), to_chunks(k.astype(f32), L),
          to_chunks(v.astype(f32), L), to_chunks(log_a.astype(f32), L))
    causal = jnp.tril(jnp.ones((L, L), dtype=bool))

    def step(state, chunk):
        qc, kc, vc, lac = chunk
        b = jnp.cumsum(lac, axis=2)
        bL = b[:, :, -1:, :]
        q_dec = qc * jnp.exp(b)
        attn = jnp.where(causal, jnp.einsum('bhtd,bhsd->bhts', q_dec, kc * jnp.exp(-b)), 0.0)
        o = jnp.einsum('bhtd,bhde->bhte', q_dec, state) + jnp.einsum('bhts,bhse->bhte', attn, vc)
        k_dec = kc * jnp.exp(bL - b)
        state = jnp.exp(bL[:, :, 0, :])[..., None] * state + jnp.einsum('bhsd,bhse->bhde', k_dec, vc)
        return state, o

    _, o = lax.scan(step, jnp.zeros((Bn, H, Dk, Dv), f32), xs)
    return from_chunks(o)

def token_mixer(h, w_in, ml_i_bias, ml_f_bias, ml_norm_g, w_ml_out, gla_w_a2, gla_a_bias,
                gla_norm_g, w_gla_out, conf_dw_w, conf_dw_b, conf_ln_g, conf_ln_b, w_conf_out,
                conf_out_b, sc_dw_w, w_sc_out, merge_gate_b, w_o):
    Bn, S, _ = h.shape
    p = split_columns(h @ w_in)
    ml = mlstm_chunked(split_heads(p["ml_q"], ML_HEADS), split_heads(p["ml_k"], ML_HEADS),
                       split_heads(p["ml_v"], ML_HEADS), p["ml_i"] + ml_i_bias, p["ml_f"] + ml_f_bias)
    ml = head_rms_norm(ml, ml_norm_g, ML_HEADS).astype(h.dtype)
    y_ml = (ml * jax.nn.sigmoid(p["ml_o"])) @ w_ml_out
    log_a = jax.nn.log_sigmoid((p["gla_a"] @ gla_w_a2 + gla_a_bias).astype(jnp.float32)) / GLA_TAU
    gl = gla_chunked(split_heads(p["gla_q"], GLA_HEADS), split_heads(p["gla_k"], GLA_HEADS),
                     split_heads(p["gla_v"], GLA_HEADS), split_heads(log_a, GLA_HEADS))
    gl = head_rms_norm(gl, gla_norm_g, GLA_HEADS).astype(h.dtype)
    y_gla = (gl * jax.nn.silu(p["gla_r"])) @ w_gla_out
    a, g = jnp.split(p["conf"], 2, axis=-1)
    u = causal_dwconv(a * jax.nn.sigmoid(g), conf_dw_w) + conf_dw_b
    u = jax.nn.silu(layer_norm(u, conf_ln_g, conf_ln_b))
    y_conf = u @ w_conf_out + conf_out_b
    bg, cg, xv = jnp.split(p["sc"], 3, axis=-1)
    y_sc = (bg * causal_dwconv(cg * xv, sc_dw_w)) @ w_sc_out
    gates = jax.nn.sigmoid(p["gate"] + merge_gate_b).reshape(Bn, S, N_BRANCH, D_MODEL)
    merged = (gates[:, :, 0] * y_ml + gates[:, :, 1] * y_gla
              + gates[:, :, 2] * y_conf + gates[:, :, 3] * y_sc)
    return merged @ w_o

def conv_ffn(h, w_up, dw_w, w_down):
    u = causal_dwconv(h @ w_up, dw_w)
    a, v = jnp.split(u, 2, axis=-1)
    return (jax.nn.silu(a) * v) @ w_down

def first_inputs(seed: int = 0) -> dict:
    key = jax.random.key(seed)
    keys = list(jax.random.split(key, 40))

    def nrm(shape, scale):
        return jax.random.normal(keys.pop(), shape, jnp.float32) * scale

    L = DEPTH
    D = D_MODEL
    return {
        "x": nrm((BATCH, SEQ, D), 1.0),
        "c": nrm((BATCH, D), 1.0),
        "ada_w": nrm((L, D, 6 * D), 0.5 * D ** -0.5),
        "ada_b": nrm((L, 6 * D), 0.02),
        "tm_pre_g": 1.0 + nrm((L, D), 0.05),
        "tm_post_g": 1.0 + nrm((L, D), 0.05),
        "cm_pre_g": 1.0 + nrm((L, D), 0.05),
        "cm_post_g": 1.0 + nrm((L, D), 0.05),
        "w_in": nrm((L, D, IN_WIDTH), D ** -0.5),
        "ml_i_bias": nrm((L, ML_HEADS), 0.1),
        "ml_f_bias": 3.0 + nrm((L, ML_HEADS), 0.5),
        "ml_norm_g": 1.0 + nrm((L, MIX), 0.05),
        "w_ml_out": nrm((L, MIX, D), MIX ** -0.5),
        "gla_w_a2": nrm((L, GLA_RANK, MIX), GLA_RANK ** -0.5),
        "gla_a_bias": nrm((L, MIX), 0.1),
        "gla_norm_g": 1.0 + nrm((L, MIX), 0.05),
        "w_gla_out": nrm((L, MIX, D), MIX ** -0.5),
        "conf_dw_w": nrm((L, CONF_WIDTH, MIX), CONF_WIDTH ** -0.5),
        "conf_dw_b": nrm((L, MIX), 0.02),
        "conf_ln_g": 1.0 + nrm((L, MIX), 0.05),
        "conf_ln_b": nrm((L, MIX), 0.02),
        "w_conf_out": nrm((L, MIX, D), MIX ** -0.5),
        "conf_out_b": nrm((L, D), 0.02),
        "sc_dw_w": nrm((L, SC_WIDTH, MIX), SC_WIDTH ** -0.5),
        "w_sc_out": nrm((L, MIX, D), MIX ** -0.5),
        "merge_gate_b": nrm((L, N_BRANCH * D), 0.02),
        "w_o": nrm((L, D, D), D ** -0.5),
        "ffn_w_up": nrm((L, D, 2 * FFN_HIDDEN), D ** -0.5),
        "ffn_dw_w": nrm((L, FFN_WIDTH, 2 * FFN_HIDDEN), FFN_WIDTH ** -0.5),
        "ffn_w_down": nrm((L, FFN_HIDDEN, D), FFN_HIDDEN ** -0.5),
    }

def first_block(x, c, ada_w, ada_b, tm_pre_g, tm_post_g, cm_pre_g, cm_post_g, w_in, ml_i_bias,
              ml_f_bias, ml_norm_g, w_ml_out, gla_w_a2, gla_a_bias, gla_norm_g, w_gla_out,
              conf_dw_w, conf_dw_b, conf_ln_g, conf_ln_b, w_conf_out, conf_out_b, sc_dw_w,
              w_sc_out, merge_gate_b, w_o, ffn_w_up, ffn_dw_w, ffn_w_down):
    c_act = jax.nn.silu(c)
    for l in range(DEPTH):
        mod = (c_act @ ada_w[l] + ada_b[l])[:, None, :]
        sh_t, sc_t, g_t, sh_c, sc_c, g_c = jnp.split(mod, 6, axis=-1)
        h = rms_norm(x, tm_pre_g[l]) * (1.0 + sc_t) + sh_t
        y = token_mixer(h, w_in[l], ml_i_bias[l], ml_f_bias[l], ml_norm_g[l], w_ml_out[l],
                        gla_w_a2[l], gla_a_bias[l], gla_norm_g[l], w_gla_out[l], conf_dw_w[l],
                        conf_dw_b[l], conf_ln_g[l], conf_ln_b[l], w_conf_out[l], conf_out_b[l],
                        sc_dw_w[l], w_sc_out[l], merge_gate_b[l], w_o[l])
        x = x + g_t * rms_norm(y, tm_post_g[l])
        h = rms_norm(x, cm_pre_g[l]) * (1.0 + sc_c) + sh_c
        y = conv_ffn(h, ffn_w_up[l], ffn_dw_w[l], ffn_w_down[l])
        x = x + g_c * rms_norm(y, cm_post_g[l])
    return x


POOL_WIDTH = D_MODEL // 2
POOL_GROUPS = 4
POOL_GROUP_DIM = POOL_WIDTH // POOL_GROUPS
POOL_WINDOWS = (2, 4, 8, 16)
N_HEADS = 8
HEAD_DIM = 64
ATTN_WIDTH = N_HEADS * HEAD_DIM
ROT_DIM = HEAD_DIM // 4
ROPE_THETA = 500000.0
IDX_HEADS = 8
IDX_DIM = 64
TOPK_MAX = 256
Q_BLOCK = 128
N_BRANCH_2 = 2
D_FF = 2816
CONV_WIDTH = 3
IN_SPLITS_2 = (POOL_WIDTH, ATTN_WIDTH, ATTN_WIDTH, ATTN_WIDTH,
             IDX_HEADS * IDX_DIM, IDX_DIM, IDX_HEADS, N_BRANCH_2 * D_MODEL)
D_IN = POOL_WIDTH + 3 * ATTN_WIDTH + IDX_HEADS * IDX_DIM + IDX_DIM + IDX_HEADS + N_BRANCH_2 * D_MODEL


def rmsnorm(x, g):
    xf = x.astype(jnp.float32)
    y = xf * lax.rsqrt(jnp.mean(xf * xf, axis=-1, keepdims=True) + EPS)
    return (y * g.astype(jnp.float32)).astype(x.dtype)

def rope_partial(x, pos):
    half = ROT_DIM // 2
    inv_freq = 1.0 / (ROPE_THETA ** (jnp.arange(half, dtype=jnp.float32) * 2.0 / ROT_DIM))
    ang = pos[:, None] * inv_freq[None, :]
    cos = jnp.cos(ang)[None, :, None, :]
    sin = jnp.sin(ang)[None, :, None, :]
    xr = x[..., :ROT_DIM].astype(jnp.float32)
    x1, x2 = xr[..., :half], xr[..., half:]
    rot = jnp.concatenate([x1 * cos - x2 * sin, x2 * cos + x1 * sin], axis=-1)
    return jnp.concatenate([rot.astype(x.dtype), x[..., ROT_DIM:]], axis=-1)

def multiscale_pool(u):
    B, S, _ = u.shape
    ug = u.astype(jnp.float32).reshape(B, S, POOL_GROUPS, POOL_GROUP_DIM)
    c0 = jnp.concatenate([jnp.zeros((B, 1, POOL_GROUPS, POOL_GROUP_DIM), jnp.float32),
                          jnp.cumsum(ug, axis=1)], axis=1)
    t = jnp.arange(S)
    outs = []
    for g, w in enumerate(POOL_WINDOWS):
        lo = jnp.maximum(t + 1 - w, 0)
        cg = c0[:, :, g]
        sums = cg[:, 1:] - cg[:, lo]
        cnt = jnp.minimum(t + 1, w).astype(jnp.float32)[None, :, None]
        outs.append(sums / cnt - ug[:, :, g])
    return jnp.stack(outs, axis=2).astype(u.dtype)

def indexed_sparse_attention(q, k, v, iq, ik, iw):
    B, S, H, Dh = q.shape
    k_top = min(TOPK_MAX, S // 4)
    nblk = S // Q_BLOCK
    kpos = jnp.arange(S)

    def to_blocks(a):
        return a.reshape((B, nblk, Q_BLOCK) + a.shape[2:]).swapaxes(0, 1)

    t_blocks = kpos.reshape(nblk, Q_BLOCK)

    def block_fn(args):
        qb, iqb, iwb, tb = args
        s = jnp.einsum('bqhd,bkd->bhqk', iqb, ik).astype(jnp.float32) * (IDX_DIM ** -0.5)
        w = iwb.astype(jnp.float32) * (IDX_HEADS ** -0.5)
        score = jnp.einsum('bqh,bhqk->bqk', w, jax.nn.relu(s))
        causal = kpos[None, :] <= tb[:, None]
        score = jnp.where(causal[None], score, -jnp.inf)
        _, idx = lax.top_k(score, k_top)
        valid = idx <= tb[None, :, None]
        kg = jax.vmap(lambda kb, ib: kb[ib])(k, idx)
        vg = jax.vmap(lambda vb, ib: vb[ib])(v, idx)
        sc = jnp.einsum('bqhd,bqkhd->bhqk', qb, kg).astype(jnp.float32) * (Dh ** -0.5)
        sc = jnp.where(valid[:, None], sc, -jnp.inf)
        p = jax.nn.softmax(sc, axis=-1)
        return jnp.einsum('bhqk,bqkhd->bqhd', p.astype(vg.dtype), vg)

    out = lax.map(block_fn, (to_blocks(q), to_blocks(iq), to_blocks(iw), t_blocks))
    return out.swapaxes(0, 1).reshape(B, S, H * Dh)

def hybrid_mixer(xn, w_in, pool_w, pool_scale, w_pool_proj, w_attn_proj, w_out):
    B, S, _ = xn.shape
    proj = xn @ w_in
    cuts = [int(c) for c in np.cumsum(IN_SPLITS_2)[:-1]]
    u_pool, q, k, v, iq, ik, iw, gates = jnp.split(proj, cuts, axis=-1)
    pos = jnp.arange(S, dtype=jnp.float32)

    pooled = multiscale_pool(u_pool)
    mixed = jnp.einsum('bsgc,gcd->bsgd', pooled, pool_w).reshape(B, S, POOL_WIDTH) * pool_scale
    y_pool = mixed @ w_pool_proj

    q = rope_partial(q.reshape(B, S, N_HEADS, HEAD_DIM), pos)
    k = rope_partial(k.reshape(B, S, N_HEADS, HEAD_DIM), pos)
    v = v.reshape(B, S, N_HEADS, HEAD_DIM)
    iq = rope_partial(iq.reshape(B, S, IDX_HEADS, IDX_DIM), pos)
    ik = rope_partial(ik.reshape(B, S, 1, IDX_DIM), pos)[:, :, 0]
    o = indexed_sparse_attention(q, k, v, iq, ik, iw)
    y_attn = o @ w_attn_proj

    g = jax.nn.sigmoid(gates.astype(jnp.float32)).reshape(B, S, N_BRANCH_2, D_MODEL)
    merged = (g[:, :, 0] * y_pool.astype(jnp.float32) + g[:, :, 1] * y_attn.astype(jnp.float32)).astype(xn.dtype)
    return merged @ w_out

def conv_ffn_2(xn, w_up, conv_w, conv_b, w_down):
    h = xn @ w_up
    C = h.shape[-1]
    h = lax.conv_general_dilated(h, conv_w[:, None, :].astype(h.dtype), window_strides=(1,),
                                 padding=[(CONV_WIDTH - 1, 0)],
                                 dimension_numbers=('NWC', 'WIO', 'NWC'),
                                 feature_group_count=C) + conv_b
    a, b = jnp.split(h, 2, axis=-1)
    return (jax.nn.silu(a) * b) @ w_down

def second_inputs(seed: int = 0) -> dict:
    key = jax.random.key(seed)
    ks = jax.random.split(key, 16)
    f32 = jnp.float32
    nrm = lambda k, shape, fan: jax.random.normal(k, shape, f32) * (fan ** -0.5)
    L = DEPTH
    return {
        "x": jax.random.normal(ks[0], (BATCH, SEQ, D_MODEL), f32),
        "norm_mix_g": 1.0 + 0.05 * jax.random.normal(ks[1], (L, D_MODEL), f32),
        "w_in": nrm(ks[2], (L, D_MODEL, D_IN), D_MODEL),
        "pool_w": nrm(ks[3], (L, POOL_GROUPS, POOL_GROUP_DIM, POOL_GROUP_DIM), POOL_GROUP_DIM),
        "pool_scale": 1.0 + 0.1 * jax.random.normal(ks[4], (L, POOL_WIDTH), f32),
        "w_pool_proj": nrm(ks[5], (L, POOL_WIDTH, D_MODEL), POOL_WIDTH),
        "w_attn_proj": nrm(ks[6], (L, ATTN_WIDTH, D_MODEL), ATTN_WIDTH),
        "w_out": nrm(ks[7], (L, D_MODEL, D_MODEL), D_MODEL),
        "norm_ffn_g": 1.0 + 0.05 * jax.random.normal(ks[8], (L, D_MODEL), f32),
        "w_up": nrm(ks[9], (L, D_MODEL, 2 * D_FF), D_MODEL),
        "conv_w": nrm(ks[10], (L, CONV_WIDTH, 2 * D_FF), CONV_WIDTH),
        "conv_b": 0.02 * jax.random.normal(ks[11], (L, 2 * D_FF), f32),
        "w_down": nrm(ks[12], (L, D_FF, D_MODEL), D_FF),
        "norm_final_g": 1.0 + 0.05 * jax.random.normal(ks[13], (D_MODEL,), f32),
    }

def second_block(x, norm_mix_g, w_in, pool_w, pool_scale, w_pool_proj, w_attn_proj, w_out,
              norm_ffn_g, w_up, conv_w, conv_b, w_down, norm_final_g):
    h = x
    for l in range(DEPTH):
        h = h + hybrid_mixer(rmsnorm(h, norm_mix_g[l]), w_in[l], pool_w[l], pool_scale[l],
                             w_pool_proj[l], w_attn_proj[l], w_out[l])
        h = h + conv_ffn_2(rmsnorm(h, norm_ffn_g[l]), w_up[l], conv_w[l], conv_b[l], w_down[l])
    return rmsnorm(h, norm_final_g)


def setup_inputs(seed=0):
    out = dict(first_inputs(seed))
    for name, value in second_inputs(seed + 1).items():
        if name != "x":
            out[name + "_2"] = value
    return out


def reference(
    x, c, ada_w, ada_b, tm_pre_g, tm_post_g, cm_pre_g, cm_post_g, w_in, ml_i_bias, ml_f_bias,
    ml_norm_g, w_ml_out, gla_w_a2, gla_a_bias, gla_norm_g, w_gla_out, conf_dw_w, conf_dw_b,
    conf_ln_g, conf_ln_b, w_conf_out, conf_out_b, sc_dw_w, w_sc_out, merge_gate_b, w_o,
    ffn_w_up, ffn_dw_w, ffn_w_down, norm_mix_g_2, w_in_2, pool_w_2, pool_scale_2, w_pool_proj_2,
    w_attn_proj_2, w_out_2, norm_ffn_g_2, w_up_2, conv_w_2, conv_b_2, w_down_2, norm_final_g_2,
):
    x = first_block(
        x, c, ada_w, ada_b, tm_pre_g, tm_post_g, cm_pre_g, cm_post_g, w_in, ml_i_bias,
        ml_f_bias, ml_norm_g, w_ml_out, gla_w_a2, gla_a_bias, gla_norm_g, w_gla_out, conf_dw_w,
        conf_dw_b, conf_ln_g, conf_ln_b, w_conf_out, conf_out_b, sc_dw_w, w_sc_out,
        merge_gate_b, w_o, ffn_w_up, ffn_dw_w, ffn_w_down,
    )
    return second_block(
        x, norm_mix_g_2, w_in_2, pool_w_2, pool_scale_2, w_pool_proj_2, w_attn_proj_2, w_out_2,
        norm_ffn_g_2, w_up_2, conv_w_2, conv_b_2, w_down_2, norm_final_g_2,
    )


_drawn_inputs = setup_inputs


def setup_inputs(seed=0):
    import zlib

    import numpy as np

    out = dict(_drawn_inputs(seed))
    spreads = {}
    factors = {'tm_post_g': 3.066,
     'cm_post_g': 3.112,
     'ml_i_bias': 64.0,
     'ml_norm_g': 7.443,
     'gla_a_bias': 6.866,
     'gla_norm_g': 6.089,
     'conf_dw_b': 8.0,
     'conf_ln_g': 6.412,
     'conf_ln_b': 34.152,
     'conf_out_b': 25.09,
     'merge_gate_b': 8.0,
     'conv_b_2': 4.422,
     'norm_mix_g_2': 2.955,
     'norm_ffn_g_2': 3.384}
    for name, (base, spread) in spreads.items():
        noise = np.random.default_rng([zlib.crc32(name.encode()), seed]).standard_normal(out[name].shape)
        drawn = base * np.exp(spread * noise) if base else spread * noise
        out[name] = __import__('jax').numpy.asarray(drawn.astype(out[name].dtype))
    for name, factor in factors.items():
        out[name] = (out[name] * factor).astype(out[name].dtype)
    return out
```

```python
import numpy as np
import concourse.bass as bass
from concourse import mybir
from contextlib import ExitStack

FP32 = mybir.dt.float32
F32R = mybir.dt.float32r
U32 = mybir.dt.uint32
ALU = mybir.AluOpType
ACT = mybir.ActivationFunctionType
AX = mybir.AxisListType

P = 128
D = 1024
S = 512
KT = D // P
TT = S // P
MIX = D // 4
MT = MIX // P
HD = 64
MH = MIX // HD
GC = 16
NC = S // GC
CPT = P // GC
CONF_W = 31
FF = 2816
FT = FF // P
EPS = 1e-6
NEG = -1.0e30
TAKEN = -3.0e38
TOPK = S // 4
NH2 = 8
POOL_G = 4
UNIT = 2048
LOWER = 0.125

C_ML, C_MLIF, C_GLA, C_GLAA = 0, 1024, 1032, 2056
C_CONF, C_SC, C_GATE = 2072, 2584, 3352
C_POOL, C_Q, C_K, C_V, C_IQ, C_IK, C_GATE2 = 0, 512, 1024, 1536, 2048, 2560, 2632
IKW = HD + NH2

VECTORS = [
    [("c", 8), ("ada_b", 48), ("tm_pre_g", 8), ("tm_post_g", 8), ("cm_pre_g", 8), ("cm_post_g", 8), ("conf_out_b", 8)],
    [("merge_gate_b", 32), ("ml_norm_g", 2), ("gla_norm_g", 2), ("gla_a_bias", 2), ("conf_dw_b", 2),
     ("conf_ln_g", 2), ("conf_ln_b", 2), ("sc_dw_w", 6), ("conf_dw_w", 62)],
    [("norm_mix_g_2", 8), ("norm_ffn_g_2", 8), ("pool_scale_2", 4), ("conv_b_2", 44), ("ffn_dw_w/0", 44)],
    [("ffn_dw_w/1", 44), ("ffn_dw_w/2", 44)],
    [("conv_w_2/0", 44), ("conv_w_2/1", 44)],
    [("conv_w_2/2", 44)],
]
N_VECTORS = sum(len(g) for g in VECTORS)
COLUMN = {}
for _g, _group in enumerate(VECTORS):
    _r = 0
    for _name, _n in _group:
        COLUMN[_name] = _g * P + _r
        _r += _n

CONSTS = [("ident", P), ("ones_d", P), ("ones_head", P), ("ones_mix", P), ("causal_st", P), ("causal_qk", P),
          ("block_causal", P), ("chunk_of", CPT), ("rope_swap", P), ("pool_count", POOL_G * 16),
          ("sel", MH * P), ("chunk_reset", S)]
CONST_AT = {}
_at = 0
for _name, _n in CONSTS:
    CONST_AT[_name] = (_at, _n)
    _at += _n
N_CONST = _at
CONST_AT["rope_cos"], CONST_AT["rope_sin"] = (N_CONST - 2 * S, S), (N_CONST - S, S)


def shape_constants():
    out = np.zeros((P, N_CONST + 2 * S), np.float32)

    def put(name, a):
        at, n = CONST_AT[name]
        at += 2 * S if name in ("rope_cos", "rope_sin") else 0
        out[:a.shape[0], at:at + n] = a

    p, q = np.arange(P)[:, None], np.arange(P)[None, :]
    put("ident", np.eye(P))
    put("ones_d", np.full((P, P), 1.0 / D))
    put("ones_head", (p // HD == q // HD) / HD)
    put("ones_mix", np.full((P, P), 1.0 / MIX))
    put("sel", np.concatenate([np.repeat((np.arange(MH) == h)[:, None], P, 1) for h in range(MH)], 1))
    put("causal_st", np.where(p <= q, 0.0, NEG))
    put("causal_qk", np.where(q <= p, 0.0, NEG))
    put("block_causal", (p // GC == q // GC) & (p <= q))
    put("chunk_of", p // GC == np.arange(CPT)[None, :])
    put("chunk_reset", np.repeat((np.arange(S) % GC != 0)[None, :], P, 0))
    rot = HD // 4
    half = rot // 2
    inv = (np.float32(1.0) / np.float32(500000.0) ** (np.arange(half, dtype=np.float32) * np.float32(2.0) / np.float32(rot)))
    ang = np.arange(S, dtype=np.float32)[:, None] * inv.astype(np.float32)[None, :]
    cos, sin = np.cos(ang).T, np.sin(ang).T
    c, s, swap = np.ones((P, S)), np.zeros((P, S)), np.zeros((P, P))
    for base in (0, HD):
        c[base:base + half] = c[base + half:base + rot] = cos
        s[base:base + half], s[base + half:base + rot] = -sin, sin
        for d in range(half):
            swap[base + d + half, base + d] = swap[base + d, base + d + half] = 1.0
    put("rope_cos", c)
    put("rope_sin", s)
    put("rope_swap", swap)
    t = np.arange(16)
    put("pool_count", np.repeat(np.concatenate([1.0 / np.minimum(t + 1, 2 ** (g + 1)) for g in range(POOL_G)])[None, :], P, 0))
    return out


class Tile:

    def __init__(self, bank, n):
        self.bank, self.n, self.full = bank, n, None


class Tiles:

    def __init__(self):
        self.used = [0] * 8
        self.turn = {}
        self.order = []

    def take(self, banks, times=1):
        k = self.turn.get(banks, 0)
        self.turn[banks] = k + 1
        b = banks[k % len(banks)]
        self.used[b] += 1
        t = Tile(b, self.used[b])
        self.used[b] += times - 1
        self.order.append((t, times))
        return t

    def number(self, full):
        n = [0] * 8
        for t, times in self.order:
            if t.full is None:
                t.full = (full[t.bank], n[t.bank] + 1, 1)
                n[t.bank] += times


GEMM, AUX, HOLD = (0, 1, 2, 3), (4, 5, 6), (7,)
GATE_OF = {"y3": "gate3", "y2": "gate2", "y0": "gate0", "y1": "gate1", "yp": "gp", "ya": "ga"}
ORDER = {0: tuple(range(8)), 1: tuple(range(8)), 2: (7, 0, 1, 2, 3, 4, 5, 6), 3: tuple(range(8))}


def program(nc, A, out):
    ctx = ExitStack()
    with ctx:
        def sb(name, shape, dt=FP32):
            return ctx.enter_context(nc.sbuf_tensor(name, shape, dt))

        sems = {}

        def sem(name):
            if name not in sems:
                sems[name] = ctx.enter_context(nc.semaphore(name))
            return sems[name]

        raw = [sb(f"w_raw{i}", [P, UNIT]) for i in range(2)]
        w_hi = [sb(f"w_hi{i}", [P, UNIT], F32R) for i in range(2)]
        w_lo = [sb(f"w_lo{i}", [P, UNIT], F32R) for i in range(2)]
        x = sb("x", [P, KT, S])
        h_hi = sb("h_hi", [P, KT, S], F32R)
        h_lo = sb("h_lo", [P, KT, S], F32R)
        y_hi = sb("y_hi", [P, 4, S], F32R)
        y_lo = sb("y_lo", [P, 4, S], F32R)
        cst = sb("cst", [P, N_CONST])
        par = sb("par", [P, len(VECTORS) * P])
        mod = sb("mod", [P, 48])
        gain = sb("gain", [P, 5, KT])
        sq = sb("sq", [P, 2, S])
        rstd = sb("rstd", [P, S])
        tbuf = sb("tbuf", [P, 2, S])
        small = sb("small", [P, 256])
        bias_if = sb("bias_if", [MH, 2])
        gl_low = sb("gl_low", [GC, S + MIX])
        WORK = 17936
        work = sb("work", [P, WORK])
        bank = [ctx.enter_context(nc.psum_tensor(f"bank{b}", [P, 512], FP32)) for b in range(8)]

        def area(at, *shape):
            n = int(np.prod(shape))
            assert at + n <= WORK, (at, n)
            v = work[:, at:at + n]
            if len(shape) == 2:
                v = v.rearrange("p (a b) -> p a b", a=shape[0])
            if len(shape) == 3:
                v = v.rearrange("p (a b c) -> p a b c", a=shape[0], b=shape[1])
            return v

        def const(name):
            at, n = CONST_AT[name]
            return cst[:, at:at + n]

        def col(name, i=0, n=1):
            at = COLUMN[name]
            return par[:, at + i:at + i + n]

        ident = const("ident")

        x_tok, rows_in = area(0, TT, D), area(4096, len(VECTORS), P)
        ada_first = [area(4864 + UNIT * k, KT, 2 * P) for k in range(6)]
        gates, merged = area(0, KT, S), area(KT * S, KT, S)
        sc_z, sc_c, sc_acc = area(0, MT, 2 + S), area(1040, MT, S), area(2080, MT, S)
        cf_u, cf_s, cf_acc = area(4096, MT, 30 + S), area(5184, MT, S), area(6208, MT, S)
        R = 2 * KT * S
        ada_later = [area(R + UNIT * k, KT, 2 * P) for k in range(4)]

        def ada_place(n):
            return ada_first[n % 6] if n < 8 else ada_later[(n + 2) % 4]

        def ada_load(eng, n):
            eng.dma_start(ada_place(n), A["ada_w"][0][:, n * 2 * P:(n + 1) * 2 * P].rearrange("(k p) n -> p k n", p=P))\
               .then_inc(sem(f"ada_in{n % 8}"), 16)

        ADA_LOADED = {(0, 0): (8, 9), (0, 1): (10, 11), (0, 2): (12, 13), (0, 4): (14, 15),
                      (1, 0): (16, 17), (1, 1): (18, 19), (1, 2): (20, 21), (1, 3): (22, 23)}
        ADA_TURNED = {(0, 2): (8, 9), (0, 3): (10, 11), (0, 4): (12, 13),
                      (1, 1): (14, 15), (1, 2): (16, 17), (1, 3): (18, 19), (1, 4): (20, 21)}
        ml_q, ml_k, ml_o = area(R, MT, S), area(R + 1024, MT, S), area(R + 2048, MT, S)
        ml_v = area(R + 3072, TT, MH * (HD + 1))
        ml_p, ml_h, ml_nm = area(R + 4112, 2, TT, S), area(R + 8208, TT, MIX), area(R + 9232, S)
        ml_rows = area(R + 4112, 6, S)
        gl_q, gl_k, gl_r, gl_v = area(R, MT, S), area(R + 1024, MT, S), area(R + 2048, MT, S), area(R + 3072, TT, MIX)
        gl_bs, gl_e, gl_kd = area(R + 4096, MT, S), area(R + 5120, 2, S), area(R + 6144, MT, S)
        gl_u, gl_ab = area(R + 4096, HD, NC), area(R + 6144, HD, NC)
        gl_sq, gl_at, gl_o = area(R + 8192, S), area(R + 8704, TT, P), area(R + 9216, S)
        gl_a = small[:, 128:128 + MT * NC]
        gl_kdt = sq
        hid, cbuf, ybuf = area(0, FT, S), area(FT * S, 2, 2, S), area(FT * S + 4 * S, KT, S)
        pool_t, pooled = area(0, 3, 16 + S), area(1584, POOL_G, S)
        iq, ik = area(4096, 4, S), area(6144, S)
        at_q, at_k, at_v = area(R, 4, S), area(R + 2048, 4, S), area(R + 4096, TT, S)
        masks = [area(R + 6144 + P * (qt * (qt + 1) // 2), (qt + 1) * P) for qt in range(TT)]
        at_s, at_pt, pool_w = area(R + 7424, 2, S), area(R + 8448, 2, S), area(R + 7424, POOL_G, P)
        o_tok, gain_final = area(0, TT, D), area(FT * S + 4 * S, D)
        c_act, ml_gt, ml_mt, ml_d, ml_ms = small[:, 0:8], small[:, 48:64], small[:, 64:80], small[:, 96:100], small[:, 100:116]
        one = small[:, 249:250]
        iw_t, at_m, at_sum = small[:, 16:48], small[:, 192:208], small[:, 208:224]
        fin_s, eps = small[:, 224:236], small[:, 255:256]

        loaded = [sem("w_loaded0"), sem("w_loaded1")]
        hi_done = sem("w_hi_done")
        parted = [sem("w_parted0"), sem("w_parted1")]
        w_used = sem("w_used")
        full = [sem(f"bank_full{b}") for b in range(8)]
        read = [sem(f"bank_read{b}") for b in range(8)]

        def wait_full(eng, t, i=0):
            s, n, step = t.full
            eng.wait_ge(s, n + i * step)

        def wait_read(eng, t, i=0):
            eng.wait_ge(read[t.bank], t.n + i)

        def wait_free(pe, t, i=0):
            if t.n > 1:
                pe.wait_ge(read[t.bank], t.n - 1 + i)

        def done(ins, t):
            ins.then_inc(t.full[0], 1)

        def release(ins, t):
            ins.then_inc(read[t.bank], 1)

        class Chain:

            def __init__(self, eng, name):
                self.eng, self.sem, self.n = eng, sem(name), 0

            def tick(self, ins):
                ins.then_inc(self.sem, 1)
                self.n += 1
                return self.n

            def link(self, ins):
                self.eng.wait_ge(self.sem, self.tick(ins))

        U, unit = {}, 0
        for name, n in [("sc", 3), ("conf", 2), ("ifa", 1), ("ml", 4), ("gate3", 4), ("y3", 1), ("gla", 4),
                        ("gate2", 4), ("y2", 1), ("gate0", 4), ("y0", 1), ("gate1", 4), ("y1", 1),
                        ("wo", 4), ("up1", FT), ("down1", FT // 2),
                        ("pool", 2), ("q", 2), ("k", 2), ("v", 2), ("iq", 2), ("ikw", 1), ("gp", 4), ("yp", 2),
                        ("ga", 4), ("ya", 2), ("wo2", 4), ("up2", FT), ("down2", FT // 2)]:
            U[name] = unit
            unit += n
        N_UNITS = unit
        IFA = U["ifa"]

        def loaded_at(u):
            return 32 * (u // 2 + 1) + (16 if u >= IFA and (u - IFA) % 2 == 0 else 0)

        tiles, T = Tiles(), {}

        def take(name, banks, n=1, times=1):
            T.setdefault(name, []).extend(tiles.take(banks, times) for _ in range(n))

        def take_all(name):
            T[name] = [tiles.take((b,)) for b in range(8)]

        take("vec", AUX, len(VECTORS))
        take("xT", AUX, KT)
        take("ss0", HOLD)
        take("ada0", AUX)
        for name, n in (("sc", 6), ("conf", 4), ("ifa", 1), ("ml", 8)):
            take(name, GEMM, n)
        take("cf_mu", AUX)
        take("cf_var", AUX)
        take("ml_cols", AUX)
        for h in range(MH):
            for j in range(TT):
                take("ml_d", AUX)
                take("ml_qk", AUX)
            take("ml_n", AUX)
        take("ml_hT", AUX, MT)
        take("gate3", GEMM, 8)
        take("y3", GEMM, 8)
        take("gla", GEMM, 8)
        take("gl_z", AUX, MT)
        take("gl_kdT", AUX, MT)
        for t in range(MT):
            take("gl_u", AUX, TT)
            take("gl_a", AUX, 2)
            take("gl_o", HOLD)
            take("gl_ms", AUX)
        take("gate2", GEMM, 8)
        take("y2", GEMM, 8)
        for b in (0, 1):
            take(f"gate{b}", GEMM, 8)
            take(f"y{b}", GEMM, 8)
            if b == 0:
                take("ada1", AUX)
        take("wo", GEMM, 8)
        take("ss1", HOLD)
        take("ss2", HOLD)
        take("up1", GEMM, 4, FT // 2)
        take_all("down1")
        take("ss3", HOLD)
        take("ss4", HOLD)
        for name, n in (("pool", 4), ("q", 4), ("k", 4), ("v", 4), ("iq", 4), ("ikw", 1)):
            take(name, GEMM, n)
        take("pl", AUX, POOL_G)
        take("rope", AUX, 13)
        take("iwT", AUX)
        take("idx", AUX, 3 * NH2)
        for name in ("gp", "yp", "ga"):
            take(name, GEMM, 8)
        for qt in range(TT):
            for h in range(NH2 + 1):
                if h < NH2:
                    take("s", AUX)
                if h:
                    take("pt", AUX)
            take("o", HOLD)
            take("oT", AUX)
        take("ya", GEMM, 8)
        take("wo2", GEMM, 8)
        take("ss5", HOLD)
        take("up2", GEMM, 4, FT // 2)
        take_all("down2")
        take("fin", GEMM, 2 * TT)
        for name, per, step in [(n, 2, 1) for n in ("sc", "conf", "ml", "gla", "gate0", "gate1", "gate2", "gate3", "wo", "pool", "q", "k",
                                                    "v", "iq", "gp", "ga", "wo2")] + \
                [("up1", 2, 2), ("up2", 2, 2), ("ifa", 1, 1), ("ikw", 1, 1), ("yp", 4, 1), ("ya", 4, 1)] + \
                [(f"y{b}", 8, 1) for b in range(4)]:
            for n in range(per - 1, len(T[name]), per):
                T[name][n].full = (w_used, U[name] + (n + 1) // per, step)
        for name in ("down1", "down2"):
            T[name][7].full = (w_used, U[name] + FT // 2, 0)
        for n in range(6):
            T[f"ss{n}"][0].full = (sem("sq_used"), KT * (n + 1), 0)
        T["ada0"][0].full, T["ada1"][0].full = (sem("ada_turned"), 8, 0), (sem("ada_turned"), 24, 0)
        tiles.number(full)
        READ_FIRST = (7, 0, 1, 2, 3, 4, 5, 6)
        IN_ORDER = tuple(range(KT))

        block = ctx.enter_context(nc.Block())

        @block.sync
        def _(sp):
            def before(u, i=0):
                if u >= 2:
                    sp.wait_ge(parted[u % 2], u // 2 + i)

            def put(u, dst, src):
                sp.dma_start(dst, src).then_inc(loaded[u % 2], 16)

            def slot(u, kt):
                return raw[u % 2][:, :].rearrange("p (k n) -> p k n", k=kt)

            def cols(u, w, kt, c0, n, i=0):
                before(u, i)
                h = kt // 2
                for a in (0, h):
                    put(u, slot(u, kt)[:, a:a + h, 0:n],
                        w[a * P:(a + h) * P, c0 if isinstance(c0, slice) else bass.ds(c0, n)].rearrange("(k p) n -> p k n", p=P))

            def column_units(name, w, c0, n=4, kt=KT):
                for c in range(n):
                    cols(U[name] + c, w, kt, c0 + c * (UNIT // kt), UNIT // kt)

            def row_unit(u, w, r0, i=0):
                before(u, i)
                for q in range(2):
                    put(u, raw[u % 2][:, q * D:(q + 1) * D], w[bass.ds(r0 + q * P, P), :])

            def ffn_units(n, w_up, w_down):
                with sp.Fori(0, FT // 2) as i:
                    for k in range(2):
                        u = U["up" + n] + k
                        before(u, i)
                        for part in range(2):
                            put(u, slot(u, KT)[:, :, part * P:part * P + P],
                                w_up[:, bass.ds(i * (2 * P) + (part * FF + k * P), P)].rearrange("(k p) n -> p k n", p=P))
                row_unit(U["down" + n], w_down, 0)
                with sp.Fori(0, FT // 4) as i:
                    for k in (1, 2):
                        row_unit(U["down" + n] + k, w_down, i * (4 * P) + k * 2 * P, i)

            w, w2 = A["w_in"][0], A["w_in_2"][0]

            for n in range(8):
                if n >= 6:
                    sp.wait_ge(sem("ada_turned"), n - 5)
                ada_load(sp, n)
            u = U["sc"]
            for c0 in (C_SC + MIX, C_SC + 2 * MIX, C_SC, C_CONF + MIX, C_CONF):
                cols(u, w, KT, c0, MIX)
                u += 1
            before(IFA)
            for c0, n, at in ((C_MLIF, MH, 0), (C_MLIF + MH, MH, 32), (C_GLAA, GC, 64)):
                put(IFA, slot(IFA, KT)[:, :, at:at + n], w[:, c0:c0 + n].rearrange("(k p) n -> p k n", p=P))
            column_units("ml", w, C_ML)
            column_units("gate3", w, C_GATE + 3 * D)
            row_unit(U["y3"], A["w_sc_out"][0], 0)
            column_units("gla", w, C_GLA)
            column_units("gate2", w, C_GATE + 2 * D)
            row_unit(U["y2"], A["w_conf_out"][0], 0)
            column_units("gate0", w, C_GATE)
            row_unit(U["y0"], A["w_ml_out"][0], 0)
            column_units("gate1", w, C_GATE + D)
            row_unit(U["y1"], A["w_gla_out"][0], 0)
            column_units("wo", A["w_o"][0], 0)
            ffn_units("1", A["ffn_w_up"][0], A["ffn_w_down"][0])
            for name, c0 in (("pool", C_POOL), ("q", C_Q), ("k", C_K), ("v", C_V), ("iq", C_IQ)):
                column_units(name, w2, c0, 2)
            cols(U["ikw"], w2, KT, C_IK, IKW)
            column_units("gp", w2, C_GATE2)
            column_units("yp", A["w_pool_proj_2"][0], 0, 2, 4)
            column_units("ga", w2, C_GATE2 + D)
            column_units("ya", A["w_attn_proj_2"][0], 0, 2, 4)
            column_units("wo2", A["w_out_2"][0], 0)
            ffn_units("2", A["w_up_2"][0], A["w_down_2"][0])
            for tt in range(TT):
                sp.wait_ge(sem("out_ready"), tt + 1)
                sp.dma_start(out[0, tt * P:(tt + 1) * P, :], o_tok[:, tt, :]).then_inc(sem("stored"), 16)
            sp.wait_ge(sem("stored"), 16 * TT)

        @block.gpsimd
        def _(pool):
            pool.dma_start(cst[:, :], A["consts"][:, 0:N_CONST]).then_inc(sem("consts_in"), 16)
            pool.dma_start(bias_if[:, 0:1], A["ml_i_bias"].rearrange("a h -> h a")).then_inc(sem("bias_in"), 16)
            pool.dma_start(bias_if[:, 1:2], A["ml_f_bias"].rearrange("a h -> h a")).then_inc(sem("bias_in"), 16)
            pool.dma_start(gl_low[:, S:S + MIX], A["gla_w_a2"][0]).then_inc(sem("bias_in"), 16)
            pool.memset(eps, EPS).then_inc(sem("eps_set"), 1)
            pool.memset(one, 1.0).then_inc(sem("eps_set"), 1)
            wait_full(pool, T["xT"][KT - 1])
            pool.memset(sc_z[:, :, 0:2], 0.0).then_inc(sem("pads"), 1)
            wait_full(pool, T["ada0"][0])
            pool.memset(cf_u[:, :, 0:30], 0.0).then_inc(sem("pads"), 1)

            def lo(u):
                pool.wait_ge(hi_done, u + 1)
                pool.tensor_tensor(w_lo[u % 2][:, :], raw[u % 2][:, :], w_hi[u % 2][:, :].bitcast(FP32), ALU.subtract)\
                    .then_inc(parted[u % 2], 1)

            for u in range(U["gate2"] + 1):
                lo(u)

            for k in range(2):
                wait_read(pool, T["gla"][4 + k])
            wait_read(pool, T["ml_qk"][MH * TT - 1])
            wait_read(pool, T["ml_qk"][MH * TT - 2])
            for n in range(MT * TT):
                t, j = divmod(n, TT)
                if n:
                    wait_full(pool, T["gl_u"][n - 1])
                for hh in range(2):
                    h = 2 * t + hh
                    pool.tensor_tensor(tbuf[:, hh, :].rearrange("p (c d) -> p c d", c=CPT),
                                       gl_v[:, j, h * HD:(h + 1) * HD].unsqueeze(1).broadcast_to([P, CPT, HD]),
                                       const("chunk_of").unsqueeze(2).broadcast_to([P, CPT, HD]), ALU.mult)\
                        .then_inc(sem("gl_placed"), 1)
            for u in range(U["gate2"] + 1, U["up1"] + 1):
                lo(u)

            def hidden(n):
                pool.nop().then_inc(sem("hid" + n), 1)
                with pool.Fori(0, FT // 2) as i:
                    for k in range(2):
                        pool.wait_ge(sem("silu" + n), i * 2 + k + 1)
                        wait_read(pool, T["up" + n][2 * k + 1], i)
                        pool.tensor_tensor(work[:, bass.ds(i * (2 * S) + k * S, S)], cbuf[:, k, 0, :], cbuf[:, k, 1, :],
                                           ALU.mult).then_inc(sem("hid" + n), 1)

            hidden("1")
            pool.wait_ge(sem("x_ready"), 3 * KT)
            pool.dma_start(pool_w[:, :, :], A["pool_w_2"][0].rearrange("g c d -> c g d")).then_inc(sem("pool_w_in"), 16)
            pool.dma_start(cst[:, N_CONST - 2 * S:N_CONST], A["consts"][:, N_CONST:]).then_inc(sem("rope_in"), 16)
            pool.memset(pool_t[:, 0, 0:16], 0.0).then_inc(sem("pads"), 1)
            pool.wait_ge(sem("rope_in"), 16)
            for u in range(U["pool"] + 1, U["q"] + 1):
                lo(u)
            for n in range(13):
                if n < 8 and n % 2 == 0:
                    lo(U["q"] + n // 2 + 1)
                if n == 8:
                    lo(U["v"] + 1)
                    lo(U["v"] + 2)
                if n >= 8 and n % 2 == 0:
                    lo(U["iq"] + (n - 8) // 2 + 1)
                wait_full(pool, T["rope"][n])
                pool.tensor_tensor(tbuf[:, n % 2, :], tbuf[:, n % 2, :], const("rope_cos"), ALU.mult).then_inc(sem("rope_kept"), 1)
            for u in range(U["ikw"] + 2, U["up2"] + 1):
                lo(u)
            pool.wait_ge(sem("x_ready"), 4 * KT)
            pool.dma_start(gain_final, A["norm_final_g_2"].partition_broadcast(P)).then_inc(sem("gain_in"), 16)
            hidden("2")

        @block.scalar
        def _(act):
            ch = Chain(act, "act_step")
            for g, group in enumerate(VECTORS):
                r = 0
                for name, n in group:
                    base, _, tap = name.partition("/")
                    a = A[base]
                    if tap:
                        src = a[0, int(tap), :].rearrange("(t p) -> t p", p=P)
                    elif len(a.shape) == 3:
                        src = a[0].rearrange("k (t p) -> (k t) p", p=P)
                    else:
                        src = a[0].rearrange("(t p) -> t p", p=P)
                    act.dma_start(rows_in[r:r + n, g, :], src).then_inc(sem("vec_in"), 16)
                    r += n
                if g == 0:
                    for tt in range(TT):
                        act.dma_start(x_tok[:, tt, :], A["x"][0, tt * P:(tt + 1) * P, :]).then_inc(sem("x_in"), 16)

            def split(u, i=0, units=0):
                act.wait_ge(loaded[u % 2], loaded_at(u) + (i * 16 if units else 0))
                if u >= 2:
                    act.wait_ge(w_used, u - 1 + i)
                act.activation(w_hi[u % 2][:, :], raw[u % 2][:, :], ACT.Copy).then_inc(hi_done, 1)

            sqn = [0]

            def square(src):
                n = sqn[0]
                if n >= 2:
                    act.wait_ge(sem("sq_used"), n - 1)
                sqn[0] += 1
                return act.activation(sq[:, n % 2, :], src, ACT.Square)

            def squares(k):
                for c in range(KT):
                    act.wait_ge(sem("x_ready"), KT * k + c + 1)
                    c = ORDER[k][c]
                    square(x[:, c, :]).then_inc(sem("sq_ready"), 1)

            def rsqrt(t, src=None):
                wait_full(act, t)
                ch.link(act.activation(rstd[:, :], bank[t.bank][:, :], ACT.Ln, bias=eps))
                act.activation(rstd[:, :], rstd[:, :], ACT.Exp, scale=-0.5).then_inc(read[t.bank], 1)

            hn = [0]

            def norm_hi(shift=None):
                for c in range(KT):
                    hn[0] += 1
                    act.wait_ge(sem("h_t"), hn[0])
                    b = 0.0 if shift is None else mod[:, shift + c:shift + c + 1]
                    act.activation(h_hi[:, c, :], tbuf[:, c % 2, :], ACT.Identity, bias=b).then_inc(sem("h_hi"), 1)

            def y_split(src, k, n):
                act.wait_ge(sem("y_src"), n)
                act.activation(y_hi[:, k, :], src, ACT.Copy).then_inc(sem("y_hi"), 1)

            def out_of(t, dst, func, **kw):
                wait_full(act, t)
                src = bank[t.bank][:, :]
                if len(dst.shape) == 3:
                    src = src[:, 0:dst.shape[1] * dst.shape[2]].rearrange("p (a b) -> p a b", a=dst.shape[1])
                release(act.activation(dst, src, func, **kw), t)

            def gate_step(name, c, bias, u, used):
                split(u + 1)
                for k in range(2):
                    cc = 2 * c + k
                    if used is not None:
                        wait_read(act, T[used][cc])
                    out_of(T[name][cc], gates[:, cc, :], ACT.Sigmoid, **({} if bias is None else {"bias": col("merge_gate_b", bias + cc)}))

            wait_read(act, T["vec"][0])
            act.activation(c_act, col("c", 0, KT), ACT.Silu).then_inc(sem("c_act"), 1)
            squares(0)
            split(0)
            act.wait_ge(sem("eps_set"), 2)
            rsqrt(T["ss0"][0])
            norm_hi(0)

            u = U["sc"]
            split(u + 1)
            for c in range(2):
                out_of(T["sc"][c], sc_c[:, c, :], ACT.Copy)
            for k in (2, 3, 4):
                split(u + k)
            for c in range(2):
                out_of(T["conf"][c], cf_s[:, c, :], ACT.Sigmoid)
            split(IFA)
            split(U["ml"])
            for k in range(2):
                y_split(sc_acc[:, k, :], k, k + 1)
            t = T["ifa"][0]
            wait_full(act, t)
            act.wait_ge(sem("bias_in"), 48)
            act.activation(gl_low[:, 0:S], bank[t.bank][64:64 + GC, :], ACT.Copy)
            act.activation(ml_rows[0:MH, 0, :], bank[t.bank][0:MH, :], ACT.Identity, bias=bias_if[:, 0:1])
            ch.link(act.activation(ml_rows[0:MH, 1, :], bank[t.bank][32:32 + MH, :], ACT.Identity, bias=bias_if[:, 1:2]))
            ch.link(act.activation(ml_rows[0:MH, 2, :], ml_rows[0:MH, 1, :], ACT.Abs))
            ch.link(act.activation(ml_rows[0:MH, 2, :], ml_rows[0:MH, 2, :], ACT.Exp, scale=-1.0))
            release(act.activation(ml_rows[0:MH, 2, :], ml_rows[0:MH, 2, :], ACT.Ln, bias=1.0), t)
            u = U["ml"]
            for k, (dst, func, scale) in enumerate(((ml_q, ACT.Copy, LOWER), (ml_k, ACT.Copy, 1.0), (None, None, None),
                                                    (ml_o, ACT.Sigmoid, 1.0))):
                split(u + k + 1)
                if dst is not None:
                    for c in range(2):
                        out_of(T["ml"][2 * k + c], dst[:, c, :], func, scale=scale)
            for c in range(2):
                act.wait_ge(sem("cf_centered"), c + 1)
                act.activation(cf_s[:, c, :], cf_acc[:, c, :], ACT.Square).then_inc(sem("cf_sq"), 1)
            rsqrt(T["cf_var"][0])
            for c in range(2):
                act.wait_ge(sem("cf_scaled"), c + 1)
                ch.link(act.activation(cf_acc[:, c, :], cf_acc[:, c, :], ACT.Silu, bias=col("conf_ln_b", c)))
                act.activation(y_hi[:, 2 + c, :], cf_acc[:, c, :], ACT.Copy).then_inc(sem("y_hi"), 1)
            act.wait_ge(sem("ml_cols"), 1)
            act.activation(ml_mt, ml_mt, ACT.Exp, scale=-1.0).then_inc(sem("ml_floor"), 1)
            for n in range(MH * TT):
                h, j = divmod(n, TT)
                N = S - j * P
                wait_full(act, T["ml_d"][n])
                if n >= 2:
                    wait_read(act, T["ml_qk"][n - 2])
                release(act.activation(tbuf[:, n % 2, 0:N], bank[T["ml_d"][n].bank][:, 0:N], ACT.Exp,
                                       bias=ml_gt[:, j * MH + h:j * MH + h + 1]), T["ml_d"][n])
            act.wait_ge(sem("ml_ms"), 1)
            ch.link(act.activation(ml_ms, ml_ms, ACT.Ln, scale=1.0 / HD, bias=eps))
            act.activation(ml_ms, ml_ms, ACT.Exp, scale=-0.5).then_inc(sem("ml_rs"), 1)
            for c in range(4):
                gate_step("gate3", c, 3 * KT, U["gate3"] + c, None)
            split(U["y3"] + 1)
            act.wait_ge(w_used, U["y3"] + 1)
            for k in range(2):
                y_split(ml_q[:, k, :], k, 3 + k)
            u = U["gla"]
            act.wait_ge(sem("y_lo"), 6)
            for k, (dst, func, scale) in enumerate(((gl_q, ACT.Copy, LOWER), (gl_k, ACT.Copy, 1.0), (None, None, None),
                                                    (gl_r, ACT.Silu, 1.0))):
                split(u + k + 1)
                if dst is not None:
                    for c in range(2):
                        out_of(T["gla"][2 * k + c], dst[:, c, :], func, scale=scale)
            for c in range(MT):
                t = T["gl_z"][c]
                wait_full(act, t)
                ch.link(act.activation(gl_e[:, c, :], bank[t.bank][:, :], ACT.Abs, bias=col("gla_a_bias", c)))
                ch.link(act.activation(gl_e[:, c, :], gl_e[:, c, :], ACT.Exp, scale=-1.0))
                act.activation(gl_e[:, c, :], gl_e[:, c, :], ACT.Ln, bias=1.0).then_inc(sem("gl_ln"), 1)
            TAU = 1.0 / 16.0
            for c in range(MT):
                act.wait_ge(sem("gl_bs"), c + 1)
                if c == 0:
                    act.wait_ge(sem("gl_bs"), 2)
                if c:
                    act.wait_ge(sem("gl_scaled"), c)
                act.activation(gl_e[:, 0, :], gl_bs[:, c, :], ACT.Exp, scale=TAU)
                act.activation(gl_e[:, 1, :], gl_bs[:, c, :], ACT.Exp, scale=-TAU)
                act.activation(gl_kd[:, c, :], gl_kd[:, c, :], ACT.Exp, scale=TAU)
                act.activation(gl_a[:, c * NC:(c + 1) * NC], gl_bs[:, c, GC - 1::GC], ACT.Exp, scale=TAU).then_inc(sem("gl_exp"), 1)
            for c in range(MT):
                t = T["gl_o"][c]
                wait_full(act, t)
                if c:
                    act.wait_ge(sem("y_src"), 4 + c)
                    wait_full(act, T["gl_ms"][c - 1])
                act.activation(gl_o, bank[t.bank][:, :], ACT.Copy)
                release(act.activation(gl_sq, bank[t.bank][:, :], ACT.Square), t)
                rsqrt(T["gl_ms"][c])
            for c in range(4):
                gate_step("gate2", c, 2 * KT, U["gate2"] + c, "y3")
            split(U["y2"] + 1)
            act.wait_ge(w_used, U["y2"] + 1)
            for k in range(2):
                y_split(gl_k[:, k, :], 2 + k, 5 + k)

            def ada_more(b, c):
                for n in ADA_LOADED.get((b, c), ()):
                    if n == 8:
                        act.wait_ge(sem("y_lo"), 8)
                    if n >= 12:
                        act.wait_ge(sem("ada_turned"), n - 3)
                    ada_load(act, n)

            for b, used in ((0, "y2"), (1, "y0")):
                for c in range(4):
                    gate_step(f"gate{b}", c, b * KT, U[f"gate{b}"] + c, used)
                    ada_more(b, c)
                split(U[f"y{b}"] + 1)
                ada_more(b, 4)

            def merged_hi(n):
                for c in range(KT):
                    act.wait_ge(sem("added"), KT * n + c + 1)
                    act.activation(h_hi[:, c, :], merged[:, c, :], ACT.Copy).then_inc(sem("h_hi"), 1)

            def keep_and_square(name, order):
                for c in order:
                    t = T[name][c]
                    wait_full(act, t)
                    act.activation(ybuf[:, c, :], bank[t.bank][:, :], ACT.Copy)
                    n = sqn[0]
                    act.wait_ge(sem("sq_used"), n - 1)
                    act.activation(sq[:, n % 2, :], bank[t.bank][:, :], ACT.Square).then_inc(read[t.bank], 1)
                    sqn[0] += 1

            merged_hi(2)
            for c in range(4):
                split(U["wo"] + c + 1)
                keep_and_square("wo", (2 * c, 2 * c + 1))
            rsqrt(T["ss1"][0])
            squares(1)
            rsqrt(T["ss2"][0])
            norm_hi(3 * KT)

            def ffn(n, taps, bias):
                up, down = U["up" + n], U["down" + n]
                with act.Fori(0, FT // 2) as i:
                    for k in range(2):
                        split(up + k + 1, i * 2, 2)
                        act.wait_ge(sem("hid" + n), i * 2 + 1)
                        for part in range(2):
                            t = T["up" + n][2 * k + part]
                            wait_full(act, t, i)
                            at = COLUMN[taps[2]] + part * FT + k
                            kw = {}
                            if bias:
                                kw["bias"] = par[:, bass.ds(i * 2 + (COLUMN[bias] + part * FT + k), 1)]
                            act.activation(cbuf[:, k, part, :], bank[t.bank][:, :], ACT.Identity,
                                           scale=par[:, bass.ds(i * 2 + at, 1)], **kw).then_inc(sem("center" + n), 1)
                        wait_read(act, T["up" + n][2 * k], i)
                        act.activation(cbuf[:, k, 0, :], cbuf[:, k, 0, :], ACT.Silu).then_inc(sem("silu" + n), 1)

                def part_hi(d, i=0, at=None):
                    act.wait_ge(sem("hid" + n), 2 * d + 3 + i * 2)
                    if d >= 2:
                        act.wait_ge(w_used, down + d - 1 + i)
                    k = 2 * (d % 2)
                    act.activation(y_hi[:, k:k + 2, :].rearrange("p a b -> p (a b)"), work[:, bass.ds(i * (2 * S) + d * 2 * S, 2 * S)],
                                   ACT.Copy).then_inc(sem("down_hi" + n), 1)

                part_hi(0)
                split(down + 1)
                part_hi(1)
                split(down + 2)
                part_hi(2)
                with act.Fori(0, 4) as i:
                    for d in (2, 3):
                        split(down + d + 1, i * 2, 2)
                        part_hi(d + 1, i * 2)
                if down + FT // 2 < N_UNITS:
                    split(down + FT // 2)

            ffn("1", ("ffn_dw_w/0", "ffn_dw_w/1", "ffn_dw_w/2"), None)
            keep_and_square("down1", READ_FIRST)
            rsqrt(T["ss3"][0])
            squares(2)
            rsqrt(T["ss4"][0])
            norm_hi()

            u = U["pool"]
            act.wait_ge(sem("x_ready"), 3 * KT)
            for g in range(POOL_G):
                if g % 2 == 0:
                    split(u + g // 2 + 1)
                if g:
                    act.wait_ge(sem("pooled"), g)
                out_of(T["pool"][g], pool_t[:, 0, 16:16 + S], ACT.Copy)
            for g in range(POOL_G):
                t = T["pl"][g]
                wait_full(act, t)
                act.activation(y_hi[:, g, :], bank[t.bank][:, :], ACT.Identity, scale=col("pool_scale_2", g)).then_inc(sem("y_hi"), 1)
            rn = [0]

            def rotary(t, scale):
                n = rn[0]
                if n >= 2:
                    act.wait_ge(sem("roped"), n - 1)
                rn[0] += 1
                return n % 2

            for name, scale in (("q", LOWER), ("k", 1.0)):
                for c in range(4):
                    if c % 2 == 0:
                        split(U[name] + c // 2 + 1)
                    k = rotary(None, None)
                    out_of(T[name][c], tbuf[:, k, :], ACT.Copy, scale=scale)
            for c in range(2):
                split(U["v"] + c + 1)
            for c in range(4):
                if c % 2 == 0:
                    split(U["iq"] + c // 2 + 1)
                k = rotary(None, None)
                out_of(T["iq"][c], tbuf[:, k, :], ACT.Copy)
            split(U["ikw"] + 1)
            t = T["ikw"][0]
            wait_full(act, t)
            k = rotary(None, None)
            act.activation(rstd[0:NH2, :], bank[t.bank][HD:HD + NH2, :], ACT.Copy, scale=float(NH2) ** -0.5)
            act.activation(tbuf[0:HD, k, :], bank[t.bank][0:HD, :], ACT.Copy)
            release(act.activation(tbuf[HD:P, k, :], bank[t.bank][0:HD, :], ACT.Copy), t)

            def indexer(qt):
                N = (qt + 1) * P
                for h in range(NH2):
                    n = (qt - 1) * NH2 + h
                    t = T["idx"][n]
                    wait_full(act, t)
                    if n >= 2:
                        act.wait_ge(sem("idx_used"), n - 1)
                    else:
                        act.wait_ge(sem("roped"), 13)
                    release(act.activation(tbuf[:, n % 2, 0:N], bank[t.bank][:, 0:N], ACT.Relu, scale=LOWER), t)

            indexer(1)
            for c in range(2):
                gate_step("gp", c, None, U["gp"] + c, None)
            indexer(2)
            for c in range(2, 4):
                gate_step("gp", c, None, U["gp"] + c, None)
            indexer(3)
            for c in range(2):
                split(U["yp"] + c + 1)
            for c in range(4):
                gate_step("ga", c, None, U["ga"] + c, "yp")

            def attention(qt):
                N = (qt + 1) * P
                for h in range(NH2 + 1):
                    if h < NH2:
                        n = qt * NH2 + h
                        act.wait_ge(sem("at_max"), n + 1)
                        act.activation(at_s[:, n % 2, 0:N], at_s[:, n % 2, 0:N], ACT.Exp, bias=at_m[:, n % 16:n % 16 + 1],
                                       accum_out=at_sum[:, n % 16:n % 16 + 1]).then_inc(sem("at_exp"), 1)
                    if h:
                        n = qt * NH2 + h - 1
                        t = T["pt"][n]
                        wait_full(act, t)
                        if n >= 2:
                            act.wait_ge(sem("at_pv"), n - 1)
                        release(act.activation(at_pt[:, n % 2, 0:N], bank[t.bank][:, 0:N], ACT.Copy), t)
                t = T["oT"][qt]
                wait_full(act, t)
                act.activation(y_hi[:, :, qt * P:(qt + 1) * P], bank[t.bank][:, :].rearrange("p (a b) -> p a b", a=4), ACT.Copy)\
                    .then_inc(sem("y_hi"), 1)

            for qt in range(TT):
                attention(qt)
            for c in range(2):
                split(U["ya"] + c + 1)
            merged_hi(3)
            for c in range(4):
                split(U["wo2"] + c + 1)
            squares(3)
            rsqrt(T["ss5"][0])
            norm_hi()
            ffn("2", ("conv_w_2/0", "conv_w_2/1", "conv_w_2/2"), "conv_b_2")
            for tt in range(TT):
                for k in range(2):
                    t = T["fin"][2 * tt + k]
                    wait_full(act, t)
                    act.activation(tbuf[:, k, :], bank[t.bank][:, :], ACT.Square,
                                   accum_out=fin_s[:, 2 * tt + k:2 * tt + k + 1]).then_inc(sem("fin_sq"), 1)
                act.wait_ge(sem("fin_sum"), tt + 1)
                r = fin_s[:, 8 + tt:9 + tt]
                ch.link(act.activation(r, r, ACT.Ln, scale=1.0 / D, bias=eps))
                act.activation(r, r, ACT.Exp, scale=-0.5).then_inc(sem("fin_rstd"), 1)

        @block.tensor
        def _(pe):
            def weights_ready(u, i=0):
                pe.wait_ge(parted[u % 2], u // 2 + 1 + i)

            def three(dst, u, at, n, hi, lo, first, last):
                s = u % 2
                pe.matmul(dst, w_hi[s][:, at:at + n], hi, start=first, stop=False)
                pe.matmul(dst, w_hi[s][:, at:at + n], lo, start=False, stop=False)
                return pe.matmul(dst, w_lo[s][:, at:at + n], hi, start=False, stop=last)

            def three_v(dst, u, at, n, hi, lo, first, last):
                s = u % 2
                pe.matmul(dst, hi, w_hi[s][:, at:at + n], start=first, stop=False)
                pe.matmul(dst, lo, w_hi[s][:, at:at + n], start=False, stop=False)
                return pe.matmul(dst, hi, w_lo[s][:, at:at + n], start=False, stop=last)

            def ada_columns(t, n, first):
                if n == first:
                    wait_free(pe, t)
                pe.wait_ge(sem("ada_summed"), n + 1)
                for k in range(2):
                    at = 2 * (n - first) + k
                    mm = pe.matmul(bank[t.bank][:, at:at + 1], ada_place(n)[:, 0, k * P:(k + 1) * P], one, start=True, stop=True)
                mm.then_inc(sem("ada_turned"), 1)

            hseen = [0]

            def column_unit(u, tl, kt=KT, hi=h_hi, lo=h_lo, i=0, j=0, rows=P, fresh=False):
                weights_ready(u, j)
                C = UNIT // kt
                for n, t in enumerate(tl):
                    wait_free(pe, t, j)
                    for k in range(kt):
                        if fresh and n == 0:
                            pe.wait_ge(sem("h_ready"), hseen[0] + k + 1)
                        mm = three(bank[t.bank][0:rows, :], u, k * C + n * P, rows, hi[:, k, :], lo[:, k, :], k == 0, k == kt - 1)
                    done(mm, t)
                if fresh:
                    hseen[0] += kt

            def token_unit(u, tl):
                weights_ready(u)
                for n, t in enumerate(tl):
                    wait_free(pe, t)
                    for m in range(2):
                        for k in range(KT):
                            tok = slice((2 * n + m) * P, (2 * n + m + 1) * P)
                            mm = three_v(bank[t.bank][:, m * 256:(m + 1) * 256], u, k * 256, 256, h_hi[:, k, tok], h_lo[:, k, tok],
                                         k == 0, k == KT - 1)
                    done(mm, t)

            def turn(t, parts):
                wait_free(pe, t)
                for at, src in parts:
                    r, n = src.shape[0], src.shape[1]
                    mm = pe.transpose(bank[t.bank][0:n, at:at + r], src, ident[0:r, 0:r])
                done(mm, t)

            sn = [0]

            def mean_square(t, banks=None, cs=range(KT)):
                if cs[0] == 0:
                    wait_free(pe, t)
                for c in cs:
                    n = sn[0]
                    if banks is None:
                        mean_square.direct += 1
                        pe.wait_ge(sem("sq_ready"), mean_square.direct)
                    else:
                        wait_read(pe, banks[c])
                    mm = pe.matmul(bank[t.bank][:, :], const("ones_d"), sq[:, n % 2, :], start=c == 0, stop=c == KT - 1)
                    mm.then_inc(sem("sq_used"), 1)
                    sn[0] += 1
            mean_square.direct = 0

            pe.wait_ge(sem("consts_in"), 16)
            pe.wait_ge(sem("vec_in"), 16 * N_VECTORS)
            for g, group in enumerate(VECTORS):
                turn(T["vec"][g], [(0, rows_in[0:sum(n for _, n in group), g, :])])
            pe.wait_ge(sem("x_in"), 16 * TT)
            for c in range(KT):
                turn(T["xT"][c], [(tt * P, x_tok[:, tt, c * P:(c + 1) * P]) for tt in range(TT)])
            mean_square(T["ss0"][0])
            pe.wait_ge(sem("eps_set"), 2)
            for n in range(8):
                ada_columns(T["ada0"][0], n, 0)
            u = U["sc"]
            for k in range(3):
                column_unit(u + k, T["sc"][2 * k:2 * k + 2], fresh=k == 0)
            for k in range(2):
                column_unit(U["conf"] + k, T["conf"][2 * k:2 * k + 2])
            column_unit(IFA, T["ifa"])
            for k in range(4):
                (token_unit if k == 2 else column_unit)(U["ml"] + k, T["ml"][2 * k:2 * k + 2])

            for name, s_name in (("cf_mu", "cf_conv"), ("cf_var", "cf_sq")):
                t = T[name][0]
                wait_free(pe, t)
                for c in range(MT):
                    pe.wait_ge(sem(s_name), c + 1)
                    mm = pe.matmul(bank[t.bank][:, :], const("ones_mix"), (cf_acc if name == "cf_mu" else cf_s)[:, c, :],
                                   start=c == 0, stop=c == MT - 1)
                done(mm, t)

            pe.wait_ge(sem("ml_gates"), 1)
            turn(T["ml_cols"][0], [(r * 16 + j * MH, ml_rows[0:MH, 4 + r, j * P:(j + 1) * P]) for r in range(2) for j in range(TT)])

            def ml_scores(h, j):
                n = h * TT + j
                t, N, lo = T["ml_d"][n], S - j * P, (h % 2) * HD
                wait_free(pe, t)
                pe.matmul(bank[t.bank][:, 0:N], const("sel")[0:MH, h * P:(h + 1) * P], ml_nm[0:MH, j * P:S], start=True, stop=False)
                done(pe.matmul(bank[t.bank][:, 0:P], ident, const("causal_st"), start=False, stop=True), t)
                t = T["ml_qk"][n]
                wait_free(pe, t)
                done(pe.matmul(bank[t.bank][:, 0:N], ml_k[lo:lo + HD, h // 2, j * P:(j + 1) * P], ml_q[lo:lo + HD, h // 2, j * P:S],
                               start=True, stop=True), t)

            def ml_values(h):
                t = T["ml_n"][h]
                wait_free(pe, t)
                for i in range(TT):
                    wait_read(pe, T["ml_qk"][h * TT + i])
                    for j in range(i + 1):
                        mm = pe.matmul(bank[t.bank][:, i * (HD + 1):(i + 1) * (HD + 1)], ml_p[:, h % 2, j, i * P:(i + 1) * P],
                                       ml_v[:, j, h * (HD + 1):(h + 1) * (HD + 1)], start=j == 0, stop=j == i)
                done(mm, t)

            for c in range(2):
                wait_read(pe, T["ml"][c])
                wait_read(pe, T["ml"][2 + c])
                wait_read(pe, T["ml"][4 + c])
            for h in range(MH):
                for j in range(TT):
                    ml_scores(h, j)
                ml_values(h)
            pe.wait_ge(sem("ml_normed"), 1)
            for c in range(MT):
                turn(T["ml_hT"][c], [(i * P, ml_h[:, i, c * P:(c + 1) * P]) for i in range(TT)])

            def gate_units(name):
                for c in range(4):
                    column_unit(U[name] + c, T[name][2 * c:2 * c + 2])

            def branch_unit(name, k0, n):
                pe.wait_ge(sem("y_lo"), n)
                column_unit(U[name], T[name], 2, y_hi[:, k0:k0 + 2, :], y_lo[:, k0:k0 + 2, :])

            gate_units("gate3")
            branch_unit("y3", 0, 2)
            for k in range(4):
                (token_unit if k == 2 else column_unit)(U["gla"] + k, T["gla"][2 * k:2 * k + 2])

            for c in range(MT):
                t = T["gl_z"][c]
                wait_free(pe, t)
                done(pe.matmul(bank[t.bank][:, :], gl_low[:, S + c * P:S + (c + 1) * P], gl_low[:, 0:S], start=True, stop=True), t)
            for c in range(MT):
                pe.wait_ge(sem("gl_kd"), c + 1)
                turn(T["gl_kdT"][c], [(j * P, gl_kd[:, c, j * P:(j + 1) * P]) for j in range(TT)])
            for c in range(MT):
                wait_read(pe, T["gl_kdT"][c])
                for j in range(TT):
                    n = c * TT + j
                    t = T["gl_u"][n]
                    wait_free(pe, t)
                    pe.wait_ge(sem("gl_placed"), 2 * n + 2)
                    for hh in range(2):
                        mm = pe.matmul(bank[t.bank][hh * HD:(hh + 1) * HD, :], gl_kdt[:, c, j * P + hh * HD:j * P + (hh + 1) * HD],
                                       tbuf[:, hh, :], start=True, stop=True)
                    done(mm, t)
                o = T["gl_o"][c]
                wait_free(pe, o)
                for hh in range(2):
                    n, rows = 2 * c + hh, slice(hh * HD, (hh + 1) * HD)
                    t = T["gl_a"][n]
                    wait_free(pe, t)
                    pe.wait_ge(sem("gl_ks"), c + 1)
                    for j in range(TT):
                        mm = pe.matmul(bank[t.bank][:, j * P:(j + 1) * P], gl_k[rows, c, j * P:(j + 1) * P],
                                       gl_q[rows, c, j * P:(j + 1) * P], start=True, stop=True)
                    done(mm, t)
                    wait_read(pe, t)
                    h = 2 * c + hh
                    for j in range(TT):
                        mm = pe.matmul(bank[o.bank][rows, j * P:(j + 1) * P], gl_v[:, j, h * HD:(h + 1) * HD], gl_at[:, j, :],
                                       start=j == 0, stop=False, skip_group_check=True)
                    mm.then_inc(sem("gl_at_used"), 1)
                    pe.wait_ge(sem("gl_state"), c + 1)
                    for k in range(1, NC):
                        mm = pe.matmul(bank[o.bank][rows, k * GC:(k + 1) * GC], gl_u[rows, :, k - 1], gl_q[rows, c, k * GC:(k + 1) * GC],
                                       start=False, stop=k == NC - 1, skip_group_check=True)
                done(mm, o)
                wait_read(pe, o)
                t = T["gl_ms"][c]
                wait_free(pe, t)
                done(pe.matmul(bank[t.bank][:, :], const("ones_head"), gl_sq, start=True, stop=True), t)

            gate_units("gate2")
            branch_unit("y2", 2, 4)
            for k in range(2):
                for c in range(4):
                    column_unit(U[f"gate{k}"] + c, T[f"gate{k}"][2 * c:2 * c + 2])
                    for p in ADA_TURNED.get((k, c), ()):
                        ada_columns(T["ada1"][0], p, 8)
                branch_unit(f"y{k}", 2 * k, 6 + 2 * k)
                for p in ADA_TURNED[(k, 4)]:
                    ada_columns(T["ada1"][0], p, 8)
            for c in range(4):
                column_unit(U["wo"] + c, T["wo"][2 * c:2 * c + 2], fresh=c == 0)
                if c == 2:
                    for p in (22, 23):
                        ada_columns(T["ada1"][0], p, 8)
                if c:
                    mean_square(T["ss1"][0], T["wo"], (2 * c - 2, 2 * c - 1))
            mean_square(T["ss1"][0], T["wo"], (6, 7))
            mean_square(T["ss2"][0])

            def ffn(n):
                up, down = U["up" + n], U["down" + n]
                for k in range(KT):
                    pe.wait_ge(sem("h_ready"), hseen[0] + k + 1)
                hseen[0] += KT
                with pe.Fori(0, FT // 2) as i:
                    for k in range(2):
                        column_unit(up + k, T["up" + n][2 * k:2 * k + 2], i=i * 2, j=i)

                def down_unit(d, i=0, first=False, last=False):
                    u = down + d
                    weights_ready(u, i)
                    pe.wait_ge(sem("down_lo" + n), d + 1 + i * 2)
                    for c in range(KT):
                        t = T["down" + n][c]
                        if first:
                            wait_free(pe, t)
                        for q in range(2):
                            k = 2 * (d % 2) + q
                            mm = three(bank[t.bank][:, :], u, q * D + c * P, P, y_hi[:, k, :], y_lo[:, k, :],
                                       first and q == 0, last and q == 1)
                        if last:
                            done(mm, t)
                    if not last:
                        mm.then_inc(w_used, 1)

                down_unit(0, first=True)
                down_unit(1)
                with pe.Fori(0, 4) as i:
                    for d in (2, 3):
                        down_unit(d, i)
                down_unit(10, last=True)

            ffn("1")
            mean_square(T["ss3"][0], [T["down1"][c] for c in READ_FIRST])
            mean_square(T["ss4"][0])

            for k in range(2):
                column_unit(U["pool"] + k, T["pool"][2 * k:2 * k + 2], fresh=k == 0)
            rn = [0]

            def swap(name):
                n = rn[0]
                t = T["rope"][n]
                wait_free(pe, t)
                done(pe.matmul(bank[t.bank][:, :], const("rope_swap"), tbuf[:, n % 2, :], start=True, stop=True), t)
                rn[0] += 1

            for g in range(POOL_G):
                t = T["pl"][g]
                wait_free(pe, t)
                pe.wait_ge(sem("pool_w_in"), 16)
                pe.wait_ge(sem("pooled"), g + 1)
                done(pe.matmul(bank[t.bank][:, :], pool_w[:, g, :], pooled[:, g, :], start=True, stop=True), t)
            for name in ("q", "k"):
                for k in range(2):
                    column_unit(U[name] + k, T[name][2 * k:2 * k + 2])
                    for c in range(2):
                        wait_read(pe, T[name][2 * k + c])
                        swap(name)
            for k in range(2):
                token_unit(U["v"] + k, T["v"][2 * k:2 * k + 2])
            for k in range(2):
                column_unit(U["iq"] + k, T["iq"][2 * k:2 * k + 2])
                for c in range(2):
                    wait_read(pe, T["iq"][2 * k + c])
                    swap("iq")
            column_unit(U["ikw"], T["ikw"], rows=P)
            wait_read(pe, T["ikw"][0])
            swap("ikw")
            turn(T["iwT"][0], [(qt * NH2, rstd[0:NH2, qt * P:(qt + 1) * P]) for qt in range(TT)])

            def indexer(qt):
                pe.wait_ge(sem("roped"), 13)
                for h in range(NH2):
                    t, lo = T["idx"][(qt - 1) * NH2 + h], (h % 2) * HD
                    wait_free(pe, t)
                    done(pe.matmul(bank[t.bank][:, 0:(qt + 1) * P], iq[lo:lo + HD, h // 2, qt * P:(qt + 1) * P],
                                   ik[lo:lo + HD, 0:(qt + 1) * P], start=True, stop=True), t)

            def gate_two(name, c0, c1):
                for c in range(c0, c1):
                    column_unit(U[name] + c, T[name][2 * c:2 * c + 2])

            def proj_units(name):
                for c in range(2):
                    column_unit(U[name] + c, T[name][4 * c:4 * c + 4], 4, y_hi, y_lo)

            indexer(1)
            gate_two("gp", 0, 2)
            indexer(2)
            gate_two("gp", 2, 4)
            indexer(3)
            pe.wait_ge(sem("y_lo"), 8 + POOL_G)
            proj_units("yp")
            gate_two("ga", 0, 4)

            def scores(qt, h):
                n, lo = qt * NH2 + h, (h % 2) * HD
                t = T["s"][n]
                wait_free(pe, t)
                done(pe.matmul(bank[t.bank][:, 0:(qt + 1) * P], at_q[lo:lo + HD, h // 2, qt * P:(qt + 1) * P],
                               at_k[lo:lo + HD, h // 2, 0:(qt + 1) * P], start=True, stop=True), t)

            def turn_weights(qt, h):
                n = qt * NH2 + h
                pe.wait_ge(sem("at_exp"), n + 1)
                turn(T["pt"][n], [(kb * P, at_s[:, n % 2, kb * P:(kb + 1) * P]) for kb in range(qt + 1)])

            def weigh_values(qt, h):
                n = qt * NH2 + h
                wait_read(pe, T["pt"][n])
                o = T["o"][qt]
                if h == 0:
                    wait_free(pe, o)
                for kb in range(qt + 1):
                    mm = pe.matmul(bank[o.bank][:, h * HD:(h + 1) * HD], at_pt[:, n % 2, kb * P:(kb + 1) * P],
                                   at_v[:, kb, h * HD:(h + 1) * HD], start=kb == 0, stop=kb == qt)
                mm.then_inc(sem("at_pv"), 1)

            for qt in range(TT):
                for h in range(NH2 + 1):
                    if h < NH2:
                        scores(qt, h)
                    if h:
                        turn_weights(qt, h - 1)
                        weigh_values(qt, h - 1)
                pe.wait_ge(sem("o_scaled"), qt + 1)
                turn(T["oT"][qt], [(c * P, tbuf[:, 0, c * P:(c + 1) * P]) for c in range(4)])
            pe.wait_ge(sem("y_lo"), 8 + POOL_G + TT)
            proj_units("ya")
            for c in range(4):
                column_unit(U["wo2"] + c, T["wo2"][2 * c:2 * c + 2], fresh=c == 0)
            mean_square(T["ss5"][0])
            ffn("2")
            for tt in range(TT):
                for k in range(2):
                    for c in range(4):
                        pe.wait_ge(sem("x_ready"), 5 * KT)
                    turn(T["fin"][2 * tt + k], [(c * P, x[:, 4 * k + c, tt * P:(tt + 1) * P]) for c in range(4)])

        @block.vector
        def _(dve):
            ch = Chain(dve, "dve_step")

            def lo(u, i=0):
                dve.wait_ge(hi_done, u + 1 + i)
                dve.tensor_tensor(w_lo[u % 2][:, :], raw[u % 2][:, :], w_hi[u % 2][:, :].bitcast(FP32), ALU.subtract)\
                   .then_inc(parted[u % 2], 1)

            hn, rs = [0], [0]

            def norm_lo(ss, gains, shift=None):
                wait_read(dve, T[ss][0])
                for c in range(KT + 1):
                    if c < KT:
                        if c >= 2:
                            dve.wait_ge(sem("h_ready"), hn[0])
                        dve.scalar_tensor_tensor(out=tbuf[:, c % 2, :], in0=x[:, c, :], scalar=gains[:, c:c + 1], in1=rstd[:, :],
                                                 op0=ALU.mult, op1=ALU.mult).then_inc(sem("h_t"), 1)
                    if c:
                        k = c - 1
                        hn[0] += 1
                        dve.wait_ge(sem("h_hi"), hn[0])
                        dve.scalar_tensor_tensor(out=h_lo[:, k, :], in0=tbuf[:, k % 2, :],
                                                 scalar=0.0 if shift is None else mod[:, shift + k:shift + k + 1],
                                                 in1=h_hi[:, k, :].bitcast(FP32), op0=ALU.add, op1=ALU.subtract)\
                           .then_inc(sem("h_ready"), 1)

            def y_lo_of(src, k, n):
                dve.wait_ge(sem("y_hi"), n)
                dve.tensor_tensor(y_lo[:, k, :], src, y_hi[:, k, :].bitcast(FP32), ALU.subtract).then_inc(sem("y_lo"), 1)

            for g, group in enumerate(VECTORS):
                t, n = T["vec"][g], sum(m for _, m in group)
                wait_full(dve, t)
                release(dve.tensor_copy(par[:, g * P:g * P + n], bank[t.bank][:, 0:n]), t)
            for c in range(KT):
                wait_full(dve, T["xT"][c])
                dve.tensor_copy(x[:, c, :], bank[T["xT"][c].bank][:, :]).then_inc(sem("x_ready"), 1)
                dve.wait_ge(sem("x_ready"), c + 1)
                dve.nop().then_inc(read[T["xT"][c].bank], 1)
            dve.wait_ge(sem("c_act"), 1)

            def ada_sum(n, unit):
                dve.wait_ge(sem(f"ada_in{n % 8}"), 16 * (n // 8 + 1))
                ch.link(dve.tensor_scalar(unit[:, 0, :], unit[:, 0, :], c_act[:, 0:1], None, ALU.mult))
                for k in range(1, KT):
                    ins = dve.scalar_tensor_tensor(out=unit[:, 0, :], in0=unit[:, k, :], scalar=c_act[:, k:k + 1], in1=unit[:, 0, :],
                                                   op0=ALU.mult, op1=ALU.add)
                    if k < KT - 1:
                        ch.link(ins)
                ins.then_inc(sem("ada_summed"), 1)

            def ada_out(t, at, n):
                wait_full(dve, t)
                release(dve.tensor_tensor(mod[:, at:at + n], bank[t.bank][:, 0:n], col("ada_b", at, n), ALU.add), t)

            for n in range(8):
                ada_sum(n, ada_place(n))
            ada_out(T["ada0"][0], 0, 2 * KT)

            def scale_gain(k, g, s):
                dve.scalar_tensor_tensor(out=gain[:, k, :], in0=mod[:, s:s + KT], scalar=1.0, in1=col(g, 0, KT),
                                         op0=ALU.add, op1=ALU.mult)

            wait_read(dve, T["ada0"][0])
            ch.link(dve.scalar_tensor_tensor(out=gain[:, 0, :], in0=mod[:, KT:2 * KT], scalar=1.0, in1=col("tm_pre_g", 0, KT),
                                             op0=ALU.add, op1=ALU.mult))
            norm_lo("ss0", gain[:, 0, :], 0)

            u = U["sc"]
            dve.wait_ge(sem("pads"), 2)
            for c in range(2):
                t = T["sc"][2 + c]
                wait_read(dve, T["sc"][c])
                wait_full(dve, t)
                release(dve.tensor_tensor(sc_z[:, c, 2:2 + S], bank[t.bank][:, :], sc_c[:, c, :], ALU.mult), t)
            for c in range(2):
                wait_read(dve, T["sc"][2 + c])
                ch.tick(dve.tensor_scalar(sc_acc[:, c, :], sc_z[:, c, 2:2 + S], col("sc_dw_w", 2 * MT + c), None, ALU.mult))
            for tap in (1, 0):
                for c in range(2):
                    dve.wait_ge(ch.sem, ch.n - 1)
                    ch.tick(dve.scalar_tensor_tensor(out=sc_acc[:, c, :], in0=sc_z[:, c, tap:tap + S], scalar=col("sc_dw_w", tap * MT + c),
                                                     in1=sc_acc[:, c, :], op0=ALU.mult, op1=ALU.add))
            for c in range(2):
                t = T["sc"][4 + c]
                wait_full(dve, t)
                dve.wait_ge(ch.sem, ch.n)
                release(dve.tensor_tensor(sc_acc[:, c, :], bank[t.bank][:, :], sc_acc[:, c, :], ALU.mult), t)
            for c in range(2):
                wait_read(dve, T["sc"][4 + c])
                dve.nop().then_inc(sem("y_src"), 1)
            for c in range(2):
                t = T["conf"][2 + c]
                wait_read(dve, T["conf"][c])
                wait_full(dve, t)
                release(dve.tensor_tensor(cf_u[:, c, 30:30 + S], bank[t.bank][:, :], cf_s[:, c, :], ALU.mult), t)
            for c in range(2):
                wait_read(dve, T["conf"][2 + c])
                ch.tick(dve.tensor_scalar(cf_acc[:, c, :], cf_u[:, c, 0:S], col("conf_dw_w", c), col("conf_dw_b", c), ALU.mult, ALU.add))
            for k in range(2):
                y_lo_of(sc_acc[:, k, :], k, k + 1)

            def conf_taps(a, b):
                for tap in range(a, b):
                    for c in range(2):
                        dve.wait_ge(ch.sem, ch.n - 1)
                        ins = dve.scalar_tensor_tensor(out=cf_acc[:, c, :], in0=cf_u[:, c, tap:tap + S], scalar=col("conf_dw_w", tap * MT + c),
                                                       in1=cf_acc[:, c, :], op0=ALU.mult, op1=ALU.add)
                        ch.tick(ins)

            r = lambda k: ml_rows[0:MH, k, :]
            nm = ml_nm[0:MH, :]
            wait_read(dve, T["ifa"][0])
            ch.tick(dve.memset(r(5), 1.0))
            ch.link(dve.tensor_scalar(r(3), r(1), 0.0, None, ALU.min))
            ch.link(dve.tensor_tensor(r(3), r(3), r(2), ALU.subtract))
            ch.link(dve.tensor_tensor_scan(r(1), r(5), r(3), 0.0, ALU.mult, ALU.add))
            ch.link(dve.tensor_tensor(r(4), r(0), r(1), ALU.subtract))
            ch.link(dve.tensor_tensor_scan(nm, r(4), r(4), 0.0, ALU.max, ALU.max))
            ch.link(dve.tensor_tensor(r(5), r(1), nm, ALU.add))
            ch.link(dve.tensor_scalar(nm, nm, -1.0, None, ALU.mult))
            dve.nop().then_inc(sem("ml_gates"), 1)
            cuts = [1, 9, 17, 25, 31]
            for k in range(4):
                if k == 2:
                    ch.tick(dve.memset(ml_v.rearrange("p j (h e) -> p (j h) e", h=MH)[:, :, HD:HD + 1], 1.0))
                    for c in range(2):
                        t = T["ml"][4 + c]
                        wait_full(dve, t)
                        for m in range(2):
                            ins = dve.tensor_copy(ml_v[:, 2 * c + m, :].rearrange("p (h e) -> p h e", h=MH)[:, :, 0:HD],
                                                  bank[t.bank][:, m * 256:(m + 1) * 256].rearrange("p (h e) -> p h e", h=MH))
                        release(ins, t)
                conf_taps(cuts[k], cuts[k + 1])
            dve.wait_ge(ch.sem, ch.n)
            for c in range(2):
                dve.nop().then_inc(sem("cf_conv"), 1)
            t = T["cf_mu"][0]
            wait_full(dve, t)
            for c in range(2):
                ins = dve.tensor_tensor(cf_acc[:, c, :], cf_acc[:, c, :], bank[t.bank][:, :], ALU.subtract)
                ins.then_inc(sem("cf_centered"), 1)
            dve.wait_ge(sem("cf_centered"), 2)
            dve.nop().then_inc(read[t.bank], 1)
            wait_read(dve, T["cf_var"][0])
            for c in range(2):
                dve.scalar_tensor_tensor(out=cf_acc[:, c, :], in0=cf_acc[:, c, :], scalar=col("conf_ln_g", c), in1=rstd[:, :],
                                         op0=ALU.mult, op1=ALU.mult).then_inc(sem("cf_scaled"), 1)
            for k in range(2):
                y_lo_of(cf_acc[:, k, :], 2 + k, 3 + k)
            t = T["ml_cols"][0]
            wait_full(dve, t)
            ins = dve.tensor_copy(small[:, 48:80], bank[t.bank][:, 0:32])
            ins.then_inc(sem("ml_cols"), 1)
            dve.wait_ge(sem("ml_cols"), 1)
            dve.nop().then_inc(read[t.bank], 1)

            def ml_weights(h, j):
                n, N = h * TT + j, S - j * P
                wait_read(dve, T["ml_d"][n])
                wait_full(dve, T["ml_qk"][n])
                release(dve.tensor_tensor(ml_p[:, h % 2, j, j * P:S], bank[T["ml_qk"][n].bank][:, 0:N], tbuf[:, n % 2, 0:N], ALU.mult),
                        T["ml_qk"][n])

            def ml_divide(h):
                t = T["ml_n"][h]
                wait_full(dve, t)
                v = bank[t.bank][:, 0:TT * (HD + 1)].rearrange("p (i e) -> p i e", i=TT)
                ch.link(dve.tensor_scalar(ml_d, v[:, :, HD], -1.0, None, ALU.mult))
                ch.link(dve.tensor_tensor(ml_d, v[:, :, HD], ml_d, ALU.max))
                ch.link(dve.tensor_tensor(ml_d, ml_d, ml_mt[:, h:16:MH], ALU.max))
                ch.link(dve.reciprocal(ml_d, ml_d))
                release(dve.tensor_tensor(ml_h[:, :, h * HD:(h + 1) * HD], v[:, :, 0:HD], ml_d.unsqueeze(2).broadcast_to([P, TT, HD]),
                                          ALU.mult), t)

            dve.wait_ge(sem("ml_floor"), 1)
            for h in range(MH):
                for j in range(TT):
                    ml_weights(h, j)
                ml_divide(h)
            for h in range(MH):
                wait_read(dve, T["ml_n"][h])
            hv = ml_h[:, :, :].rearrange("p i (h e) -> p (i h) e", h=MH)
            h2 = ml_p[:, 0, 0:2, :].rearrange("p a (b e) -> p (a b) e", e=HD)
            ch.link(dve.tensor_tensor(h2, hv, hv, ALU.mult))
            dve.tensor_reduce(ml_ms, h2, AX.X, ALU.add).then_inc(sem("ml_ms"), 1)
            dve.wait_ge(sem("ml_rs"), 1)
            dve.tensor_tensor(hv, hv, ml_ms.unsqueeze(2).broadcast_to([P, TT * MH, HD]), ALU.mult).then_inc(sem("ml_normed"), 1)
            for c in range(MT):
                t = T["ml_hT"][c]
                wait_full(dve, t)
                wait_read(dve, T["ml"][6 + c])
                release(dve.scalar_tensor_tensor(out=ml_q[:, c, :], in0=bank[t.bank][:, :], scalar=col("ml_norm_g", c), in1=ml_o[:, c, :],
                                                 op0=ALU.mult, op1=ALU.mult), t)
                wait_read(dve, t)
                dve.nop().then_inc(sem("y_src"), 1)

            gn = [0]

            def product(c):
                return rstd[:, :] if c % 3 == 2 else tbuf[:, c % 3, :]

            def add(t, c):
                wait_read(dve, t)
                gn[0] += 1
                dve.tensor_tensor(merged[:, c, :], merged[:, c, :], product(c), ALU.add).then_inc(sem("added"), 1)

            def gated(name, bias=None, first=False):
                for c in range(KT):
                    t = T[name][c]
                    wait_full(dve, t)
                    wait_read(dve, T[GATE_OF[name]][c])
                    dst = merged[:, c, :] if first else product(c)
                    if not first and gn[0] >= 2:
                        dve.wait_ge(sem("added"), gn[0] - 1)
                    ins = dve.scalar_tensor_tensor(out=dst, in0=bank[t.bank][:, :], scalar=0.0 if bias is None else col(bias, c),
                                                   in1=gates[:, c, :], op0=ALU.add, op1=ALU.mult)
                    release(ins, t)
                    if not first and c:
                        add(T[name][c - 1], c - 1)
                if not first:
                    add(T[name][KT - 1], KT - 1)

            gated("y3", first=True)
            for k in range(2):
                y_lo_of(ml_q[:, k, :], k, 5 + k)
            u = U["gla"]
            for k in range(4):
                if k == 2:
                    for c in range(2):
                        t = T["gla"][4 + c]
                        wait_full(dve, t)
                        release(dve.tensor_copy(gl_v[:, 2 * c:2 * c + 2, :], bank[t.bank][:, :].rearrange("p (a b) -> p a b", a=2)), t)
            for c in range(MT):
                t = T["gl_z"][c]
                dve.wait_ge(sem("gl_ln"), c + 1)
                release(dve.tensor_scalar(gl_bs[:, c, :], bank[t.bank][:, :], col("gla_a_bias", c), 0.0, ALU.add, ALU.min), t)
                wait_read(dve, t)
                ch.link(dve.tensor_tensor(gl_bs[:, c, :], gl_bs[:, c, :], gl_e[:, c, :], ALU.subtract))
                ch.link(dve.tensor_tensor_scan(gl_bs[:, c, :], const("chunk_reset"), gl_bs[:, c, :], 0.0, ALU.mult, ALU.add))
                b = gl_bs[:, c, :].rearrange("p (n k) -> p n k", k=GC)
                dve.tensor_tensor(gl_kd[:, c, :].rearrange("p (n k) -> p n k", k=GC), b[:, :, GC - 1:GC].broadcast_to([P, NC, GC]), b,
                                  ALU.subtract).then_inc(sem("gl_bs"), 1)
            for c in range(2):
                for k in (0, 2):
                    wait_read(dve, T["gla"][k + c])
            for c in range(MT):
                dve.wait_ge(sem("gl_exp"), c + 1)
                ch.tick(dve.tensor_tensor(gl_q[:, c, :], gl_q[:, c, :], gl_e[:, 0, :], ALU.mult))
                dve.tensor_tensor(gl_kd[:, c, :], gl_kd[:, c, :], gl_k[:, c, :], ALU.mult).then_inc(sem("gl_kd"), 1)
                ins = dve.tensor_tensor(gl_k[:, c, :], gl_k[:, c, :], gl_e[:, 1, :], ALU.mult)
                ins.then_inc(sem("gl_ks"), 1)
                dve.wait_ge(sem("gl_ks"), c + 1)
                dve.nop().then_inc(sem("gl_scaled"), 1)
            for c in range(MT):
                t = T["gl_kdT"][c]
                wait_full(dve, t)
                release(dve.tensor_copy(gl_kdt[:, c, :], bank[t.bank][:, :]), t)
            dve.memset(gl_at[:, :, :], 0.0).then_inc(sem("gl_zero"), 1)
            dve.memset(gl_a[:, 0:1], 0.0)
            dve.memset(gl_a[:, NC:NC + 1], 0.0).then_inc(sem("gl_zero"), 1)
            dve.wait_ge(sem("gl_zero"), 2)
            for c in range(MT):
                if c:
                    wait_full(dve, T["gl_o"][c - 1])
                for j in range(TT):
                    t = T["gl_u"][c * TT + j]
                    wait_full(dve, t)
                    release(dve.tensor_copy(gl_u[:, :, j * CPT:(j + 1) * CPT].rearrange("p e k -> p k e"),
                                            bank[t.bank][:, :].rearrange("p (k e) -> p k e", k=CPT)), t)
                ch.link(dve.tensor_copy(gl_ab[:, :, :], gl_a[:, c * NC:(c + 1) * NC].unsqueeze(1).broadcast_to([P, HD, NC])))
                for j in range(TT):
                    wait_read(dve, T["gl_u"][c * TT + j])
                flat = lambda a: a.rearrange("p e k -> p (e k)")
                dve.tensor_tensor_scan(flat(gl_u[:, :, :]), flat(gl_ab[:, :, :]), flat(gl_u[:, :, :]), 0.0, ALU.mult, ALU.add)\
                   .then_inc(sem("gl_state"), 1)
                for hh in range(2):
                    n = 2 * c + hh
                    t = T["gl_a"][n]
                    wait_full(dve, t)
                    if n:
                        dve.wait_ge(sem("gl_at_used"), n)
                    release(dve.copy_predicated(gl_at[:, :, :], const("block_causal").bitcast(U32).unsqueeze(1).broadcast_to([P, TT, P]),
                                                bank[t.bank][:, :].rearrange("p (a b) -> p a b", a=TT)), t)
                wait_read(dve, T["gl_ms"][c])
                ch.link(dve.scalar_tensor_tensor(out=gl_o, in0=gl_o, scalar=col("gla_norm_g", c), in1=rstd[:, :], op0=ALU.mult, op1=ALU.mult))
                wait_read(dve, T["gla"][6 + c])
                dve.tensor_tensor(gl_k[:, c, :], gl_o, gl_r[:, c, :], ALU.mult).then_inc(sem("y_src"), 1)
            gated("y2", "conf_out_b")
            for k in range(2):
                y_lo_of(gl_k[:, k, :], 2 + k, 7 + k)
            for n in range(8, 14):
                ada_sum(n, ada_place(n))
            gated("y0")
            for n in range(14, 22):
                ada_sum(n, ada_place(n))
            gated("y1")

            def merged_lo():
                for c in range(KT):
                    hn[0] += 1
                    dve.wait_ge(sem("h_hi"), hn[0])
                    dve.tensor_tensor(h_lo[:, c, :], merged[:, c, :], h_hi[:, c, :].bitcast(FP32), ALU.subtract).then_inc(sem("h_ready"), 1)

            merged_lo()
            for n in (22, 23):
                ada_sum(n, ada_place(n))
            ada_out(T["ada1"][0], 2 * KT, 4 * KT)
            wait_read(dve, T["ada1"][0])
            ch.tick(dve.tensor_tensor(gain[:, 1, :], mod[:, 2 * KT:3 * KT], col("tm_post_g", 0, KT), ALU.mult))
            ch.tick(dve.scalar_tensor_tensor(out=gain[:, 2, :], in0=mod[:, 4 * KT:5 * KT], scalar=1.0, in1=col("cm_pre_g", 0, KT),
                                             op0=ALU.add, op1=ALU.mult))
            ch.tick(dve.tensor_tensor(gain[:, 3, :], mod[:, 5 * KT:6 * KT], col("cm_post_g", 0, KT), ALU.mult))

            dve.wait_ge(ch.sem, ch.n)

            def residual(ss, k, order):
                wait_read(dve, T[ss][0])
                for n in range(KT + 1):
                    if n < KT:
                        c = order[n]
                        ch.tick(dve.scalar_tensor_tensor(out=ybuf[:, c, :], in0=ybuf[:, c, :], scalar=gain[:, k, c:c + 1], in1=rstd[:, :],
                                                         op0=ALU.mult, op1=ALU.mult))
                    if n:
                        c = order[n - 1]
                        dve.wait_ge(ch.sem, ch.n - (1 if n < KT else 0))
                        dve.tensor_tensor(x[:, c, :], x[:, c, :], ybuf[:, c, :], ALU.add).then_inc(sem("x_ready"), 1)

            residual("ss1", 1, ORDER[1])
            norm_lo("ss2", gain[:, 2, :], 3 * KT)

            def ffn(n, taps):
                up, down = U["up" + n], U["down" + n]
                with dve.Fori(0, FT // 2) as i:
                    for k in range(2):
                        lo(up + k + 1, i * 2)
                        for tap in (1, 0):
                            for part in range(2):
                                t, c = T["up" + n][2 * k + part], cbuf[:, k, part, :]
                                if tap:
                                    dve.wait_ge(sem("center" + n), i * 4 + (2 * k + part + 1))
                                else:
                                    dve.wait_ge(sem("tap" + n), i * 4 + (2 * k + part + 1))
                                w = par[:, bass.ds(i * 2 + (COLUMN[taps[tap]] + part * FT + k), 1)]
                                back = 2 - tap
                                ins = dve.scalar_tensor_tensor(out=c[:, back:S], in0=bank[t.bank][:, 0:S - back], scalar=w,
                                                               in1=c[:, back:S], op0=ALU.mult, op1=ALU.add)
                                ins.then_inc(sem("tap" + n), 1) if tap else release(ins, t)

                def part_lo(d, i=0):
                    dve.wait_ge(sem("down_hi" + n), d + 1 + i)
                    k = 2 * (d % 2)
                    flat = lambda a: a[:, k:k + 2, :].rearrange("p a b -> p (a b)")
                    dve.tensor_tensor(flat(y_lo), work[:, bass.ds(i * (2 * S) + d * 2 * S, 2 * S)], flat(y_hi).bitcast(FP32),
                                      ALU.subtract).then_inc(sem("down_lo" + n), 1)

                part_lo(0)
                lo(down + 1)
                part_lo(1)
                lo(down + 2)
                part_lo(2)
                with dve.Fori(0, 4) as i:
                    for d in (2, 3):
                        lo(down + d + 1, i * 2)
                        part_lo(d + 1, i * 2)
                if down + FT // 2 < N_UNITS:
                    lo(down + FT // 2)

            ffn("1", ("ffn_dw_w/0", "ffn_dw_w/1"))
            residual("ss3", 3, ORDER[2])
            norm_lo("ss4", col("norm_mix_g_2", 0, KT))

            dve.wait_ge(sem("pads"), 3)
            for g in range(POOL_G):
                wait_read(dve, T["pool"][g])
                src, dst = 0, 1
                for k in range(g + 1):
                    b = 2 ** k
                    a0 = 2 * b - 1
                    ch.link(dve.tensor_tensor(pool_t[:, dst, a0:], pool_t[:, src, a0:], pool_t[:, src, a0 - b:16 + S - b], ALU.add))
                    src, dst = dst, 3 - dst
                pc = const("pool_count")[:, g * 16:(g + 1) * 16]
                ch.link(dve.tensor_tensor(pooled[:, g, 0:16], pool_t[:, src, 16:32], pc, ALU.mult))
                ch.tick(dve.tensor_tensor(pooled[:, g, 0:16], pooled[:, g, 0:16], pool_t[:, 0, 16:32], ALU.subtract))
                dve.scalar_tensor_tensor(out=pooled[:, g, 16:S], in0=pool_t[:, src, 32:16 + S], scalar=0.5 ** (g + 1),
                                         in1=pool_t[:, 0, 32:16 + S], op0=ALU.mult, op1=ALU.subtract).then_inc(sem("pool_done"), 1)
                dve.wait_ge(sem("pool_done"), g + 1)
                dve.wait_ge(ch.sem, ch.n)
                dve.nop().then_inc(sem("pooled"), 1)
            for g in range(POOL_G):
                t = T["pl"][g]
                wait_full(dve, t)
                dve.wait_ge(sem("y_hi"), 8 + g + 1)
                ins = dve.scalar_tensor_tensor(out=y_lo[:, g, :], in0=bank[t.bank][:, :], scalar=col("pool_scale_2", g),
                                               in1=y_hi[:, g, :].bitcast(FP32), op0=ALU.mult, op1=ALU.subtract)
                ins.then_inc(sem("y_lo"), 1)
                dve.wait_ge(sem("y_lo"), 8 + g + 1)
                dve.nop().then_inc(read[t.bank], 1)
            rn = [0]

            def rope(dst):
                n = rn[0]
                t = T["rope"][n]
                wait_full(dve, t)
                release(dve.tensor_tensor(dst, bank[t.bank][:, :], const("rope_sin"), ALU.mult), t)
                wait_read(dve, t)
                dve.wait_ge(sem("rope_kept"), n + 1)
                dve.tensor_tensor(dst, dst, tbuf[:, n % 2, :], ALU.add).then_inc(sem("roped"), 1)
                rn[0] += 1

            dve.wait_ge(sem("rope_in"), 16)
            for name, dst in (("q", at_q), ("k", at_k)):
                for c in range(4):
                    rope(dst[:, c, :])
            for k in range(2):
                for c in range(2):
                    t = T["v"][2 * k + c]
                    wait_full(dve, t)
                    release(dve.tensor_copy(at_v[:, 2 * c:2 * c + 2, k * 256:(k + 1) * 256], bank[t.bank][:, :].rearrange("p (a b) -> p a b", a=2)), t)
            for c in range(4):
                rope(iq[:, c, :])
            rope(ik)
            t = T["iwT"][0]
            wait_full(dve, t)
            release(dve.tensor_copy(iw_t, bank[t.bank][:, 0:TT * NH2]), t)
            wait_read(dve, t)

            def indexer(qt):
                N = (qt + 1) * P
                acc = sq[:, qt % 2, 0:N]
                for h in range(NH2):
                    n = (qt - 1) * NH2 + h
                    wait_read(dve, T["idx"][n])
                    w = iw_t[:, qt * NH2 + h:qt * NH2 + h + 1]
                    if h == 0:
                        ins = dve.tensor_scalar(acc, tbuf[:, n % 2, 0:N], w, None, ALU.mult)
                    else:
                        ins = dve.scalar_tensor_tensor(out=acc, in0=tbuf[:, n % 2, 0:N], scalar=w, in1=acc, op0=ALU.mult, op1=ALU.add)
                    ins.then_inc(sem("idx_used"), 1)
                    dve.wait_ge(sem("idx_used"), n + 1)
                ch.link(dve.tensor_tensor(acc[:, qt * P:N], acc[:, qt * P:N], const("causal_qk"), ALU.add))

            best = small[:, 240:248]

            def top_rounds(qt, a, b):
                N = (qt + 1) * P
                acc = sq[:, qt % 2, 0:N]
                for _ in range(a, b):
                    ch.link(dve.max(best, acc))
                    ch.link(dve.match_replace(out=acc, in_to_replace=best, in_values=acc, imm_value=TAKEN))
                if b == TOPK // 8:
                    ch.link(dve.tensor_scalar(masks[qt], acc, 0.5 * TAKEN, NEG, ALU.is_gt, ALU.mult))

            ch.link(dve.tensor_copy(masks[0], const("causal_qk")))
            indexer(1)
            for c in range(2):
                top_rounds(1, 8 * c, 8 * c + 8)
            indexer(2)
            for c in range(2):
                top_rounds(2, 8 * c, 8 * c + 8)
            indexer(3)
            gated("yp", first=True)
            for c in range(4):
                top_rounds(3, 4 * c, 4 * c + 4)

            def attention(qt):
                N = (qt + 1) * P
                for h in range(NH2):
                    n = qt * NH2 + h
                    t, m = T["s"][n], at_m[:, n % 16:n % 16 + 1]
                    wait_full(dve, t)
                    if n >= 2:
                        wait_full(dve, T["pt"][n - 2])
                    release(dve.tensor_tensor_reduce(at_s[:, n % 2, 0:N], bank[t.bank][:, 0:N], masks[qt], 1.0, 4.0 * NEG, ALU.add, ALU.max, m), t)
                    wait_read(dve, t)
                    dve.tensor_scalar(m, m, -1.0, None, ALU.mult).then_inc(sem("at_max"), 1)
                t = T["o"][qt]
                dve.wait_ge(sem("at_pv"), (qt + 1) * NH2)
                s = at_sum[:, (qt % 2) * NH2:(qt % 2) * NH2 + NH2]
                ch.link(dve.reciprocal(s, s))
                if qt:
                    wait_full(dve, T["oT"][qt - 1])
                ins = dve.tensor_tensor(tbuf[:, 0, :].rearrange("p (h e) -> p h e", h=NH2), bank[t.bank][:, :].rearrange("p (h e) -> p h e", h=NH2),
                                        s.unsqueeze(2).broadcast_to([P, NH2, HD]), ALU.mult)
                release(ins, t)
                wait_read(dve, t)
                dve.nop().then_inc(sem("o_scaled"), 1)
                t = T["oT"][qt]
                dve.wait_ge(sem("y_hi"), 8 + POOL_G + qt + 1)
                tok = slice(qt * P, (qt + 1) * P)
                dve.tensor_tensor(y_lo[:, :, tok], bank[t.bank][:, :].rearrange("p (a b) -> p a b", a=4), y_hi[:, :, tok].bitcast(FP32),
                                  ALU.subtract).then_inc(sem("y_lo"), 1)
                dve.wait_ge(sem("y_lo"), 8 + POOL_G + qt + 1)
                dve.nop().then_inc(read[t.bank], 1)

            for qt in range(TT):
                attention(qt)
            gated("ya")
            merged_lo()
            for c in range(4):
                for k in range(2):
                    t = T["wo2"][2 * c + k]
                    wait_full(dve, t)
                    dve.tensor_tensor(x[:, 2 * c + k, :], bank[t.bank][:, :], x[:, 2 * c + k, :], ALU.add).then_inc(sem("x_ready"), 1)
                    dve.wait_ge(sem("x_ready"), 3 * KT + 2 * c + k + 1)
                    dve.nop().then_inc(read[t.bank], 1)
            norm_lo("ss5", col("norm_ffn_g_2", 0, KT))
            ffn("2", ("conv_w_2/0", "conv_w_2/1"))
            for c in range(KT):
                t = T["down2"][c]
                wait_full(dve, t)
                dve.tensor_tensor(x[:, c, :], bank[t.bank][:, :], x[:, c, :], ALU.add).then_inc(sem("x_ready"), 1)
                dve.wait_ge(sem("x_ready"), 4 * KT + c + 1)
                dve.nop().then_inc(read[t.bank], 1)
            dve.wait_ge(sem("gain_in"), 16)
            for tt in range(TT):
                dve.wait_ge(sem("fin_sq"), 2 * tt + 2)
                dve.tensor_tensor(fin_s[:, 8 + tt:9 + tt], fin_s[:, 2 * tt:2 * tt + 1], fin_s[:, 2 * tt + 1:2 * tt + 2], ALU.add)\
                   .then_inc(sem("fin_sum"), 1)
                dve.wait_ge(sem("fin_rstd"), tt + 1)
                for k in range(2):
                    t = T["fin"][2 * tt + k]
                    release(dve.scalar_tensor_tensor(out=o_tok[:, tt, k * S:(k + 1) * S], in0=bank[t.bank][:, :], scalar=fin_s[:, 8 + tt:9 + tt],
                                                     in1=gain_final[:, k * S:(k + 1) * S], op0=ALU.mult, op1=ALU.mult), t)
                for k in range(2):
                    wait_read(dve, T["fin"][2 * tt + k])
                dve.nop().then_inc(sem("out_ready"), 1)


_INS = ["x", "c", "ada_w", "ada_b", "tm_pre_g", "tm_post_g", "cm_pre_g", "cm_post_g", "w_in", "ml_i_bias", "ml_f_bias", "ml_norm_g",
        "w_ml_out", "gla_w_a2", "gla_a_bias", "gla_norm_g", "w_gla_out", "conf_dw_w", "conf_dw_b", "conf_ln_g", "conf_ln_b",
        "w_conf_out", "conf_out_b", "sc_dw_w", "w_sc_out", "merge_gate_b", "w_o", "ffn_w_up", "ffn_dw_w", "ffn_w_down",
        "norm_mix_g_2", "w_in_2", "pool_w_2", "pool_scale_2", "w_pool_proj_2", "w_attn_proj_2", "w_out_2", "norm_ffn_g_2",
        "w_up_2", "conv_w_2", "conv_b_2", "w_down_2", "norm_final_g_2"]


def kernel(**inputs):
    import concourse.bacc as bacc
    from concourse.bass_utils import run_bass_kernel_spmd

    nc = bacc.Bacc("TRN2", target_bir_lowering=False, num_devices=1)
    arrays, args = {}, {}
    for name in _INS:
        a = np.ascontiguousarray(inputs[name])
        arrays[f"in_{name}"] = a
        args[name] = nc.dram_tensor(f"in_{name}", a.shape, mybir.dt.from_np(a.dtype), kind="ExternalInput").ap()
    arrays["in_consts"] = shape_constants()
    args["consts"] = nc.dram_tensor("in_consts", (P, N_CONST + 2 * S), FP32, kind="ExternalInput").ap()
    out = nc.dram_tensor("out", (1, S, D), FP32, kind="ExternalOutput").ap()
    program(nc, args, out)
    return run_bass_kernel_spmd(nc, [arrays], core_ids=[0]).results[0]["out"]
```

```python
import numpy as np
import concourse.bass as bass
from concourse import mybir
from contextlib import ExitStack

FP32 = mybir.dt.float32
F32R = mybir.dt.float32r
U32 = mybir.dt.uint32
ALU = mybir.AluOpType
ACT = mybir.ActivationFunctionType
AX = mybir.AxisListType

P = 128
D = 1024
S = 512
KT = D // P
TT = S // P
MIX = D // 4
MT = MIX // P
HD = 64
MH = MIX // HD
GC = 16
NC = S // GC
CPT = P // GC
CONF_W = 31
FF = 2816
FT = FF // P
EPS = 1e-6
NEG = -1.0e30
TAKEN = -3.0e38
TOPK = S // 4
NH2 = 8
POOL_G = 4
UNIT = 2048
HEAD_SCALE = 0.125

C_ML, C_MLIF, C_GLA, C_GLAA = 0, 1024, 1032, 2056
C_CONF, C_SC, C_GATE = 2072, 2584, 3352
C_POOL, C_Q, C_K, C_V, C_IQ, C_IK, C_GATE2 = 0, 512, 1024, 1536, 2048, 2560, 2632
IKW = HD + NH2

VECTORS = [
    [("c", 8), ("ada_b", 48), ("tm_pre_g", 8), ("tm_post_g", 8), ("cm_pre_g", 8), ("cm_post_g", 8), ("conf_out_b", 8)],
    [("merge_gate_b", 32), ("ml_norm_g", 2), ("gla_norm_g", 2), ("gla_a_bias", 2), ("conf_dw_b", 2),
     ("conf_ln_g", 2), ("conf_ln_b", 2), ("sc_dw_w", 6), ("conf_dw_w", 62)],
    [("norm_mix_g_2", 8), ("norm_ffn_g_2", 8), ("pool_scale_2", 4), ("conv_b_2", 44), ("ffn_dw_w/0", 44)],
    [("ffn_dw_w/1", 44), ("ffn_dw_w/2", 44)],
    [("conv_w_2/0", 44), ("conv_w_2/1", 44)],
    [("conv_w_2/2", 44)],
]
COLUMN = {}
for _g, _group in enumerate(VECTORS):
    _r = 0
    for _name, _n in _group:
        COLUMN[_name] = _g * P + _r
        _r += _n

CONSTS = [("ident", P), ("ones_d", P), ("ones_head", P), ("ones_mix", P), ("causal_st", P), ("causal_qk", P),
          ("block_causal", P), ("chunk_of", CPT), ("rope_swap", P), ("pool_count", POOL_G * 16),
          ("sel", MH * P), ("chunk_reset", S)]
CONST_AT = {}
_at = 0
for _name, _n in CONSTS:
    CONST_AT[_name] = (_at, _n)
    _at += _n
N_CONST = _at
CONST_AT["rope_cos"], CONST_AT["rope_sin"] = (N_CONST - 2 * S, S), (N_CONST - S, S)


def shape_constants():
    out = np.zeros((P, N_CONST + 2 * S), np.float32)

    def put(name, a):
        at, n = CONST_AT[name]
        at += 2 * S if name in ("rope_cos", "rope_sin") else 0
        out[:a.shape[0], at:at + n] = a

    p, q = np.arange(P)[:, None], np.arange(P)[None, :]
    put("ident", np.eye(P))
    put("ones_d", np.full((P, P), 1.0 / D))
    put("ones_head", (p // HD == q // HD) / HD)
    put("ones_mix", np.full((P, P), 1.0 / MIX))
    put("sel", np.concatenate([np.repeat((np.arange(MH) == h)[:, None], P, 1) for h in range(MH)], 1))
    put("causal_st", np.where(p <= q, 0.0, NEG))
    put("causal_qk", np.where(q <= p, 0.0, NEG))
    put("block_causal", (p // GC == q // GC) & (p <= q))
    put("chunk_of", p // GC == np.arange(CPT)[None, :])
    put("chunk_reset", np.repeat((np.arange(S) % GC != 0)[None, :], P, 0))
    rot = HD // 4
    half = rot // 2
    inv = (np.float32(1.0) / np.float32(500000.0) ** (np.arange(half, dtype=np.float32) * np.float32(2.0) / np.float32(rot)))
    ang = np.arange(S, dtype=np.float32)[:, None] * inv.astype(np.float32)[None, :]
    cos, sin = np.cos(ang).T, np.sin(ang).T
    c, s, swap = np.ones((P, S)), np.zeros((P, S)), np.zeros((P, P))
    for base in (0, HD):
        c[base:base + half] = c[base + half:base + rot] = cos
        s[base:base + half], s[base + half:base + rot] = -sin, sin
        for d in range(half):
            swap[base + d + half, base + d] = swap[base + d, base + d + half] = 1.0
    put("rope_cos", c)
    put("rope_sin", s)
    put("rope_swap", swap)
    t = np.arange(16)
    put("pool_count", np.repeat(np.concatenate([1.0 / np.minimum(t + 1, 2 ** (g + 1)) for g in range(POOL_G)])[None, :], P, 0))
    return out


class Tile:

    def __init__(self, bank, n):
        self.bank, self.n, self.full = bank, n, None


class Tiles:

    def __init__(self):
        self.used = [0] * 8
        self.turn = {}
        self.order = []

    def take(self, banks, times=1):
        k = self.turn.get(banks, 0)
        self.turn[banks] = k + 1
        b = banks[k % len(banks)]
        self.used[b] += 1
        t = Tile(b, self.used[b])
        self.used[b] += times - 1
        self.order.append((t, times))
        return t

    def number(self, full):
        n = [0] * 8
        for t, times in self.order:
            if t.full is None:
                t.full = (full[t.bank], n[t.bank] + 1, 1)
                n[t.bank] += times


GEMM, AUX, HOLD = (0, 1, 2, 3), (4, 5, 6), (7,)
GATE_OF = {"y3": "gate3", "y2": "gate2", "y0": "gate0", "y1": "gate1", "yp": "gp", "ya": "ga"}
ORDER = {0: tuple(range(8)), 1: tuple(range(8)), 2: (7, 0, 1, 2, 3, 4, 5, 6), 3: tuple(range(8))}


def program(nc, A, out):
    ctx = ExitStack()
    with ctx:
        def sb(name, shape, dt=FP32):
            return ctx.enter_context(nc.sbuf_tensor(name, shape, dt))

        sems = {}

        def sem(name):
            if name not in sems:
                sems[name] = ctx.enter_context(nc.semaphore(name))
            return sems[name]

        raw = [sb(f"w_raw{i}", [P, UNIT]) for i in range(2)]
        w_hi = [sb(f"w_hi{i}", [P, UNIT], F32R) for i in range(2)]
        w_lo = [sb(f"w_lo{i}", [P, UNIT], F32R) for i in range(2)]
        x = sb("x", [P, KT, S])
        h_hi = sb("h_hi", [P, KT, S], F32R)
        h_lo = sb("h_lo", [P, KT, S], F32R)
        y_hi = sb("y_hi", [P, 4, S], F32R)
        y_lo = sb("y_lo", [P, 4, S], F32R)
        cst = sb("cst", [P, N_CONST])
        par = sb("par", [P, len(VECTORS) * P])
        mod = sb("mod", [P, 48])
        gain = sb("gain", [P, 5, KT])
        sq = sb("sq", [P, 2, S])
        rstd = sb("rstd", [P, S])
        tbuf = sb("tbuf", [P, 2, S])
        small = sb("small", [P, 256])
        bias_if = sb("bias_if", [MH, 2])
        gl_low = sb("gl_low", [GC, S + MIX])
        WORK = 17936
        work = sb("work", [P, WORK])
        bank = [ctx.enter_context(nc.psum_tensor(f"bank{b}", [P, 512], FP32)) for b in range(8)]

        def area(at, *shape):
            n = int(np.prod(shape))
            assert at + n <= WORK, (at, n)
            v = work[:, at:at + n]
            if len(shape) == 2:
                v = v.rearrange("p (a b) -> p a b", a=shape[0])
            if len(shape) == 3:
                v = v.rearrange("p (a b c) -> p a b c", a=shape[0], b=shape[1])
            return v

        def const(name):
            at, n = CONST_AT[name]
            return cst[:, at:at + n]

        def col(name, i=0, n=1):
            at = COLUMN[name]
            return par[:, at + i:at + i + n]

        ident = const("ident")

        x_tok, rows_in = area(0, TT, D), area(4096, len(VECTORS), P)
        ada_first = [area(4864 + UNIT * k, KT, 2 * P) for k in range(6)]
        gates, merged = area(0, KT, S), area(KT * S, KT, S)
        sc_z, sc_c, sc_acc = area(0, MT, 2 + S), area(1040, MT, S), area(2080, MT, S)
        cf_u, cf_s, cf_acc = area(4096, MT, 30 + S), area(5184, MT, S), area(6208, MT, S)
        R = 2 * KT * S
        ada_later = [area(R + UNIT * k, KT, 2 * P) for k in range(4)]

        def ada_place(n):
            return ada_first[n % 6] if n < 8 else ada_later[(n + 2) % 4]

        def ada_load(eng, n):
            eng.dma_start(ada_place(n), A["ada_w"][0][:, n * 2 * P:(n + 1) * 2 * P].rearrange("(k p) n -> p k n", p=P))\
               .then_inc(sem(f"ada_in{n % 8}"), 16)

        ADA_BY_PE = (2, 5)

        def summed(n):
            return n + 1 - sum(m < n for m in ADA_BY_PE)

        def vector_load(eng, g):
            r = 0
            for name, n in VECTORS[g]:
                base, _, tap = name.partition("/")
                a = A[base]
                if tap:
                    src = a[0, int(tap), :].rearrange("(t p) -> t p", p=P)
                elif len(a.shape) == 3:
                    src = a[0].rearrange("k (t p) -> (k t) p", p=P)
                else:
                    src = a[0].rearrange("(t p) -> t p", p=P)
                eng.dma_start(rows_in[r:r + n, g, :], src).then_inc(sem(f"vec_in{g}"), 16)
                r += n

        ADA_LOADED = {(0, 0): (8, 9), (0, 1): (10, 11), (0, 2): (12, 13), (0, 4): (14, 15),
                      (1, 0): (16, 17), (1, 1): (18, 19), (1, 2): (20, 21), (1, 3): (22, 23)}
        ADA_TURNED = {(0, 2): (8, 9), (0, 3): (10, 11), (0, 4): (12, 13),
                      (1, 1): (14, 15), (1, 2): (16, 17), (1, 3): (18, 19), (1, 4): (20, 21)}
        ml_q, ml_k, ml_o = area(R, MT, S), area(R + 1024, MT, S), area(R + 2048, MT, S)
        ml_v = area(R + 3072, TT, MH * (HD + 1))
        ml_p, ml_h, ml_nm = area(R + 4112, 2, TT, S), area(R + 8208, TT, MIX), area(R + 9232, S)
        ml_rows = area(R + 4112, 6, S)
        gl_q, gl_k, gl_r, gl_v = area(R, MT, S), area(R + 1024, MT, S), area(R + 2048, MT, S), area(R + 3072, TT, MIX)
        gl_bs, gl_e, gl_kd = area(R + 4096, MT, S), area(R + 5120, 2, S), area(R + 6144, MT, S)
        gl_u, gl_ab = area(R + 4096, HD, NC), area(R + 6144, HD, NC)
        gl_sq, gl_at, gl_o = area(R + 8192, S), area(R + 8704, TT, P), area(R + 9216, S)
        gl_a = small[:, 128:128 + MT * NC]
        gl_kdt = sq
        hid, cbuf, ybuf = area(0, FT, S), area(FT * S, 2, 2, S), area(FT * S + 4 * S, KT, S)
        pool_t, pooled = area(0, 3, 16 + S), area(1584, POOL_G, S)
        iq, ik = area(4096, 4, S), area(6144, S)
        at_q, at_k, at_v = area(R, 4, S), area(R + 2048, 4, S), area(R + 4096, TT, S)
        masks = [area(R + 6144 + P * (qt * (qt + 1) // 2), (qt + 1) * P) for qt in range(TT)]
        at_s, at_pt, pool_w = area(R + 7424, 2, S), area(R + 8448, 2, S), area(R + 7424, POOL_G, P)
        o_tok, gain_final = area(0, TT, D), area(FT * S + 4 * S, D)
        c_act, ml_gt, ml_mt, ml_d, ml_ms = small[:, 0:8], small[:, 48:64], small[:, 64:80], small[:, 96:100], small[:, 100:116]
        one = small[:, 249:250]
        iw_t, at_m, at_sum = small[:, 16:48], small[:, 192:208], small[:, 208:224]
        fin_s, eps = small[:, 224:236], small[:, 255:256]

        loaded = [sem("w_loaded0"), sem("w_loaded1")]
        hi_done = sem("w_hi_done")
        parted = [sem("w_parted0"), sem("w_parted1")]
        w_used = sem("w_used")
        full = [sem(f"bank_full{b}") for b in range(8)]
        read = [sem(f"bank_read{b}") for b in range(8)]

        def wait_full(eng, t, i=0):
            s, n, step = t.full
            eng.wait_ge(s, n + i * step)

        def wait_read(eng, t, i=0):
            eng.wait_ge(read[t.bank], t.n + i)

        def wait_free(pe, t, i=0):
            if t.n > 1:
                pe.wait_ge(read[t.bank], t.n - 1 + i)

        def done(ins, t):
            ins.then_inc(t.full[0], 1)

        def release(ins, t):
            ins.then_inc(read[t.bank], 1)

        class Chain:

            def __init__(self, eng, name):
                self.eng, self.sem, self.n = eng, sem(name), 0

            def tick(self, ins):
                ins.then_inc(self.sem, 1)
                self.n += 1
                return self.n

            def link(self, ins):
                self.eng.wait_ge(self.sem, self.tick(ins))

        U, unit = {}, 0
        for name, n in [("sc", 3), ("conf", 2), ("ifa", 1), ("ml", 4), ("gate3", 4), ("y3", 1), ("gla", 4),
                        ("gate2", 4), ("y2", 1), ("gate0", 4), ("y0", 1), ("gate1", 4), ("y1", 1),
                        ("wo", 4), ("up1", FT), ("down1", FT // 2),
                        ("pool", 2), ("q", 2), ("k", 2), ("v", 2), ("iq", 2), ("ikw", 1), ("gp", 4), ("yp", 2),
                        ("ga", 4), ("ya", 2), ("wo2", 4), ("up2", FT), ("down2", FT // 2)]:
            U[name] = unit
            unit += n
        N_UNITS = unit
        IFA = U["ifa"]

        def loaded_at(u):
            return 32 * (u // 2 + 1) + (16 if u >= IFA and (u - IFA) % 2 == 0 else 0)

        CF_VAR_AT = 4
        GATE3_AFTER = {1: 0, 3: 1, 5: 2, 7: 3, 9: 4, 13: 5}
        GATE2_AFTER = {0: 0, 1: 1, 2: 2, 3: 3, 5: 5, 6: 6}
        HEADS = TT * NH2

        def out_step(n):
            qt = (n - NH2 - 3) // NH2
            return qt if n >= NH2 + 3 and (n - NH2 - 3) % NH2 == 0 else None

        def ga_step(n):
            return n // 2 if n < 16 and n % 2 else None

        tiles, T = Tiles(), {}

        def take(name, banks, n=1, times=1):
            T.setdefault(name, []).extend(tiles.take(banks, times) for _ in range(n))

        def take_all(name):
            T[name] = [tiles.take((b,)) for b in range(8)]

        take("vec", AUX)
        take("xT", AUX, KT)
        take("ss0", HOLD)
        take("vec", AUX, len(VECTORS) - 1)
        take("ada0", AUX)
        for name, n in (("sc", 6), ("conf", 4), ("ifa", 1), ("ml", 8)):
            take(name, GEMM, n)
        take("ml_cols", AUX)
        take("cf_mu", AUX)
        for h in range(MH):
            for j in range(TT):
                if h * TT + j == CF_VAR_AT:
                    take("cf_var", AUX + HOLD)
                take("ml_d", AUX + HOLD)
                take("ml_qk", AUX + HOLD)
                if h and j == 1:
                    take("ml_n", AUX + HOLD)
        take("ml_n", AUX + HOLD)
        take("ml_hT", AUX, MT)
        take("gate3", GEMM, 8)
        take("y3", GEMM, 8)
        take("gla", GEMM, 8)
        take("gl_z", AUX, MT)
        take("gl_kdT", AUX, MT)
        take("gl_u", AUX, TT)
        take("gl_a", AUX, 2)
        take("gl_u", AUX)
        take("gl_ms", AUX)
        take("gl_u", AUX, TT - 1)
        take("gl_a", AUX, 2)
        take("gl_ms", AUX)
        take("gl_o", HOLD, MT)
        take("gate2", GEMM, 8)
        take("y2", GEMM, 8)
        for b in (0, 1):
            take(f"gate{b}", GEMM, 8)
            take(f"y{b}", GEMM, 8)
            if b == 0:
                take("ada1", AUX)
        take("wo", GEMM, 8)
        take("ss1", HOLD)
        take("ss2", HOLD)
        take("up1", GEMM, 4, FT // 2)
        take_all("down1")
        take("ss3", HOLD)
        take("ss4", HOLD)
        for name, n in (("pool", 4), ("q", 4), ("k", 4), ("v", 4), ("iq", 4), ("ikw", 1)):
            take(name, GEMM, n)
        take("pl", AUX, POOL_G)
        take("rope", AUX, 13)
        take("iwT", AUX)
        take("idx", AUX, 3 * NH2)
        for name in ("gp", "yp"):
            take(name, GEMM, 8)
        take("ga", GEMM[:3], 8)
        take("o", HOLD + GEMM[3:], TT)
        for n in range(HEADS + 4):
            if n < HEADS:
                take("s", AUX)
            if 1 <= n <= HEADS:
                take("pt", AUX)
            if out_step(n) is not None:
                take("oT", AUX)
        take("ya", GEMM, 8)
        take("wo2", GEMM, 8)
        take("ss5", HOLD)
        take("up2", GEMM, 4, FT // 2)
        take_all("down2")
        take("fin", tuple(range(8)), 2 * TT)
        for name, per, step in [(n, 2, 1) for n in ("sc", "conf", "ml", "gla", "gate0", "gate1", "gate2", "gate3", "wo", "pool", "q", "k",
                                                    "v", "iq", "gp", "ga", "wo2")] + \
                [("up1", 2, 2), ("up2", 2, 2), ("ifa", 1, 1), ("ikw", 1, 1), ("yp", 4, 1), ("ya", 4, 1)] + \
                [(f"y{b}", 8, 1) for b in range(4)]:
            for n in range(per - 1, len(T[name]), per):
                T[name][n].full = (w_used, U[name] + (n + 1) // per, step)
        for name in ("down1", "down2"):
            T[name][7].full = (w_used, U[name] + FT // 2, 0)
        for n in range(6):
            T[f"ss{n}"][0].full = (sem("sq_used"), KT * (n + 1), 0)
        for qt in range(TT):
            T["o"][qt].full = (sem("at_pv"), (qt + 1) * NH2, 0)
        T["ada0"][0].full, T["ada1"][0].full = (sem("ada_turned"), 8, 0), (sem("ada_turned"), 24, 0)
        tiles.number(full)
        READ_FIRST = (7, 0, 1, 2, 3, 4, 5, 6)

        block = ctx.enter_context(nc.Block())

        @block.sync
        def _(sp):
            def before(u, i=0):
                if u >= 2:
                    sp.wait_ge(parted[u % 2], u // 2 + i)

            def put(u, dst, src):
                sp.dma_start(dst, src).then_inc(loaded[u % 2], 16)

            def slot(u, kt):
                return raw[u % 2][:, :].rearrange("p (k n) -> p k n", k=kt)

            def cols(u, w, kt, c0, n, i=0):
                before(u, i)
                h = kt // 2
                for a in (0, h):
                    put(u, slot(u, kt)[:, a:a + h, 0:n],
                        w[a * P:(a + h) * P, c0 if isinstance(c0, slice) else bass.ds(c0, n)].rearrange("(k p) n -> p k n", p=P))

            def column_units(name, w, c0, n=4, kt=KT):
                for c in range(n):
                    cols(U[name] + c, w, kt, c0 + c * (UNIT // kt), UNIT // kt)

            def row_unit(u, w, r0, i=0):
                before(u, i)
                for q in range(2):
                    put(u, raw[u % 2][:, q * D:(q + 1) * D], w[bass.ds(r0 + q * P, P), :])

            def ffn_units(n, w_up, w_down):
                with sp.Fori(0, FT // 2) as i:
                    for k in range(2):
                        u = U["up" + n] + k
                        before(u, i)
                        for part in range(2):
                            put(u, slot(u, KT)[:, :, part * P:part * P + P],
                                w_up[:, bass.ds(i * (2 * P) + (part * FF + k * P), P)].rearrange("(k p) n -> p k n", p=P))
                row_unit(U["down" + n], w_down, 0)
                with sp.Fori(0, FT // 4) as i:
                    for k in (1, 2):
                        row_unit(U["down" + n] + k, w_down, i * (4 * P) + k * 2 * P, i)

            w, w2 = A["w_in"][0], A["w_in_2"][0]

            for tt in range(TT):
                sp.dma_start(x_tok[:, tt, :], A["x"][0, tt * P:(tt + 1) * P, :]).then_inc(sem("x_in"), 16)
            for n in range(8):
                if n == 6:
                    for g in range(1, len(VECTORS)):
                        vector_load(sp, g)
                if n >= 6:
                    sp.wait_ge(sem("ada_turned"), n - 5)
                ada_load(sp, n)
            u = U["sc"]
            for c0 in (C_SC + MIX, C_SC + 2 * MIX, C_SC, C_CONF + MIX, C_CONF):
                cols(u, w, KT, c0, MIX)
                u += 1
            before(IFA)
            for c0, n, at in ((C_MLIF, MH, 0), (C_MLIF + MH, MH, 32), (C_GLAA, GC, 64)):
                put(IFA, slot(IFA, KT)[:, :, at:at + n], w[:, c0:c0 + n].rearrange("(k p) n -> p k n", p=P))
            column_units("ml", w, C_ML)
            column_units("gate3", w, C_GATE + 3 * D)
            row_unit(U["y3"], A["w_sc_out"][0], 0)
            column_units("gla", w, C_GLA)
            column_units("gate2", w, C_GATE + 2 * D)
            row_unit(U["y2"], A["w_conf_out"][0], 0)
            column_units("gate0", w, C_GATE)
            row_unit(U["y0"], A["w_ml_out"][0], 0)
            column_units("gate1", w, C_GATE + D)
            row_unit(U["y1"], A["w_gla_out"][0], 0)
            column_units("wo", A["w_o"][0], 0)
            ffn_units("1", A["ffn_w_up"][0], A["ffn_w_down"][0])
            for name, c0 in (("pool", C_POOL), ("q", C_Q), ("k", C_K), ("v", C_V), ("iq", C_IQ)):
                column_units(name, w2, c0, 2)
            cols(U["ikw"], w2, KT, C_IK, IKW)
            column_units("gp", w2, C_GATE2)
            column_units("yp", A["w_pool_proj_2"][0], 0, 2, 4)
            column_units("ga", w2, C_GATE2 + D)
            column_units("ya", A["w_attn_proj_2"][0], 0, 2, 4)
            column_units("wo2", A["w_out_2"][0], 0)
            ffn_units("2", A["w_up_2"][0], A["w_down_2"][0])
            for tt in range(TT):
                sp.wait_ge(sem("out_ready"), tt + 1)
                sp.dma_start(out[0, tt * P:(tt + 1) * P, :], o_tok[:, tt, :]).then_inc(sem("stored"), 16)
            sp.wait_ge(sem("stored"), 16 * TT)

        @block.gpsimd
        def _(pool):
            pool.dma_start(cst[:, :], A["consts"][:, 0:N_CONST]).then_inc(sem("consts_in"), 16)
            pool.dma_start(bias_if[:, 0:1], A["ml_i_bias"].rearrange("a h -> h a")).then_inc(sem("bias_in"), 16)
            pool.dma_start(bias_if[:, 1:2], A["ml_f_bias"].rearrange("a h -> h a")).then_inc(sem("bias_in"), 16)
            pool.dma_start(gl_low[:, S:S + MIX], A["gla_w_a2"][0]).then_inc(sem("bias_in"), 16)
            pool.memset(eps, EPS).then_inc(sem("eps_set"), 1)
            pool.memset(one, 1.0).then_inc(sem("eps_set"), 1)
            wait_full(pool, T["xT"][KT - 1])
            pool.memset(sc_z[:, :, 0:2], 0.0).then_inc(sem("pads"), 1)
            wait_full(pool, T["ada0"][0])
            pool.memset(cf_u[:, :, 0:30], 0.0).then_inc(sem("pads"), 1)

            def lo(u):
                pool.wait_ge(hi_done, u + 1)
                pool.tensor_tensor(w_lo[u % 2][:, :], raw[u % 2][:, :], w_hi[u % 2][:, :].bitcast(FP32), ALU.subtract)\
                    .then_inc(parted[u % 2], 1)

            for u in range(U["gate2"] + 1):
                lo(u)

            for k in range(2):
                wait_read(pool, T["gla"][4 + k])
            wait_read(pool, T["ml_qk"][MH * TT - 1])
            wait_read(pool, T["ml_qk"][MH * TT - 2])
            for n in range(MT * TT):
                t, j = divmod(n, TT)
                if n:
                    wait_full(pool, T["gl_u"][n - 1])
                for hh in range(2):
                    h = 2 * t + hh
                    pool.tensor_tensor(tbuf[:, hh, :].rearrange("p (c d) -> p c d", c=CPT),
                                       gl_v[:, j, h * HD:(h + 1) * HD].unsqueeze(1).broadcast_to([P, CPT, HD]),
                                       const("chunk_of").unsqueeze(2).broadcast_to([P, CPT, HD]), ALU.mult)\
                        .then_inc(sem("gl_placed"), 1)
            for u in range(U["y2"], U["up1"] + 1):
                lo(u)

            def hidden(n):
                pool.nop().then_inc(sem("hid" + n), 1)
                with pool.Fori(0, FT // 2) as i:
                    for k in range(2):
                        pool.wait_ge(sem("silu" + n), i * 2 + k + 1)
                        wait_read(pool, T["up" + n][2 * k + 1], i)
                        pool.tensor_tensor(work[:, bass.ds(i * (2 * S) + k * S, S)], cbuf[:, k, 0, :], cbuf[:, k, 1, :],
                                           ALU.mult).then_inc(sem("hid" + n), 1)

            hidden("1")
            pool.wait_ge(sem("x_ready"), 3 * KT)
            pool.dma_start(pool_w[:, :, :], A["pool_w_2"][0].rearrange("g c d -> c g d")).then_inc(sem("pool_w_in"), 16)
            pool.dma_start(cst[:, N_CONST - 2 * S:N_CONST], A["consts"][:, N_CONST:]).then_inc(sem("rope_in"), 16)
            pool.memset(pool_t[:, 0, 0:16], 0.0).then_inc(sem("pads"), 1)
            pool.wait_ge(sem("rope_in"), 16)
            for u in range(U["pool"] + 1, U["q"] + 1):
                lo(u)
            for n in range(13):
                if n < 8 and n % 2 == 0:
                    lo(U["q"] + n // 2 + 1)
                if n == 8:
                    lo(U["v"] + 1)
                    lo(U["v"] + 2)
                if n >= 8 and n % 2 == 0:
                    lo(U["iq"] + (n - 8) // 2 + 1)
                wait_full(pool, T["rope"][n])
                pool.tensor_tensor(tbuf[:, n % 2, :], tbuf[:, n % 2, :], const("rope_cos"), ALU.mult).then_inc(sem("rope_kept"), 1)
            for u in range(U["ikw"] + 2, U["up2"] + 1):
                lo(u)
            pool.wait_ge(sem("x_ready"), 4 * KT)
            pool.dma_start(gain_final, A["norm_final_g_2"].partition_broadcast(P)).then_inc(sem("gain_in"), 16)
            hidden("2")

        @block.scalar
        def _(act):
            ch = Chain(act, "act_step")
            vector_load(act, 0)

            def split(u, i=0, units=0):
                act.wait_ge(loaded[u % 2], loaded_at(u) + (i * 16 if units else 0))
                if u >= 2:
                    act.wait_ge(w_used, u - 1 + i)
                act.activation(w_hi[u % 2][:, :], raw[u % 2][:, :], ACT.Copy).then_inc(hi_done, 1)

            sqn = [0]

            def square(src):
                n = sqn[0]
                if n >= 2:
                    act.wait_ge(sem("sq_used"), n - 1)
                sqn[0] += 1
                return act.activation(sq[:, n % 2, :], src, ACT.Square)

            def squares(k):
                for c in range(KT):
                    act.wait_ge(sem("x_ready"), KT * k + c + 1)
                    c = ORDER[k][c]
                    square(x[:, c, :]).then_inc(sem("sq_ready"), 1)

            def log_and_exp():
                act.preload_act_table_set("natural_log_exp_and_others")

            def rsqrt(t):
                wait_full(act, t)
                ch.link(act.activation(rstd[:, :], bank[t.bank][:, :], ACT.Ln, bias=eps))
                act.activation(rstd[:, :], rstd[:, :], ACT.Exp, scale=-0.5).then_inc(read[t.bank], 1)

            hn = [0]

            def norm_hi(shift=None):
                for c in range(KT):
                    hn[0] += 1
                    act.wait_ge(sem("h_t"), hn[0])
                    b = 0.0 if shift is None else mod[:, shift + c:shift + c + 1]
                    act.activation(h_hi[:, c, :], tbuf[:, c % 2, :], ACT.Identity, bias=b).then_inc(sem("h_hi"), 1)

            def y_split(src, k, n):
                act.wait_ge(sem("y_src"), n)
                act.activation(y_hi[:, k, :], src, ACT.Copy).then_inc(sem("y_hi"), 1)

            def out_of(t, dst, func, **kw):
                wait_full(act, t)
                src = bank[t.bank][:, :]
                if len(dst.shape) == 3:
                    src = src[:, 0:dst.shape[1] * dst.shape[2]].rearrange("p (a b) -> p a b", a=dst.shape[1])
                release(act.activation(dst, src, func, **kw), t)

            def gate_step(name, c, bias, u, used):
                split(u + 1)
                for k in range(2):
                    cc = 2 * c + k
                    if used is not None:
                        wait_read(act, T[used][cc])
                    out_of(T[name][cc], gates[:, cc, :], ACT.Sigmoid, **({} if bias is None else {"bias": col("merge_gate_b", bias + cc)}))

            wait_read(act, T["vec"][0])
            act.activation(c_act, col("c", 0, KT), ACT.Silu).then_inc(sem("c_act"), 1)
            log_and_exp()
            for c in range(KT):
                wait_full(act, T["xT"][c])
                act.activation(x[:, c, :], bank[T["xT"][c].bank][:, :], ACT.Copy).then_inc(sem("x_ready"), 1)
                act.wait_ge(sem("x_ready"), c + 1)
                act.nop().then_inc(read[T["xT"][c].bank], 1)
                square(x[:, c, :]).then_inc(sem("sq_ready"), 1)
            split(0)
            act.wait_ge(sem("eps_set"), 2)
            rsqrt(T["ss0"][0])
            norm_hi(0)

            u = U["sc"]
            split(u + 1)
            for c in range(2):
                out_of(T["sc"][c], sc_c[:, c, :], ACT.Copy)
            for k in (2, 3, 4):
                split(u + k)
            for c in range(2):
                out_of(T["conf"][c], cf_s[:, c, :], ACT.Sigmoid)
            split(IFA)
            split(U["ml"])
            for k in range(2):
                y_split(sc_acc[:, k, :], k, k + 1)
            log_and_exp()
            t = T["ifa"][0]
            wait_full(act, t)
            act.wait_ge(sem("bias_in"), 48)
            act.activation(gl_low[:, 0:S], bank[t.bank][64:64 + GC, :], ACT.Copy)
            act.activation(ml_rows[0:MH, 0, :], bank[t.bank][0:MH, :], ACT.Identity, bias=bias_if[:, 0:1])
            ch.link(act.activation(ml_rows[0:MH, 1, :], bank[t.bank][32:32 + MH, :], ACT.Identity, bias=bias_if[:, 1:2]))
            ch.link(act.activation(ml_rows[0:MH, 2, :], ml_rows[0:MH, 1, :], ACT.Abs))
            ch.link(act.activation(ml_rows[0:MH, 2, :], ml_rows[0:MH, 2, :], ACT.Exp, scale=-1.0))
            release(act.activation(ml_rows[0:MH, 2, :], ml_rows[0:MH, 2, :], ACT.Ln, bias=1.0), t)
            u = U["ml"]
            for k, (dst, func, scale) in enumerate(((ml_q, ACT.Copy, HEAD_SCALE), (ml_k, ACT.Copy, 1.0), (None, None, None),
                                                    (ml_o, ACT.Sigmoid, 1.0))):
                split(u + k + 1)
                if dst is not None:
                    for c in range(2):
                        out_of(T["ml"][2 * k + c], dst[:, c, :], func, scale=scale)
            log_and_exp()
            for c in range(2):
                act.wait_ge(sem("cf_centered"), c + 1)
                act.activation(cf_s[:, c, :], cf_acc[:, c, :], ACT.Square).then_inc(sem("cf_sq"), 1)

            def raw_gate(name, cc, bias=None):
                out_of(T[name][cc], gates[:, cc, :], ACT.Identity, **({} if bias is None else {"bias": col("merge_gate_b", bias + cc)}))

            def open_gates(name):
                for cc in range(KT):
                    wait_read(act, T[name][cc])
                    act.activation(gates[:, cc, :], gates[:, cc, :], ACT.Sigmoid).then_inc(sem(f"{name}_open"), 1)

            act.wait_ge(sem("ml_cols"), 1)
            act.activation(ml_mt, ml_mt, ACT.Exp, scale=-1.0).then_inc(sem("ml_floor"), 1)
            for n in range(MH * TT):
                h, j = divmod(n, TT)
                N = S - j * P
                if n == CF_VAR_AT + 1:
                    rsqrt(T["cf_var"][0])
                wait_full(act, T["ml_d"][n])
                if n >= 2:
                    wait_read(act, T["ml_qk"][n - 2])
                release(act.activation(tbuf[:, n % 2, 0:N], bank[T["ml_d"][n].bank][:, 0:N], ACT.Exp,
                                       bias=ml_gt[:, j * MH + h:j * MH + h + 1]), T["ml_d"][n])
                if GATE3_AFTER.get(n, 1) % 2 == 0:
                    split(U["gate3"] + GATE3_AFTER[n] // 2 + 1)
                if n - 2 in GATE3_AFTER:
                    raw_gate("gate3", GATE3_AFTER[n - 2], 3 * KT)
            split(U["gate3"] + 4)
            for c in range(2):
                act.wait_ge(sem("cf_scaled"), c + 1)
                ch.link(act.activation(cf_acc[:, c, :], cf_acc[:, c, :], ACT.Silu, bias=col("conf_ln_b", c)))
                act.activation(y_hi[:, 2 + c, :], cf_acc[:, c, :], ACT.Copy).then_inc(sem("y_hi"), 1)
            log_and_exp()
            act.wait_ge(sem("ml_ms"), 1)
            ch.link(act.activation(ml_ms, ml_ms, ACT.Ln, scale=1.0 / HD, bias=eps))
            act.activation(ml_ms, ml_ms, ACT.Exp, scale=-0.5).then_inc(sem("ml_rs"), 1)
            for cc in (6, 7):
                raw_gate("gate3", cc, 3 * KT)
            open_gates("gate3")
            split(U["y3"] + 1)
            act.wait_ge(w_used, U["y3"] + 1)
            for k in range(2):
                y_split(ml_q[:, k, :], k, 3 + k)
            u = U["gla"]
            split(u + 1)
            log_and_exp()
            act.wait_ge(sem("y_lo"), 6)
            for c in range(MT):
                t = T["gl_z"][c]
                wait_full(act, t)
                ch.link(act.activation(gl_e[:, c, :], bank[t.bank][:, :], ACT.Abs, bias=col("gla_a_bias", c)))
                ch.link(act.activation(gl_e[:, c, :], gl_e[:, c, :], ACT.Exp, scale=-1.0))
                act.activation(gl_e[:, c, :], gl_e[:, c, :], ACT.Ln, bias=1.0).then_inc(sem("gl_ln"), 1)
            split(u + 2)
            for c in range(2):
                out_of(T["gla"][c], gl_q[:, c, :], ACT.Copy, scale=HEAD_SCALE)
            TAU = 1.0 / 16.0
            for c in range(MT):
                act.wait_ge(sem("gl_bs"), c + 1)
                if c == 0:
                    act.wait_ge(sem("gl_bs"), 2)
                if c:
                    for k in range(2):
                        out_of(T["gla"][2 + k], gl_k[:, k, :], ACT.Copy)
                    split(u + 3)
                    act.wait_ge(sem("gl_scaled"), c)
                act.activation(gl_e[:, 0, :], gl_bs[:, c, :], ACT.Exp, scale=TAU)
                act.activation(gl_e[:, 1, :], gl_bs[:, c, :], ACT.Exp, scale=-TAU)
                act.activation(gl_kd[:, c, :], gl_kd[:, c, :], ACT.Exp, scale=TAU)
                act.activation(gl_a[:, c * NC:(c + 1) * NC], gl_bs[:, c, GC - 1::GC], ACT.Exp, scale=TAU).then_inc(sem("gl_exp"), 1)
            split(u + 4)
            for c in range(2):
                out_of(T["gla"][6 + c], gl_r[:, c, :], ACT.Silu)

            def gate2(tiles):
                for cc in tiles:
                    if cc % 2 == 0:
                        split(U["gate2"] + cc // 2 + 1)
                    wait_read(act, T["y3"][cc])
                    raw_gate("gate2", cc, 2 * KT)

            def gla_squares(c):
                t = T["gl_o"][c]
                wait_full(act, t)
                if c:
                    act.wait_ge(sem("y_src"), 4 + c)
                    wait_full(act, T["gl_ms"][c - 1])
                act.activation(gl_o, bank[t.bank][:, :], ACT.Copy)
                release(act.activation(gl_sq, bank[t.bank][:, :], ACT.Square), t)

            gate2(range(5))
            log_and_exp()
            gla_squares(0)
            rsqrt(T["gl_ms"][0])
            gate2(range(5, KT))
            open_gates("gate2")
            log_and_exp()
            gla_squares(1)
            rsqrt(T["gl_ms"][1])
            split(U["y2"] + 1)
            act.wait_ge(w_used, U["y2"] + 1)
            for k in range(2):
                y_split(gl_k[:, k, :], 2 + k, 5 + k)

            def ada_more(b, c):
                for n in ADA_LOADED.get((b, c), ()):
                    if n == 8:
                        act.wait_ge(sem("y_lo"), 8)
                    if n >= 12:
                        act.wait_ge(sem("ada_turned"), n - 3)
                    ada_load(act, n)

            for b, used in ((0, "y2"), (1, "y0")):
                for c in range(4):
                    gate_step(f"gate{b}", c, b * KT, U[f"gate{b}"] + c, used)
                    ada_more(b, c)
                split(U[f"y{b}"] + 1)
                ada_more(b, 4)

            def merged_hi(n):
                for c in range(KT):
                    act.wait_ge(sem("added"), KT * n + c + 1)
                    act.activation(h_hi[:, c, :], merged[:, c, :], ACT.Copy).then_inc(sem("h_hi"), 1)

            def keep_and_square(name, order):
                for c in order:
                    t = T[name][c]
                    wait_full(act, t)
                    act.activation(ybuf[:, c, :], bank[t.bank][:, :], ACT.Copy)
                    n = sqn[0]
                    act.wait_ge(sem("sq_used"), n - 1)
                    act.activation(sq[:, n % 2, :], bank[t.bank][:, :], ACT.Square).then_inc(read[t.bank], 1)
                    sqn[0] += 1

            log_and_exp()
            merged_hi(2)
            for c in range(4):
                split(U["wo"] + c + 1)
                keep_and_square("wo", (2 * c, 2 * c + 1))
            rsqrt(T["ss1"][0])
            squares(1)
            rsqrt(T["ss2"][0])
            norm_hi(3 * KT)

            def ffn(n, taps, bias):
                up, down = U["up" + n], U["down" + n]

                def part_hi(d, i=0):
                    act.wait_ge(sem("hid" + n), 2 * d + 3 + i * 2)
                    if d >= 2:
                        act.wait_ge(w_used, down + d - 1 + i)
                    k = 2 * (d % 2)
                    act.activation(y_hi[:, k:k + 2, :].rearrange("p a b -> p (a b)"), work[:, bass.ds(i * (2 * S) + d * 2 * S, 2 * S)],
                                   ACT.Copy).then_inc(sem("down_hi" + n), 1)

                def up_units(i, last=False):
                    for k in range(2):
                        split(up + k + 1, i * 2, 2)
                        if last:
                            part_hi(k)
                        act.wait_ge(sem("hid" + n), i * 2 + 1)
                        for part in range(2):
                            t = T["up" + n][2 * k + part]
                            wait_full(act, t, i)
                            at = COLUMN[taps[2]] + part * FT + k
                            kw = {}
                            if bias:
                                kw["bias"] = par[:, bass.ds(i * 2 + (COLUMN[bias] + part * FT + k), 1)]
                            act.activation(cbuf[:, k, part, :], bank[t.bank][:, :], ACT.Identity,
                                           scale=par[:, bass.ds(i * 2 + at, 1)], **kw).then_inc(sem("center" + n), 1)
                        wait_read(act, T["up" + n][2 * k], i)
                        act.activation(cbuf[:, k, 0, :], cbuf[:, k, 0, :], ACT.Silu).then_inc(sem("silu" + n), 1)

                with act.Fori(0, FT // 2 - 1) as i:
                    up_units(i)
                up_units(FT // 2 - 1, last=True)
                split(down + 1)
                split(down + 2)
                part_hi(2)
                with act.Fori(0, 4) as i:
                    for d in (2, 3):
                        split(down + d + 1, i * 2, 2)
                        part_hi(d + 1, i * 2)
                if down + FT // 2 < N_UNITS:
                    split(down + FT // 2)

            ffn("1", ("ffn_dw_w/0", "ffn_dw_w/1", "ffn_dw_w/2"), None)
            log_and_exp()
            keep_and_square("down1", READ_FIRST)
            rsqrt(T["ss3"][0])
            squares(2)
            rsqrt(T["ss4"][0])
            norm_hi()

            u = U["pool"]
            act.wait_ge(sem("x_ready"), 3 * KT)
            for g in range(POOL_G):
                if g % 2 == 0:
                    split(u + g // 2 + 1)
                if g:
                    act.wait_ge(sem("pooled"), g)
                out_of(T["pool"][g], pool_t[:, 0, 16:16 + S], ACT.Copy)
            split(U["q"] + 1)
            for g in range(POOL_G):
                t = T["pl"][g]
                wait_full(act, t)
                act.activation(y_hi[:, g, :], bank[t.bank][:, :], ACT.Identity, scale=col("pool_scale_2", g)).then_inc(sem("y_hi"), 1)
            rn = [0]

            def rotary():
                n = rn[0]
                if n >= 2:
                    act.wait_ge(sem("roped"), n - 1)
                rn[0] += 1
                return n % 2

            for name, scale in (("q", HEAD_SCALE), ("k", 1.0)):
                for c in range(4):
                    if c % 2 == 0 and (name, c) != ("q", 0):
                        split(U[name] + c // 2 + 1)
                    k = rotary()
                    out_of(T[name][c], tbuf[:, k, :], ACT.Copy, scale=scale)
            for c in range(2):
                split(U["v"] + c + 1)
            for c in range(4):
                if c % 2 == 0:
                    split(U["iq"] + c // 2 + 1)
                k = rotary()
                out_of(T["iq"][c], tbuf[:, k, :], ACT.Copy)
            split(U["ikw"] + 1)
            t = T["ikw"][0]
            wait_full(act, t)
            k = rotary()
            act.activation(rstd[0:NH2, :], bank[t.bank][HD:HD + NH2, :], ACT.Copy, scale=float(NH2) ** -0.5)
            act.activation(tbuf[0:HD, k, :], bank[t.bank][0:HD, :], ACT.Copy)
            release(act.activation(tbuf[HD:P, k, :], bank[t.bank][0:HD, :], ACT.Copy), t)

            def indexer(qt):
                N = (qt + 1) * P
                for h in range(NH2):
                    n = (qt - 1) * NH2 + h
                    t = T["idx"][n]
                    wait_full(act, t)
                    if n >= 2:
                        act.wait_ge(sem("idx_used"), n - 1)
                    else:
                        act.wait_ge(sem("roped"), 13)
                    release(act.activation(tbuf[:, n % 2, 0:N], bank[t.bank][:, 0:N], ACT.Relu, scale=HEAD_SCALE), t)

            indexer(1)
            for c in range(2):
                gate_step("gp", c, None, U["gp"] + c, None)
            indexer(2)
            for c in range(2, 4):
                gate_step("gp", c, None, U["gp"] + c, None)
            indexer(3)
            for c in range(2):
                split(U["yp"] + c + 1)

            def at_exponentials(n):
                N = (n // NH2 + 1) * P
                act.wait_ge(sem("at_max"), n + 1)
                act.activation(at_s[:, n % 2, 0:N], at_s[:, n % 2, 0:N], ACT.Exp, bias=at_m[:, n % 16:n % 16 + 1],
                               accum_out=at_sum[:, n % 16:n % 16 + 1]).then_inc(sem("at_exp"), 1)

            def at_turned(n):
                N, t = (n // NH2 + 1) * P, T["pt"][n]
                wait_full(act, t)
                if n >= 2:
                    act.wait_ge(sem("at_pv"), n - 1)
                release(act.activation(at_pt[:, n % 2, 0:N], bank[t.bank][:, 0:N], ACT.Copy), t)

            for n in range(HEADS + 4):
                if n < HEADS:
                    at_exponentials(n)
                if 1 <= n <= HEADS:
                    at_turned(n - 1)
                if n and ga_step(n - 1) is not None:
                    cc = ga_step(n - 1)
                    wait_read(act, T["yp"][cc])
                    raw_gate("ga", cc)
                if ga_step(n) is not None and ga_step(n) % 2 == 0:
                    split(U["ga"] + ga_step(n) // 2 + 1)
                if out_step(n) is not None:
                    qt = out_step(n)
                    t = T["oT"][qt]
                    wait_full(act, t)
                    act.activation(y_hi[:, :, qt * P:(qt + 1) * P], bank[t.bank][:, :].rearrange("p (a b) -> p a b", a=4), ACT.Copy)\
                        .then_inc(sem("y_hi"), 1)
            split(U["ya"] + 1)
            open_gates("ga")
            split(U["ya"] + 2)
            merged_hi(3)
            for c in range(4):
                split(U["wo2"] + c + 1)
            log_and_exp()
            squares(3)
            rsqrt(T["ss5"][0])
            norm_hi()
            ffn("2", ("conv_w_2/0", "conv_w_2/1", "conv_w_2/2"), "conv_b_2")
            log_and_exp()
            for n in range(2 * TT):
                t = T["fin"][n]
                wait_full(act, t)
                act.activation(h_hi[:, n, :], bank[t.bank][:, :], ACT.Square, accum_out=fin_s[:, n:n + 1]).then_inc(sem("fin_sq"), 1)
            act.wait_ge(sem("fin_sum"), 1)
            r = fin_s[:, 2 * TT:3 * TT]
            ch.link(act.activation(r, r, ACT.Ln, scale=1.0 / D, bias=eps))
            act.activation(r, r, ACT.Exp, scale=-0.5).then_inc(sem("fin_rstd"), 1)

        @block.tensor
        def _(pe):
            def weights_ready(u, i=0):
                pe.wait_ge(parted[u % 2], u // 2 + 1 + i)

            def three(dst, u, at, n, hi, lo, first, last):
                s = u % 2
                pe.matmul(dst, w_hi[s][:, at:at + n], hi, start=first, stop=False)
                pe.matmul(dst, w_hi[s][:, at:at + n], lo, start=False, stop=False)
                return pe.matmul(dst, w_lo[s][:, at:at + n], hi, start=False, stop=last)

            def three_v(dst, u, at, n, hi, lo, first, last):
                s = u % 2
                pe.matmul(dst, hi, w_hi[s][:, at:at + n], start=first, stop=False)
                pe.matmul(dst, lo, w_hi[s][:, at:at + n], start=False, stop=False)
                return pe.matmul(dst, hi, w_lo[s][:, at:at + n], start=False, stop=last)

            def ada_columns(t, n, first):
                if n == first:
                    wait_free(pe, t)
                alone = n in ADA_BY_PE
                if alone:
                    pe.wait_ge(sem(f"ada_in{n}"), 16)
                    pe.wait_ge(sem("c_act"), 1)
                else:
                    pe.wait_ge(sem("ada_summed"), summed(n))
                for k in range(2):
                    at = 2 * (n - first) + k
                    for r in range(KT if alone else 1):
                        mm = pe.matmul(bank[t.bank][:, at:at + 1], ada_place(n)[:, r, k * P:(k + 1) * P],
                                       c_act[:, r:r + 1] if alone else one, start=r == 0, stop=r == KT - 1 or not alone)
                mm.then_inc(sem("ada_turned"), 1)

            hseen = [0]

            def column_unit(u, tl, kt=KT, hi=h_hi, lo=h_lo, j=0, rows=P, fresh=False, at=0):
                weights_ready(u, j)
                C = UNIT // kt
                for n, t in enumerate(tl):
                    wait_free(pe, t, j)
                    for k in range(kt):
                        if fresh and n == 0:
                            pe.wait_ge(sem("h_ready"), hseen[0] + k + 1)
                        mm = three(bank[t.bank][0:rows, :], u, k * C + (at + n) * P, rows, hi[:, k, :], lo[:, k, :], k == 0, k == kt - 1)
                    done(mm, t)
                if fresh:
                    hseen[0] += kt

            def column_tile(name, n):
                column_unit(U[name] + n // 2, [T[name][n]], at=n % 2)

            def token_unit(u, tl):
                weights_ready(u)
                for n, t in enumerate(tl):
                    wait_free(pe, t)
                    for m in range(2):
                        for k in range(KT):
                            tok = slice((2 * n + m) * P, (2 * n + m + 1) * P)
                            mm = three_v(bank[t.bank][:, m * 256:(m + 1) * 256], u, k * 256, 256, h_hi[:, k, tok], h_lo[:, k, tok],
                                         k == 0, k == KT - 1)
                    done(mm, t)

            def turn(t, parts):
                wait_free(pe, t)
                for at, src in parts:
                    r, n = src.shape[0], src.shape[1]
                    mm = pe.transpose(bank[t.bank][0:n, at:at + r], src, ident[0:r, 0:r])
                done(mm, t)

            sn = [0]

            def mean_square(t, banks=None, cs=range(KT)):
                if cs[0] == 0:
                    wait_free(pe, t)
                for c in cs:
                    n = sn[0]
                    if banks is None:
                        mean_square.direct += 1
                        pe.wait_ge(sem("sq_ready"), mean_square.direct)
                    else:
                        wait_read(pe, banks[c])
                    mm = pe.matmul(bank[t.bank][:, :], const("ones_d"), sq[:, n % 2, :], start=c == 0, stop=c == KT - 1)
                    mm.then_inc(sem("sq_used"), 1)
                    sn[0] += 1
            mean_square.direct = 0

            pe.wait_ge(sem("consts_in"), 16)

            def turn_vectors(g):
                pe.wait_ge(sem(f"vec_in{g}"), 16 * len(VECTORS[g]))
                turn(T["vec"][g], [(0, rows_in[0:sum(n for _, n in VECTORS[g]), g, :])])

            turn_vectors(0)
            pe.wait_ge(sem("x_in"), 16 * TT)
            for c in range(KT):
                turn(T["xT"][c], [(tt * P, x_tok[:, tt, c * P:(c + 1) * P]) for tt in range(TT)])
                if c >= 2:
                    mean_square(T["ss0"][0], cs=(c - 2,))
            mean_square(T["ss0"][0], cs=(KT - 2, KT - 1))
            for g in range(1, len(VECTORS)):
                turn_vectors(g)
            pe.wait_ge(sem("eps_set"), 2)
            for n in range(8):
                ada_columns(T["ada0"][0], n, 0)
            u = U["sc"]
            for k in range(3):
                column_unit(u + k, T["sc"][2 * k:2 * k + 2], fresh=k == 0)
            for k in range(2):
                column_unit(U["conf"] + k, T["conf"][2 * k:2 * k + 2])
            column_unit(IFA, T["ifa"])
            for k in range(3):
                (token_unit if k == 2 else column_unit)(U["ml"] + k, T["ml"][2 * k:2 * k + 2])

            def conformer_mean(t, src, there):
                wait_free(pe, t)
                for c in range(MT):
                    pe.wait_ge(there, c + 1)
                    mm = pe.matmul(bank[t.bank][:, :], const("ones_mix"), src[:, c, :], start=c == 0, stop=c == MT - 1)
                done(mm, t)

            pe.wait_ge(sem("ml_gates"), 1)
            turn(T["ml_cols"][0], [(r * 16 + j * MH, ml_rows[0:MH, 4 + r, j * P:(j + 1) * P]) for r in range(2) for j in range(TT)])
            column_unit(U["ml"] + 3, T["ml"][6:8])
            conformer_mean(T["cf_mu"][0], cf_acc, sem("cf_conv"))

            def ml_scores(h, j):
                n = h * TT + j
                t, N, lo = T["ml_d"][n], S - j * P, (h % 2) * HD
                wait_free(pe, t)
                pe.matmul(bank[t.bank][:, 0:N], const("sel")[0:MH, h * P:(h + 1) * P], ml_nm[0:MH, j * P:S], start=True, stop=False)
                done(pe.matmul(bank[t.bank][:, 0:P], ident, const("causal_st"), start=False, stop=True), t)
                t = T["ml_qk"][n]
                wait_free(pe, t)
                done(pe.matmul(bank[t.bank][:, 0:N], ml_k[lo:lo + HD, h // 2, j * P:(j + 1) * P], ml_q[lo:lo + HD, h // 2, j * P:S],
                               start=True, stop=True), t)

            def ml_values(h):
                t = T["ml_n"][h]
                wait_free(pe, t)
                for i in range(TT):
                    wait_read(pe, T["ml_qk"][h * TT + i])
                    for j in range(i + 1):
                        mm = pe.matmul(bank[t.bank][:, i * (HD + 1):(i + 1) * (HD + 1)], ml_p[:, h % 2, j, i * P:(i + 1) * P],
                                       ml_v[:, j, h * (HD + 1):(h + 1) * (HD + 1)], start=j == 0, stop=j == i)
                done(mm, t)

            for c in range(2):
                wait_read(pe, T["ml"][c])
                wait_read(pe, T["ml"][2 + c])
                wait_read(pe, T["ml"][4 + c])
            for n in range(MH * TT):
                h, j = divmod(n, TT)
                if n == CF_VAR_AT:
                    conformer_mean(T["cf_var"][0], cf_s, sem("cf_sq"))
                ml_scores(h, j)
                if h and j == 1:
                    ml_values(h - 1)
                if n in GATE3_AFTER:
                    column_tile("gate3", GATE3_AFTER[n])
            ml_values(MH - 1)
            for cc in (6, 7):
                column_tile("gate3", cc)
            pe.wait_ge(sem("ml_normed"), 1)
            for c in range(MT):
                turn(T["ml_hT"][c], [(i * P, ml_h[:, i, c * P:(c + 1) * P]) for i in range(TT)])

            def branch_unit(name, k0, n):
                pe.wait_ge(sem("y_lo"), n)
                column_unit(U[name], T[name], 2, y_hi[:, k0:k0 + 2, :], y_lo[:, k0:k0 + 2, :])

            branch_unit("y3", 0, 2)
            for c in range(MT):
                t = T["gl_z"][c]
                wait_free(pe, t)
                done(pe.matmul(bank[t.bank][:, :], gl_low[:, S + c * P:S + (c + 1) * P], gl_low[:, 0:S], start=True, stop=True), t)
            for k in range(3):
                (token_unit if k == 2 else column_unit)(U["gla"] + k, T["gla"][2 * k:2 * k + 2])
            for c in range(MT):
                pe.wait_ge(sem("gl_kd"), c + 1)
                turn(T["gl_kdT"][c], [(j * P, gl_kd[:, c, j * P:(j + 1) * P]) for j in range(TT)])
            column_unit(U["gla"] + 3, T["gla"][6:8])

            def gla_states(n):
                c, j = divmod(n, TT)
                t = T["gl_u"][n]
                wait_free(pe, t)
                pe.wait_ge(sem("gl_placed"), 2 * n + 2)
                for hh in range(2):
                    mm = pe.matmul(bank[t.bank][hh * HD:(hh + 1) * HD, :], gl_kdt[:, c, j * P + hh * HD:j * P + (hh + 1) * HD],
                                   tbuf[:, hh, :], start=True, stop=True)
                done(mm, t)
                if n in GATE2_AFTER:
                    column_tile("gate2", GATE2_AFTER[n])

            def gla_scores(n):
                c, hh = divmod(n, 2)
                rows, t = slice(hh * HD, (hh + 1) * HD), T["gl_a"][n]
                wait_free(pe, t)
                pe.wait_ge(sem("gl_ks"), c + 1)
                for j in range(TT):
                    mm = pe.matmul(bank[t.bank][:, j * P:(j + 1) * P], gl_k[rows, c, j * P:(j + 1) * P],
                                   gl_q[rows, c, j * P:(j + 1) * P], start=True, stop=True)
                done(mm, t)

            def gla_within(n):
                c, hh = divmod(n, 2)
                rows, o = slice(hh * HD, (hh + 1) * HD), T["gl_o"][c]
                wait_read(pe, T["gl_a"][n])
                for j in range(TT):
                    mm = pe.matmul(bank[o.bank][rows, j * P:(j + 1) * P], gl_v[:, j, n * HD:(n + 1) * HD], gl_at[:, j, :],
                                   start=j == 0, stop=False, skip_group_check=True)
                mm.then_inc(sem("gl_at_used"), 1)

            def gla_before(n):
                c, hh = divmod(n, 2)
                rows, o = slice(hh * HD, (hh + 1) * HD), T["gl_o"][c]
                pe.wait_ge(sem("gl_state"), c + 1)
                for k in range(1, NC):
                    mm = pe.matmul(bank[o.bank][rows, k * GC:(k + 1) * GC], gl_u[rows, :, k - 1], gl_q[rows, c, k * GC:(k + 1) * GC],
                                   start=False, stop=k == NC - 1, skip_group_check=True)
                return mm

            def gla_result(c, tile):
                gla_scores(2 * c)
                column_tile("gate2", tile)
                wait_free(pe, T["gl_o"][c])
                gla_within(2 * c)
                gla_scores(2 * c + 1)
                gla_before(2 * c)
                gla_within(2 * c + 1)
                done(gla_before(2 * c + 1), T["gl_o"][c])

            def gla_mean_square(c):
                wait_read(pe, T["gl_o"][c])
                t = T["gl_ms"][c]
                wait_free(pe, t)
                done(pe.matmul(bank[t.bank][:, :], const("ones_head"), gl_sq, start=True, stop=True), t)

            for c in range(MT):
                wait_read(pe, T["gl_kdT"][c])
            for n in range(TT):
                gla_states(n)
            gla_result(0, 4)
            gla_states(TT)
            gla_mean_square(0)
            for n in range(TT + 1, 2 * TT):
                gla_states(n)
            gla_result(1, 7)
            gla_mean_square(1)
            branch_unit("y2", 2, 4)
            for k in range(2):
                for c in range(4):
                    column_unit(U[f"gate{k}"] + c, T[f"gate{k}"][2 * c:2 * c + 2])
                    for p in ADA_TURNED.get((k, c), ()):
                        ada_columns(T["ada1"][0], p, 8)
                branch_unit(f"y{k}", 2 * k, 6 + 2 * k)
                for p in ADA_TURNED[(k, 4)]:
                    ada_columns(T["ada1"][0], p, 8)
            for c in range(4):
                column_unit(U["wo"] + c, T["wo"][2 * c:2 * c + 2], fresh=c == 0)
                if c == 2:
                    for p in (22, 23):
                        ada_columns(T["ada1"][0], p, 8)
                if c:
                    mean_square(T["ss1"][0], T["wo"], (2 * c - 2, 2 * c - 1))
            mean_square(T["ss1"][0], T["wo"], (6, 7))
            mean_square(T["ss2"][0])

            def ffn(n):
                up, down = U["up" + n], U["down" + n]
                for k in range(2):
                    column_unit(up + k, T["up" + n][2 * k:2 * k + 2], fresh=k == 0)
                with pe.Fori(1, FT // 2) as i:
                    for k in range(2):
                        column_unit(up + k, T["up" + n][2 * k:2 * k + 2], j=i)

                def down_unit(d, i=0, first=False, last=False):
                    u = down + d
                    weights_ready(u, i)
                    pe.wait_ge(sem("down_lo" + n), d + 1 + i * 2)
                    for c in range(KT):
                        t = T["down" + n][c]
                        if first:
                            wait_free(pe, t)
                        for q in range(2):
                            k = 2 * (d % 2) + q
                            mm = three(bank[t.bank][:, :], u, q * D + c * P, P, y_hi[:, k, :], y_lo[:, k, :],
                                       first and q == 0, last and q == 1)
                        if last:
                            done(mm, t)
                    if not last:
                        mm.then_inc(w_used, 1)

                down_unit(0, first=True)
                down_unit(1)
                with pe.Fori(0, 4) as i:
                    for d in (2, 3):
                        down_unit(d, i)
                down_unit(10, last=True)

            ffn("1")
            mean_square(T["ss3"][0], [T["down1"][c] for c in READ_FIRST])
            mean_square(T["ss4"][0])

            for k in range(2):
                column_unit(U["pool"] + k, T["pool"][2 * k:2 * k + 2], fresh=k == 0)
            rn = [0]

            def swap():
                n = rn[0]
                t = T["rope"][n]
                wait_free(pe, t)
                done(pe.matmul(bank[t.bank][:, :], const("rope_swap"), tbuf[:, n % 2, :], start=True, stop=True), t)
                rn[0] += 1

            def project_pooled():
                for g in range(POOL_G):
                    t = T["pl"][g]
                    wait_free(pe, t)
                    pe.wait_ge(sem("pool_w_in"), 16)
                    pe.wait_ge(sem("pooled"), g + 1)
                    done(pe.matmul(bank[t.bank][:, :], pool_w[:, g, :], pooled[:, g, :], start=True, stop=True), t)

            for name in ("q", "k"):
                for k in range(2):
                    column_unit(U[name] + k, T[name][2 * k:2 * k + 2])
                    if (name, k) == ("q", 0):
                        project_pooled()
                    for c in range(2):
                        wait_read(pe, T[name][2 * k + c])
                        swap()
            for k in range(2):
                token_unit(U["v"] + k, T["v"][2 * k:2 * k + 2])
            for k in range(2):
                column_unit(U["iq"] + k, T["iq"][2 * k:2 * k + 2])
                for c in range(2):
                    wait_read(pe, T["iq"][2 * k + c])
                    swap()
            column_unit(U["ikw"], T["ikw"], rows=P)
            wait_read(pe, T["ikw"][0])
            swap()
            turn(T["iwT"][0], [(qt * NH2, rstd[0:NH2, qt * P:(qt + 1) * P]) for qt in range(TT)])

            def indexer(qt):
                pe.wait_ge(sem("roped"), 13)
                for h in range(NH2):
                    t, lo = T["idx"][(qt - 1) * NH2 + h], (h % 2) * HD
                    wait_free(pe, t)
                    done(pe.matmul(bank[t.bank][:, 0:(qt + 1) * P], iq[lo:lo + HD, h // 2, qt * P:(qt + 1) * P],
                                   ik[lo:lo + HD, 0:(qt + 1) * P], start=True, stop=True), t)

            def gate_two(name, c0, c1):
                for c in range(c0, c1):
                    column_unit(U[name] + c, T[name][2 * c:2 * c + 2])

            def proj_units(name):
                for c in range(2):
                    column_unit(U[name] + c, T[name][4 * c:4 * c + 4], 4, y_hi, y_lo)

            indexer(1)
            gate_two("gp", 0, 2)
            indexer(2)
            gate_two("gp", 2, 4)
            indexer(3)
            pe.wait_ge(sem("y_lo"), 8 + POOL_G)
            proj_units("yp")

            def scores(n):
                qt, h = divmod(n, NH2)
                lo = (h % 2) * HD
                t = T["s"][n]
                wait_free(pe, t)
                done(pe.matmul(bank[t.bank][:, 0:(qt + 1) * P], at_q[lo:lo + HD, h // 2, qt * P:(qt + 1) * P],
                               at_k[lo:lo + HD, h // 2, 0:(qt + 1) * P], start=True, stop=True), t)

            def turn_weights(n):
                qt = n // NH2
                pe.wait_ge(sem("at_exp"), n + 1)
                turn(T["pt"][n], [(kb * P, at_s[:, n % 2, kb * P:(kb + 1) * P]) for kb in range(qt + 1)])

            def weigh_values(n):
                qt, h = divmod(n, NH2)
                wait_read(pe, T["pt"][n])
                o = T["o"][qt]
                if h == 0:
                    wait_free(pe, o)
                for kb in range(qt + 1):
                    mm = pe.matmul(bank[o.bank][:, h * HD:(h + 1) * HD], at_pt[:, n % 2, kb * P:(kb + 1) * P],
                                   at_v[:, kb, h * HD:(h + 1) * HD], start=kb == 0, stop=kb == qt)
                mm.then_inc(sem("at_pv"), 1)

            for n in range(HEADS + 4):
                if n < HEADS:
                    scores(n)
                if 1 <= n <= HEADS:
                    turn_weights(n - 1)
                if 2 <= n <= HEADS + 1:
                    weigh_values(n - 2)
                if ga_step(n) is not None:
                    column_tile("ga", ga_step(n))
                if out_step(n) is not None:
                    qt = out_step(n)
                    pe.wait_ge(sem("o_scaled"), qt + 1)
                    turn(T["oT"][qt], [(c * P, tbuf[:, qt % 2, c * P:(c + 1) * P]) for c in range(4)])
            pe.wait_ge(sem("y_lo"), 8 + POOL_G + TT)
            proj_units("ya")
            for c in range(4):
                column_unit(U["wo2"] + c, T["wo2"][2 * c:2 * c + 2], fresh=c == 0)
            mean_square(T["ss5"][0])
            ffn("2")
            for k in range(2):
                for tt in range(TT):
                    pe.wait_ge(sem("x_ready"), 4 * KT + 4 * (k + 1))
                    turn(T["fin"][tt + TT * k], [(c * P, x[:, 4 * k + c, tt * P:(tt + 1) * P]) for c in range(4)])

        @block.vector
        def _(dve):
            ch = Chain(dve, "dve_step")

            def lo(u, i=0):
                dve.wait_ge(hi_done, u + 1 + i)
                dve.tensor_tensor(w_lo[u % 2][:, :], raw[u % 2][:, :], w_hi[u % 2][:, :].bitcast(FP32), ALU.subtract)\
                   .then_inc(parted[u % 2], 1)

            hn = [0]

            def norm_lo(ss, gains, shift=None):
                wait_read(dve, T[ss][0])
                for c in range(KT + 1):
                    if c < KT:
                        if c >= 2:
                            dve.wait_ge(sem("h_ready"), hn[0])
                        dve.scalar_tensor_tensor(out=tbuf[:, c % 2, :], in0=x[:, c, :], scalar=gains[:, c:c + 1], in1=rstd[:, :],
                                                 op0=ALU.mult, op1=ALU.mult).then_inc(sem("h_t"), 1)
                    if c:
                        k = c - 1
                        hn[0] += 1
                        dve.wait_ge(sem("h_hi"), hn[0])
                        dve.scalar_tensor_tensor(out=h_lo[:, k, :], in0=tbuf[:, k % 2, :],
                                                 scalar=0.0 if shift is None else mod[:, shift + k:shift + k + 1],
                                                 in1=h_hi[:, k, :].bitcast(FP32), op0=ALU.add, op1=ALU.subtract)\
                           .then_inc(sem("h_ready"), 1)

            def y_lo_of(src, k, n):
                dve.wait_ge(sem("y_hi"), n)
                dve.tensor_tensor(y_lo[:, k, :], src, y_hi[:, k, :].bitcast(FP32), ALU.subtract).then_inc(sem("y_lo"), 1)

            def take_vectors(g):
                t, n = T["vec"][g], sum(m for _, m in VECTORS[g])
                wait_full(dve, t)
                release(dve.tensor_copy(par[:, g * P:g * P + n], bank[t.bank][:, 0:n]), t)

            take_vectors(0)
            dve.wait_ge(sem("c_act"), 1)

            def ada_sum(n, unit):
                dve.wait_ge(sem(f"ada_in{n % 8}"), 16 * (n // 8 + 1))
                ch.link(dve.tensor_scalar(unit[:, 0, :], unit[:, 0, :], c_act[:, 0:1], None, ALU.mult))
                for k in range(1, KT):
                    ins = dve.scalar_tensor_tensor(out=unit[:, 0, :], in0=unit[:, k, :], scalar=c_act[:, k:k + 1], in1=unit[:, 0, :],
                                                   op0=ALU.mult, op1=ALU.add)
                    if k < KT - 1:
                        ch.link(ins)
                ins.then_inc(sem("ada_summed"), 1)

            def ada_out(t, at, n):
                wait_full(dve, t)
                release(dve.tensor_tensor(mod[:, at:at + n], bank[t.bank][:, 0:n], col("ada_b", at, n), ALU.add), t)

            for n in range(8):
                if n == 4:
                    for g in range(1, len(VECTORS)):
                        take_vectors(g)
                if n not in ADA_BY_PE:
                    ada_sum(n, ada_place(n))
            ada_out(T["ada0"][0], 0, 2 * KT)

            wait_read(dve, T["ada0"][0])
            ch.link(dve.scalar_tensor_tensor(out=gain[:, 0, :], in0=mod[:, KT:2 * KT], scalar=1.0, in1=col("tm_pre_g", 0, KT),
                                             op0=ALU.add, op1=ALU.mult))
            norm_lo("ss0", gain[:, 0, :], 0)

            u = U["sc"]
            dve.wait_ge(sem("pads"), 2)
            for c in range(2):
                t = T["sc"][2 + c]
                wait_read(dve, T["sc"][c])
                wait_full(dve, t)
                release(dve.tensor_tensor(sc_z[:, c, 2:2 + S], bank[t.bank][:, :], sc_c[:, c, :], ALU.mult), t)
            for c in range(2):
                wait_read(dve, T["sc"][2 + c])
                ch.tick(dve.tensor_scalar(sc_acc[:, c, :], sc_z[:, c, 2:2 + S], col("sc_dw_w", 2 * MT + c), None, ALU.mult))
            for tap in (1, 0):
                for c in range(2):
                    dve.wait_ge(ch.sem, ch.n - 1)
                    ch.tick(dve.scalar_tensor_tensor(out=sc_acc[:, c, :], in0=sc_z[:, c, tap:tap + S], scalar=col("sc_dw_w", tap * MT + c),
                                                     in1=sc_acc[:, c, :], op0=ALU.mult, op1=ALU.add))
            for c in range(2):
                t = T["sc"][4 + c]
                wait_full(dve, t)
                dve.wait_ge(ch.sem, ch.n)
                release(dve.tensor_tensor(sc_acc[:, c, :], bank[t.bank][:, :], sc_acc[:, c, :], ALU.mult), t)
            for c in range(2):
                wait_read(dve, T["sc"][4 + c])
                dve.nop().then_inc(sem("y_src"), 1)
            for c in range(2):
                t = T["conf"][2 + c]
                wait_read(dve, T["conf"][c])
                wait_full(dve, t)
                release(dve.tensor_tensor(cf_u[:, c, 30:30 + S], bank[t.bank][:, :], cf_s[:, c, :], ALU.mult), t)
            for c in range(2):
                wait_read(dve, T["conf"][2 + c])
                ch.tick(dve.tensor_scalar(cf_acc[:, c, :], cf_u[:, c, 0:S], col("conf_dw_w", c), col("conf_dw_b", c), ALU.mult, ALU.add))
            for k in range(2):
                y_lo_of(sc_acc[:, k, :], k, k + 1)

            def conf_taps(a, b):
                for tap in range(a, b):
                    for c in range(2):
                        dve.wait_ge(ch.sem, ch.n - 1)
                        ins = dve.scalar_tensor_tensor(out=cf_acc[:, c, :], in0=cf_u[:, c, tap:tap + S], scalar=col("conf_dw_w", tap * MT + c),
                                                       in1=cf_acc[:, c, :], op0=ALU.mult, op1=ALU.add)
                        ch.tick(ins)

            TAPS_FIRST = 12
            conf_taps(1, TAPS_FIRST)

            r = lambda k: ml_rows[0:MH, k, :]
            nm = ml_nm[0:MH, :]
            wait_read(dve, T["ifa"][0])
            ch.tick(dve.memset(r(5), 1.0))
            ch.link(dve.tensor_scalar(r(3), r(1), 0.0, None, ALU.min))
            ch.link(dve.tensor_tensor(r(3), r(3), r(2), ALU.subtract))
            ch.link(dve.tensor_tensor_scan(r(1), r(5), r(3), 0.0, ALU.mult, ALU.add))
            ch.link(dve.tensor_tensor(r(4), r(0), r(1), ALU.subtract))
            ch.link(dve.tensor_tensor_scan(nm, r(4), r(4), 0.0, ALU.max, ALU.max))
            ch.link(dve.tensor_tensor(r(5), r(1), nm, ALU.add))
            ch.link(dve.tensor_scalar(nm, nm, -1.0, None, ALU.mult))
            dve.nop().then_inc(sem("ml_gates"), 1)
            conf_taps(TAPS_FIRST, CONF_W)
            dve.wait_ge(ch.sem, ch.n)
            for c in range(2):
                dve.nop().then_inc(sem("cf_conv"), 1)
            ch.tick(dve.memset(ml_v.rearrange("p j (h e) -> p (j h) e", h=MH)[:, :, HD:HD + 1], 1.0))
            for c in range(2):
                t = T["ml"][4 + c]
                wait_full(dve, t)
                for m in range(2):
                    ins = dve.tensor_copy(ml_v[:, 2 * c + m, :].rearrange("p (h e) -> p h e", h=MH)[:, :, 0:HD],
                                          bank[t.bank][:, m * 256:(m + 1) * 256].rearrange("p (h e) -> p h e", h=MH))
                release(ins, t)
            t = T["cf_mu"][0]
            wait_full(dve, t)
            for c in range(2):
                ins = dve.tensor_tensor(cf_acc[:, c, :], cf_acc[:, c, :], bank[t.bank][:, :], ALU.subtract)
                ins.then_inc(sem("cf_centered"), 1)
            dve.wait_ge(sem("cf_centered"), 2)
            dve.nop().then_inc(read[t.bank], 1)
            t = T["ml_cols"][0]
            wait_full(dve, t)
            ins = dve.tensor_copy(small[:, 48:80], bank[t.bank][:, 0:32])
            ins.then_inc(sem("ml_cols"), 1)
            dve.wait_ge(sem("ml_cols"), 1)
            dve.nop().then_inc(read[t.bank], 1)

            def ml_weights(h, j):
                n, N = h * TT + j, S - j * P
                wait_read(dve, T["ml_d"][n])
                wait_full(dve, T["ml_qk"][n])
                release(dve.tensor_tensor(ml_p[:, h % 2, j, j * P:S], bank[T["ml_qk"][n].bank][:, 0:N], tbuf[:, n % 2, 0:N], ALU.mult),
                        T["ml_qk"][n])

            def ml_divide(h):
                t = T["ml_n"][h]
                wait_full(dve, t)
                v = bank[t.bank][:, 0:TT * (HD + 1)].rearrange("p (i e) -> p i e", i=TT)
                ch.link(dve.tensor_scalar(ml_d, v[:, :, HD], -1.0, None, ALU.mult))
                ch.link(dve.tensor_tensor(ml_d, v[:, :, HD], ml_d, ALU.max))
                ch.link(dve.tensor_tensor(ml_d, ml_d, ml_mt[:, h:16:MH], ALU.max))
                ch.link(dve.reciprocal(ml_d, ml_d))
                release(dve.tensor_tensor(ml_h[:, :, h * HD:(h + 1) * HD], v[:, :, 0:HD], ml_d.unsqueeze(2).broadcast_to([P, TT, HD]),
                                          ALU.mult), t)

            dve.wait_ge(sem("ml_floor"), 1)
            for h in range(MH):
                for j in range(TT):
                    ml_weights(h, j)
                    if h * TT + j == CF_VAR_AT + 1:
                        wait_read(dve, T["cf_var"][0])
                        for c in range(2):
                            dve.scalar_tensor_tensor(out=cf_acc[:, c, :], in0=cf_acc[:, c, :], scalar=col("conf_ln_g", c), in1=rstd[:, :],
                                                     op0=ALU.mult, op1=ALU.mult).then_inc(sem("cf_scaled"), 1)
                    if h and j == 1:
                        ml_divide(h - 1)
            ml_divide(MH - 1)
            for h in range(MH):
                wait_read(dve, T["ml_n"][h])
            hv = ml_h[:, :, :].rearrange("p i (h e) -> p (i h) e", h=MH)
            h2 = ml_p[:, 0, 0:2, :].rearrange("p a (b e) -> p (a b) e", e=HD)
            ch.link(dve.tensor_tensor(h2, hv, hv, ALU.mult))
            dve.tensor_reduce(ml_ms, h2, AX.X, ALU.add).then_inc(sem("ml_ms"), 1)
            dve.wait_ge(sem("ml_rs"), 1)
            dve.tensor_tensor(hv, hv, ml_ms.unsqueeze(2).broadcast_to([P, TT * MH, HD]), ALU.mult).then_inc(sem("ml_normed"), 1)
            for k in range(2):
                y_lo_of(cf_acc[:, k, :], 2 + k, 3 + k)
            for c in range(MT):
                t = T["ml_hT"][c]
                wait_full(dve, t)
                wait_read(dve, T["ml"][6 + c])
                release(dve.scalar_tensor_tensor(out=ml_q[:, c, :], in0=bank[t.bank][:, :], scalar=col("ml_norm_g", c), in1=ml_o[:, c, :],
                                                 op0=ALU.mult, op1=ALU.mult), t)
                wait_read(dve, t)
                dve.nop().then_inc(sem("y_src"), 1)

            gn = [0]

            def product(c):
                return rstd[:, :] if c % 3 == 2 else tbuf[:, c % 3, :]

            def add(t, c):
                wait_read(dve, t)
                gn[0] += 1
                dve.tensor_tensor(merged[:, c, :], merged[:, c, :], product(c), ALU.add).then_inc(sem("added"), 1)

            def gated(name, bias=None, first=False):
                for c in range(KT):
                    t = T[name][c]
                    wait_full(dve, t)
                    if GATE_OF[name] in ("gate3", "gate2", "ga"):
                        dve.wait_ge(sem(f"{GATE_OF[name]}_open"), c + 1)
                    else:
                        wait_read(dve, T[GATE_OF[name]][c])
                    dst = merged[:, c, :] if first else product(c)
                    if not first and gn[0] >= 2:
                        dve.wait_ge(sem("added"), gn[0] - 1)
                    ins = dve.scalar_tensor_tensor(out=dst, in0=bank[t.bank][:, :], scalar=0.0 if bias is None else col(bias, c),
                                                   in1=gates[:, c, :], op0=ALU.add, op1=ALU.mult)
                    release(ins, t)
                    if not first and c:
                        add(T[name][c - 1], c - 1)
                if not first:
                    add(T[name][KT - 1], KT - 1)

            gated("y3", first=True)
            for k in range(2):
                y_lo_of(ml_q[:, k, :], k, 5 + k)
            for c in range(MT):
                t = T["gl_z"][c]
                dve.wait_ge(sem("gl_ln"), c + 1)
                release(dve.tensor_scalar(gl_bs[:, c, :], bank[t.bank][:, :], col("gla_a_bias", c), 0.0, ALU.add, ALU.min), t)
                wait_read(dve, t)
                ch.link(dve.tensor_tensor(gl_bs[:, c, :], gl_bs[:, c, :], gl_e[:, c, :], ALU.subtract))
                ch.link(dve.tensor_tensor_scan(gl_bs[:, c, :], const("chunk_reset"), gl_bs[:, c, :], 0.0, ALU.mult, ALU.add))
                b = gl_bs[:, c, :].rearrange("p (n k) -> p n k", k=GC)
                dve.tensor_tensor(gl_kd[:, c, :].rearrange("p (n k) -> p n k", k=GC), b[:, :, GC - 1:GC].broadcast_to([P, NC, GC]), b,
                                  ALU.subtract).then_inc(sem("gl_bs"), 1)
            for c in range(2):
                for k in (0, 2):
                    wait_read(dve, T["gla"][k + c])
            for c in range(MT):
                dve.wait_ge(sem("gl_exp"), c + 1)
                ch.tick(dve.tensor_tensor(gl_q[:, c, :], gl_q[:, c, :], gl_e[:, 0, :], ALU.mult))
                dve.tensor_tensor(gl_kd[:, c, :], gl_kd[:, c, :], gl_k[:, c, :], ALU.mult).then_inc(sem("gl_kd"), 1)
                ins = dve.tensor_tensor(gl_k[:, c, :], gl_k[:, c, :], gl_e[:, 1, :], ALU.mult)
                ins.then_inc(sem("gl_ks"), 1)
                dve.wait_ge(sem("gl_ks"), c + 1)
                dve.nop().then_inc(sem("gl_scaled"), 1)
            for c in range(2):
                t = T["gla"][4 + c]
                wait_full(dve, t)
                release(dve.tensor_copy(gl_v[:, 2 * c:2 * c + 2, :], bank[t.bank][:, :].rearrange("p (a b) -> p a b", a=2)), t)
            for c in range(MT):
                t = T["gl_kdT"][c]
                wait_full(dve, t)
                release(dve.tensor_copy(gl_kdt[:, c, :], bank[t.bank][:, :]), t)
            dve.memset(gl_at[:, :, :], 0.0).then_inc(sem("gl_zero"), 1)
            dve.memset(gl_a[:, 0:1], 0.0)
            dve.memset(gl_a[:, NC:NC + 1], 0.0).then_inc(sem("gl_zero"), 1)
            dve.wait_ge(sem("gl_zero"), 2)

            def gla_norm(c):
                wait_read(dve, T["gl_ms"][c])
                ch.link(dve.scalar_tensor_tensor(out=gl_o, in0=gl_o, scalar=col("gla_norm_g", c), in1=rstd[:, :], op0=ALU.mult, op1=ALU.mult))
                wait_read(dve, T["gla"][6 + c])
                dve.tensor_tensor(gl_k[:, c, :], gl_o, gl_r[:, c, :], ALU.mult).then_inc(sem("y_src"), 1)

            for c in range(MT):
                if c:
                    wait_full(dve, T["gl_o"][c - 1])
                for j in range(TT):
                    if c == 0 and j in (1, 3):
                        lo(U["gate2"] + (j + 1) // 2)
                    t = T["gl_u"][c * TT + j]
                    wait_full(dve, t)
                    release(dve.tensor_copy(gl_u[:, :, j * CPT:(j + 1) * CPT].rearrange("p e k -> p k e"),
                                            bank[t.bank][:, :].rearrange("p (k e) -> p k e", k=CPT)), t)
                ch.link(dve.tensor_copy(gl_ab[:, :, :], gl_a[:, c * NC:(c + 1) * NC].unsqueeze(1).broadcast_to([P, HD, NC])))
                for j in range(TT):
                    wait_read(dve, T["gl_u"][c * TT + j])
                flat = lambda a: a.rearrange("p e k -> p (e k)")
                dve.tensor_tensor_scan(flat(gl_u[:, :, :]), flat(gl_ab[:, :, :]), flat(gl_u[:, :, :]), 0.0, ALU.mult, ALU.add)\
                   .then_inc(sem("gl_state"), 1)
                if c:
                    gla_norm(0)
                for hh in range(2):
                    n = 2 * c + hh
                    if n == 1:
                        lo(U["gate2"] + 3)
                    t = T["gl_a"][n]
                    wait_full(dve, t)
                    if n:
                        dve.wait_ge(sem("gl_at_used"), n)
                    release(dve.copy_predicated(gl_at[:, :, :], const("block_causal").bitcast(U32).unsqueeze(1).broadcast_to([P, TT, P]),
                                                bank[t.bank][:, :].rearrange("p (a b) -> p a b", a=TT)), t)
            gla_norm(1)
            gated("y2", "conf_out_b")
            for k in range(2):
                y_lo_of(gl_k[:, k, :], 2 + k, 7 + k)
            for n in range(8, 14):
                ada_sum(n, ada_place(n))
            gated("y0")
            for n in range(14, 22):
                ada_sum(n, ada_place(n))
            gated("y1")

            def merged_lo():
                for c in range(KT):
                    hn[0] += 1
                    dve.wait_ge(sem("h_hi"), hn[0])
                    dve.tensor_tensor(h_lo[:, c, :], merged[:, c, :], h_hi[:, c, :].bitcast(FP32), ALU.subtract).then_inc(sem("h_ready"), 1)

            merged_lo()
            for n in (22, 23):
                ada_sum(n, ada_place(n))
            ada_out(T["ada1"][0], 2 * KT, 4 * KT)
            wait_read(dve, T["ada1"][0])
            ch.tick(dve.tensor_tensor(gain[:, 1, :], mod[:, 2 * KT:3 * KT], col("tm_post_g", 0, KT), ALU.mult))
            ch.tick(dve.scalar_tensor_tensor(out=gain[:, 2, :], in0=mod[:, 4 * KT:5 * KT], scalar=1.0, in1=col("cm_pre_g", 0, KT),
                                             op0=ALU.add, op1=ALU.mult))
            ch.tick(dve.tensor_tensor(gain[:, 3, :], mod[:, 5 * KT:6 * KT], col("cm_post_g", 0, KT), ALU.mult))

            dve.wait_ge(ch.sem, ch.n)

            def residual(ss, k, order):
                wait_read(dve, T[ss][0])
                for n in range(KT + 1):
                    if n < KT:
                        c = order[n]
                        ch.tick(dve.scalar_tensor_tensor(out=ybuf[:, c, :], in0=ybuf[:, c, :], scalar=gain[:, k, c:c + 1], in1=rstd[:, :],
                                                         op0=ALU.mult, op1=ALU.mult))
                    if n:
                        c = order[n - 1]
                        dve.wait_ge(ch.sem, ch.n - (1 if n < KT else 0))
                        dve.tensor_tensor(x[:, c, :], x[:, c, :], ybuf[:, c, :], ALU.add).then_inc(sem("x_ready"), 1)

            residual("ss1", 1, ORDER[1])
            norm_lo("ss2", gain[:, 2, :], 3 * KT)

            def ffn(n, taps):
                up, down = U["up" + n], U["down" + n]

                def part_lo(d, i=0):
                    dve.wait_ge(sem("down_hi" + n), d + 1 + i)
                    k = 2 * (d % 2)
                    flat = lambda a: a[:, k:k + 2, :].rearrange("p a b -> p (a b)")
                    dve.tensor_tensor(flat(y_lo), work[:, bass.ds(i * (2 * S) + d * 2 * S, 2 * S)], flat(y_hi).bitcast(FP32),
                                      ALU.subtract).then_inc(sem("down_lo" + n), 1)

                def up_units(i, last=False):
                    for k in range(2):
                        lo(up + k + 1, i * 2)
                        if last:
                            part_lo(k)
                        for tap in (1, 0):
                            for part in range(2):
                                t, c = T["up" + n][2 * k + part], cbuf[:, k, part, :]
                                if tap:
                                    dve.wait_ge(sem("center" + n), i * 4 + (2 * k + part + 1))
                                else:
                                    dve.wait_ge(sem("tap" + n), i * 4 + (2 * k + part + 1))
                                w = par[:, bass.ds(i * 2 + (COLUMN[taps[tap]] + part * FT + k), 1)]
                                back = 2 - tap
                                ins = dve.scalar_tensor_tensor(out=c[:, back:S], in0=bank[t.bank][:, 0:S - back], scalar=w,
                                                               in1=c[:, back:S], op0=ALU.mult, op1=ALU.add)
                                ins.then_inc(sem("tap" + n), 1) if tap else release(ins, t)

                with dve.Fori(0, FT // 2 - 1) as i:
                    up_units(i)
                up_units(FT // 2 - 1, last=True)
                lo(down + 1)
                lo(down + 2)
                part_lo(2)
                with dve.Fori(0, 4) as i:
                    for d in (2, 3):
                        lo(down + d + 1, i * 2)
                        part_lo(d + 1, i * 2)
                if down + FT // 2 < N_UNITS:
                    lo(down + FT // 2)

            ffn("1", ("ffn_dw_w/0", "ffn_dw_w/1"))
            residual("ss3", 3, ORDER[2])
            norm_lo("ss4", col("norm_mix_g_2", 0, KT))

            dve.wait_ge(sem("pads"), 3)
            for g in range(POOL_G):
                wait_read(dve, T["pool"][g])
                src, dst = 0, 1
                for k in range(g + 1):
                    b = 2 ** k
                    a0 = 2 * b - 1
                    ch.link(dve.tensor_tensor(pool_t[:, dst, a0:], pool_t[:, src, a0:], pool_t[:, src, a0 - b:16 + S - b], ALU.add))
                    src, dst = dst, 3 - dst
                pc = const("pool_count")[:, g * 16:(g + 1) * 16]
                ch.link(dve.tensor_tensor(pooled[:, g, 0:16], pool_t[:, src, 16:32], pc, ALU.mult))
                ch.tick(dve.tensor_tensor(pooled[:, g, 0:16], pooled[:, g, 0:16], pool_t[:, 0, 16:32], ALU.subtract))
                dve.scalar_tensor_tensor(out=pooled[:, g, 16:S], in0=pool_t[:, src, 32:16 + S], scalar=0.5 ** (g + 1),
                                         in1=pool_t[:, 0, 32:16 + S], op0=ALU.mult, op1=ALU.subtract).then_inc(sem("pool_done"), 1)
                dve.wait_ge(sem("pool_done"), g + 1)
                dve.wait_ge(ch.sem, ch.n)
                dve.nop().then_inc(sem("pooled"), 1)
            for g in range(POOL_G):
                t = T["pl"][g]
                wait_full(dve, t)
                dve.wait_ge(sem("y_hi"), 8 + g + 1)
                ins = dve.scalar_tensor_tensor(out=y_lo[:, g, :], in0=bank[t.bank][:, :], scalar=col("pool_scale_2", g),
                                               in1=y_hi[:, g, :].bitcast(FP32), op0=ALU.mult, op1=ALU.subtract)
                ins.then_inc(sem("y_lo"), 1)
                dve.wait_ge(sem("y_lo"), 8 + g + 1)
                dve.nop().then_inc(read[t.bank], 1)
            rn = [0]

            def rope(dst):
                n = rn[0]
                t = T["rope"][n]
                wait_full(dve, t)
                release(dve.tensor_tensor(dst, bank[t.bank][:, :], const("rope_sin"), ALU.mult), t)
                wait_read(dve, t)
                dve.wait_ge(sem("rope_kept"), n + 1)
                dve.tensor_tensor(dst, dst, tbuf[:, n % 2, :], ALU.add).then_inc(sem("roped"), 1)
                rn[0] += 1

            dve.wait_ge(sem("rope_in"), 16)
            for name, dst in (("q", at_q), ("k", at_k)):
                for c in range(4):
                    rope(dst[:, c, :])
            for k in range(2):
                for c in range(2):
                    t = T["v"][2 * k + c]
                    wait_full(dve, t)
                    release(dve.tensor_copy(at_v[:, 2 * c:2 * c + 2, k * 256:(k + 1) * 256], bank[t.bank][:, :].rearrange("p (a b) -> p a b", a=2)), t)
            for c in range(4):
                rope(iq[:, c, :])
            rope(ik)
            t = T["iwT"][0]
            wait_full(dve, t)
            release(dve.tensor_copy(iw_t, bank[t.bank][:, 0:TT * NH2]), t)
            wait_read(dve, t)

            def indexer(qt):
                N = (qt + 1) * P
                acc = sq[:, qt % 2, 0:N]
                for h in range(NH2):
                    n = (qt - 1) * NH2 + h
                    wait_read(dve, T["idx"][n])
                    w = iw_t[:, qt * NH2 + h:qt * NH2 + h + 1]
                    if h == 0:
                        ins = dve.tensor_scalar(acc, tbuf[:, n % 2, 0:N], w, None, ALU.mult)
                    else:
                        ins = dve.scalar_tensor_tensor(out=acc, in0=tbuf[:, n % 2, 0:N], scalar=w, in1=acc, op0=ALU.mult, op1=ALU.add)
                    ins.then_inc(sem("idx_used"), 1)
                    dve.wait_ge(sem("idx_used"), n + 1)
                ch.link(dve.tensor_tensor(acc[:, qt * P:N], acc[:, qt * P:N], const("causal_qk"), ALU.add))

            best = small[:, 240:248]

            def top_rounds(qt, a, b):
                N = (qt + 1) * P
                acc = sq[:, qt % 2, 0:N]
                for _ in range(a, b):
                    ch.link(dve.max(best, acc))
                    ch.link(dve.match_replace(out=acc, in_to_replace=best, in_values=acc, imm_value=TAKEN))
                if b == TOPK // 8:
                    ch.link(dve.tensor_scalar(masks[qt], acc, 0.5 * TAKEN, NEG, ALU.is_gt, ALU.mult))

            ch.link(dve.tensor_copy(masks[0], const("causal_qk")))
            indexer(1)
            for c in range(2):
                top_rounds(1, 8 * c, 8 * c + 8)
            indexer(2)
            for c in range(2):
                top_rounds(2, 8 * c, 8 * c + 8)
            indexer(3)
            gated("yp", first=True)

            def at_maximum(n):
                qt = n // NH2
                N = (qt + 1) * P
                t, m = T["s"][n], at_m[:, n % 16:n % 16 + 1]
                wait_full(dve, t)
                if n >= 2:
                    wait_full(dve, T["pt"][n - 2])
                release(dve.tensor_tensor_reduce(at_s[:, n % 2, 0:N], bank[t.bank][:, 0:N], masks[qt], 1.0, 4.0 * NEG, ALU.add, ALU.max, m), t)
                wait_read(dve, t)
                dve.tensor_scalar(m, m, -1.0, None, ALU.mult).then_inc(sem("at_max"), 1)

            def at_scaled(qt):
                t = T["o"][qt]
                wait_full(dve, t)
                s = at_sum[:, (qt % 2) * NH2:(qt % 2) * NH2 + NH2]
                ch.link(dve.reciprocal(s, s))
                if qt >= 2:
                    wait_full(dve, T["oT"][qt - 2])
                ins = dve.tensor_tensor(tbuf[:, qt % 2, :].rearrange("p (h e) -> p h e", h=NH2), bank[t.bank][:, :].rearrange("p (h e) -> p h e", h=NH2),
                                        s.unsqueeze(2).broadcast_to([P, NH2, HD]), ALU.mult)
                release(ins, t)
                wait_read(dve, t)
                dve.nop().then_inc(sem("o_scaled"), 1)

            def at_lo(qt):
                t = T["oT"][qt]
                dve.wait_ge(sem("y_hi"), 8 + POOL_G + qt + 1)
                tok = slice(qt * P, (qt + 1) * P)
                dve.tensor_tensor(y_lo[:, :, tok], bank[t.bank][:, :].rearrange("p (a b) -> p a b", a=4), y_hi[:, :, tok].bitcast(FP32),
                                  ALU.subtract).then_inc(sem("y_lo"), 1)
                dve.wait_ge(sem("y_lo"), 8 + POOL_G + qt + 1)
                dve.nop().then_inc(read[t.bank], 1)

            for n in range(HEADS + 4):
                if n < HEADS:
                    at_maximum(n)
                if n < TOPK // 8:
                    top_rounds(3, n, n + 1)
                if out_step(n + 2) is not None:
                    at_scaled(out_step(n + 2))
                if out_step(n) is not None:
                    at_lo(out_step(n))
            gated("ya")
            merged_lo()
            for c in range(4):
                for k in range(2):
                    t = T["wo2"][2 * c + k]
                    wait_full(dve, t)
                    dve.tensor_tensor(x[:, 2 * c + k, :], bank[t.bank][:, :], x[:, 2 * c + k, :], ALU.add).then_inc(sem("x_ready"), 1)
                    dve.wait_ge(sem("x_ready"), 3 * KT + 2 * c + k + 1)
                    dve.nop().then_inc(read[t.bank], 1)
            norm_lo("ss5", col("norm_ffn_g_2", 0, KT))
            ffn("2", ("conv_w_2/0", "conv_w_2/1"))
            for c in range(KT):
                t = T["down2"][c]
                wait_full(dve, t)
                dve.tensor_tensor(x[:, c, :], bank[t.bank][:, :], x[:, c, :], ALU.add).then_inc(sem("x_ready"), 1)
                dve.wait_ge(sem("x_ready"), 4 * KT + c + 1)
                dve.nop().then_inc(read[t.bank], 1)
            dve.wait_ge(sem("gain_in"), 16)
            dve.wait_ge(sem("fin_sq"), 2 * TT)
            dve.tensor_tensor(fin_s[:, 2 * TT:3 * TT], fin_s[:, 0:TT], fin_s[:, TT:2 * TT], ALU.add).then_inc(sem("fin_sum"), 1)
            dve.wait_ge(sem("fin_rstd"), 1)
            for tt in range(TT):
                for k in range(2):
                    t = T["fin"][tt + TT * k]
                    release(dve.scalar_tensor_tensor(out=o_tok[:, tt, k * S:(k + 1) * S], in0=bank[t.bank][:, :], scalar=fin_s[:, 8 + tt:9 + tt],
                                                     in1=gain_final[:, k * S:(k + 1) * S], op0=ALU.mult, op1=ALU.mult), t)
                for k in range(2):
                    wait_read(dve, T["fin"][tt + TT * k])
                dve.nop().then_inc(sem("out_ready"), 1)


_INS = ["x", "c", "ada_w", "ada_b", "tm_pre_g", "tm_post_g", "cm_pre_g", "cm_post_g", "w_in", "ml_i_bias", "ml_f_bias", "ml_norm_g",
        "w_ml_out", "gla_w_a2", "gla_a_bias", "gla_norm_g", "w_gla_out", "conf_dw_w", "conf_dw_b", "conf_ln_g", "conf_ln_b",
        "w_conf_out", "conf_out_b", "sc_dw_w", "w_sc_out", "merge_gate_b", "w_o", "ffn_w_up", "ffn_dw_w", "ffn_w_down",
        "norm_mix_g_2", "w_in_2", "pool_w_2", "pool_scale_2", "w_pool_proj_2", "w_attn_proj_2", "w_out_2", "norm_ffn_g_2",
        "w_up_2", "conv_w_2", "conv_b_2", "w_down_2", "norm_final_g_2"]


def kernel(**inputs):
    import concourse.bacc as bacc
    from concourse.bass_utils import run_bass_kernel_spmd

    nc = bacc.Bacc("TRN2", target_bir_lowering=False, num_devices=1)
    arrays, args = {}, {}
    for name in _INS:
        a = np.ascontiguousarray(inputs[name])
        arrays[f"in_{name}"] = a
        args[name] = nc.dram_tensor(f"in_{name}", a.shape, mybir.dt.from_np(a.dtype), kind="ExternalInput").ap()
    arrays["in_consts"] = shape_constants()
    args["consts"] = nc.dram_tensor("in_consts", (P, N_CONST + 2 * S), FP32, kind="ExternalInput").ap()
    out = nc.dram_tensor("out", (1, S, D), FP32, kind="ExternalOutput").ap()
    program(nc, args, out)
    return run_bass_kernel_spmd(nc, [arrays], core_ids=[0]).results[0]["out"]
```
